# Optimizing a Trainium2 kernel written in Bass

```python
import math
import jax, jax.numpy as jnp
from jax import lax
import numpy as np

D_MODEL = 1024
BATCH = 1
SEQ = 512
DEPTH = 2

GRID_W = 64
CTX_LEN = 256
D_FF = 4 * D_MODEL
N_MOD = 6

MLA_HEADS = 8
QK_NOPE = 64
QK_ROPE = 32
QK_DIM = QK_NOPE + QK_ROPE
V_DIM = 64
MLA_WIDTH = MLA_HEADS * V_DIM
Q_LORA = 256
KV_LORA = 128
AXIS_DIM = QK_ROPE // 2
ROPE_THETA = 10000.0
Q_BLOCK = 128
SM_SCALE = 1.0 / math.sqrt(QK_DIM)

CONF_WIDTH = 256
CONF_K = 31
SC_WIDTH = 256
SC_K = 3

MIX_WIDTH = MLA_WIDTH + CONF_WIDTH + SC_WIDTH

Q_END = Q_LORA
KV_START = Q_END
KV_END = KV_START + KV_LORA
ROPE_END = KV_END + QK_ROPE
CONF_END = ROPE_END + 2 * CONF_WIDTH
IN_WIDTH = CONF_END + 3 * SC_WIDTH

EPS = 1e-6


def rmsnorm(u, g):
    uf = u.astype(jnp.float32)
    y = uf * lax.rsqrt(jnp.mean(uf * uf, axis=-1, keepdims=True) + EPS)
    return (y * g.astype(jnp.float32)).astype(u.dtype)

def layernorm(u, g, b):
    uf = u.astype(jnp.float32)
    mu = jnp.mean(uf, axis=-1, keepdims=True)
    d = uf - mu
    y = d * lax.rsqrt(jnp.mean(d * d, axis=-1, keepdims=True) + EPS)
    return (y * g.astype(jnp.float32) + b.astype(jnp.float32)).astype(u.dtype)

def modulation(cvec, w_mod, b_mod):
    m = jax.nn.silu(cvec) @ w_mod + b_mod
    return jnp.split(m[:, None, :], N_MOD, axis=-1)

def modulate(h, shift, scale):
    return h * (1.0 + scale) + shift

def axial_rope_tables(rows):
    row = jnp.broadcast_to(jnp.arange(rows)[:, None], (rows, GRID_W)).reshape(-1).astype(jnp.float32)
    col = jnp.broadcast_to(jnp.arange(GRID_W)[None, :], (rows, GRID_W)).reshape(-1).astype(jnp.float32)
    inv = 1.0 / (ROPE_THETA ** (jnp.arange(0, AXIS_DIM, 2, dtype=jnp.float32) / AXIS_DIM))
    ar = row[:, None] * inv
    ac = col[:, None] * inv
    ang = jnp.concatenate([ar, ar, ac, ac], axis=-1)
    return jnp.cos(ang), jnp.sin(ang)

def apply_axial_rope(u, cos, sin):
    def rot(p):
        h = p.shape[-1] // 2
        return jnp.concatenate([-p[..., h:], p[..., :h]], axis=-1)
    rotated = jnp.concatenate([rot(u[..., :AXIS_DIM]), rot(u[..., AXIS_DIM:])], axis=-1)
    return (u.astype(jnp.float32) * cos + rotated.astype(jnp.float32) * sin).astype(u.dtype)

def mla_queries(zq, g_q, w_q_b, rope):
    b, s, _ = zq.shape
    q = (rmsnorm(zq, g_q) @ w_q_b).reshape(b, s, MLA_HEADS, QK_DIM)
    if rope is None:
        return q
    cos, sin = rope
    q_rope = apply_axial_rope(q[..., QK_NOPE:], cos[:, None, :], sin[:, None, :])
    return jnp.concatenate([q[..., :QK_NOPE], q_rope], axis=-1)

def mla_keys_values(zkv, g_kv, w_kv_b, rope):
    b, s, _ = zkv.shape
    ckv, k_rope = zkv[..., :KV_LORA], zkv[..., KV_LORA:]
    kv = (rmsnorm(ckv, g_kv) @ w_kv_b).reshape(b, s, MLA_HEADS, QK_NOPE + V_DIM)
    k_nope, v = kv[..., :QK_NOPE], kv[..., QK_NOPE:]
    if rope is not None:
        cos, sin = rope
        k_rope = apply_axial_rope(k_rope, cos, sin)
    k_rope = jnp.broadcast_to(k_rope[:, :, None, :], (b, s, MLA_HEADS, QK_ROPE))
    return jnp.concatenate([k_nope, k_rope], axis=-1), v

def block_attention(q, k, v):
    b, s, h, dq = q.shape
    dv = v.shape[-1]
    nb = s // Q_BLOCK
    qb = jnp.moveaxis(q.reshape(b, nb, Q_BLOCK, h, dq), 1, 0)

    def attend(qblk):
        logits = jnp.einsum('bqhd,bkhd->bhqk', qblk, k).astype(jnp.float32) * SM_SCALE
        p = jax.nn.softmax(logits, axis=-1).astype(v.dtype)
        return jnp.einsum('bhqk,bkhd->bqhd', p, v)

    o = lax.map(attend, qb)
    return jnp.moveaxis(o, 0, 1).reshape(b, s, h * dv)

def depthwise_conv(u, w):
    k, ch = w.shape
    return lax.conv_general_dilated(
        u, w[:, None, :].astype(u.dtype), window_strides=(1,),
        padding=[(k // 2, k // 2)], dimension_numbers=('NWC', 'WIO', 'NWC'),
        feature_group_count=ch)

def conformer_branch(z, dw_w, dw_b, ln_g, ln_b):
    a, g = jnp.split(z, 2, axis=-1)
    u = a * jax.nn.sigmoid(g)
    u = depthwise_conv(u, dw_w) + dw_b
    u = layernorm(u, ln_g, ln_b)
    return jax.nn.silu(u)

def shortconv_branch(z, w):
    b_gate, c_gate, h = jnp.split(z, 3, axis=-1)
    return b_gate * depthwise_conv(c_gate * h, w)

def mix_stream(z, k, v, rope, g_q, w_q_b, conf_dw_w, conf_dw_b, conf_ln_g, conf_ln_b,
               sc_dw_w, g_branch, w_o):
    q = mla_queries(z[..., :Q_END], g_q, w_q_b, rope)
    attn = block_attention(q, k, v)
    conf = conformer_branch(z[..., ROPE_END:CONF_END], conf_dw_w, conf_dw_b, conf_ln_g, conf_ln_b)
    sc = shortconv_branch(z[..., CONF_END:], sc_dw_w)
    merged = jnp.concatenate([
        rmsnorm(attn, g_branch[:MLA_WIDTH]),
        rmsnorm(conf, g_branch[MLA_WIDTH:MLA_WIDTH + CONF_WIDTH]),
        rmsnorm(sc, g_branch[MLA_WIDTH + CONF_WIDTH:])], axis=-1)
    return merged @ w_o

def sqrelu_mlp(h, w1, w2):
    a = jax.nn.relu(h @ w1)
    return (a * a) @ w2

def first_inputs(seed: int = 0) -> dict:
    key = jax.random.key(seed)
    ks = jax.random.split(key, 32)
    f32 = jnp.float32

    def nrm(k, shape, scale):
        return jax.random.normal(k, shape, f32) * scale

    def gain(k, shape):
        return 1.0 + 0.05 * jax.random.normal(k, shape, f32)

    L, D = DEPTH, D_MODEL
    return {
        "x": nrm(ks[0], (BATCH, SEQ, D), 1.0),
        "c": nrm(ks[1], (BATCH, D), 1.0),
        "ctx": nrm(ks[2], (BATCH, CTX_LEN, D), 1.0),
        "c_ctx": nrm(ks[3], (D,), 1.0),
        "w_mod": nrm(ks[4], (L, D, N_MOD * D), 0.5 * D ** -0.5),
        "b_mod": nrm(ks[5], (L, N_MOD * D), 0.02),
        "g_pre_mix": gain(ks[6], (L, D)),
        "g_post_mix": gain(ks[7], (L, D)),
        "g_pre_mlp": gain(ks[8], (L, D)),
        "g_post_mlp": gain(ks[9], (L, D)),
        "w_in": nrm(ks[10], (L, D, IN_WIDTH), D ** -0.5),
        "g_q": gain(ks[11], (L, Q_LORA)),
        "w_q_b": nrm(ks[12], (L, Q_LORA, MLA_HEADS * QK_DIM), Q_LORA ** -0.5),
        "g_kv": gain(ks[13], (L, KV_LORA)),
        "w_kv_b": nrm(ks[14], (L, KV_LORA, MLA_HEADS * (QK_NOPE + V_DIM)), KV_LORA ** -0.5),
        "conf_dw_w": nrm(ks[15], (L, CONF_K, CONF_WIDTH), CONF_K ** -0.5),
        "conf_dw_b": nrm(ks[16], (L, CONF_WIDTH), 0.02),
        "conf_ln_g": gain(ks[17], (L, CONF_WIDTH)),
        "conf_ln_b": nrm(ks[18], (L, CONF_WIDTH), 0.02),
        "sc_dw_w": nrm(ks[19], (L, SC_K, SC_WIDTH), SC_K ** -0.5),
        "g_branch": gain(ks[20], (L, MIX_WIDTH)),
        "w_o": nrm(ks[21], (L, MIX_WIDTH, D), MIX_WIDTH ** -0.5),
        "w_mlp_in": nrm(ks[22], (L, D, D_FF), D ** -0.5),
        "w_mlp_out": nrm(ks[23], (L, D_FF, D), D_FF ** -0.5),
    }

def first_block(x, c, ctx, c_ctx, w_mod, b_mod, g_pre_mix, g_post_mix, g_pre_mlp, g_post_mlp,
              w_in, g_q, w_q_b, g_kv, w_kv_b, conf_dw_w, conf_dw_b, conf_ln_g, conf_ln_b,
              sc_dw_w, g_branch, w_o, w_mlp_in, w_mlp_out):
    n_lat = x.shape[1]
    rows = n_lat // GRID_W
    rope = axial_rope_tables(rows)
    xl, xc = x, ctx
    for i in range(DEPTH):
        last = i == DEPTH - 1
        ml = modulation(c, w_mod[i], b_mod[i])
        mc = modulation(c_ctx[None, :], w_mod[i], b_mod[i])

        hl = modulate(rmsnorm(xl, g_pre_mix[i]), ml[0], ml[1])
        hc = modulate(rmsnorm(xc, g_pre_mix[i]), mc[0], mc[1])
        zl = hl @ w_in[i]
        if last:
            zc_kv = hc @ w_in[i][:, KV_START:ROPE_END]
        else:
            zc = hc @ w_in[i]
            zc_kv = zc[..., KV_START:ROPE_END]

        k_c, v_c = mla_keys_values(zc_kv, g_kv[i], w_kv_b[i], None)
        k_l, v_l = mla_keys_values(zl[..., KV_START:ROPE_END], g_kv[i], w_kv_b[i], rope)
        y_l = mix_stream(zl, jnp.concatenate([k_c, k_l], axis=1), jnp.concatenate([v_c, v_l], axis=1),
                         rope, g_q[i], w_q_b[i], conf_dw_w[i], conf_dw_b[i], conf_ln_g[i],
                         conf_ln_b[i], sc_dw_w[i], g_branch[i], w_o[i])
        xl_new = xl + ml[2] * rmsnorm(y_l, g_post_mix[i])

        h2 = modulate(rmsnorm(xl_new, g_pre_mlp[i]), ml[3], ml[4])
        xl_new = xl_new + ml[5] * rmsnorm(sqrelu_mlp(h2, w_mlp_in[i], w_mlp_out[i]), g_post_mlp[i])

        if not last:
            y_c = mix_stream(zc, k_c, v_c, None, g_q[i], w_q_b[i], conf_dw_w[i], conf_dw_b[i],
                             conf_ln_g[i], conf_ln_b[i], sc_dw_w[i], g_branch[i], w_o[i])
            xc_new = xc + mc[2] * rmsnorm(y_c, g_post_mix[i])
            h2c = modulate(rmsnorm(xc_new, g_pre_mlp[i]), mc[3], mc[4])
            xc = xc_new + mc[5] * rmsnorm(sqrelu_mlp(h2c, w_mlp_in[i], w_mlp_out[i]), g_post_mlp[i])
        xl = xl_new
    return xl


DEPTH_2 = 1

HEAD_DIM = 64
ROPE_DIMS = HEAD_DIM // 4
ROPE_THETA_2 = 500000.0
NORM_EPS = 1e-6
NEG_INF = -1e30

NSA_HEADS = 8
NSA_KV_GROUPS = 2
NSA_Q_PER_KV = NSA_HEADS // NSA_KV_GROUPS
CMP_BLOCK = 32
CMP_STRIDE = 16
CMP_HIDDEN = 256
SLC_BLOCK = 64
SLC_TOPN = 16
FORCE_SCORE = 1e3
WIN = 512
NSA_QBLOCK = 64

DIL_PATTERNS = ((128, 1), (512, 4), (2048, 16))
DIL_GROUPS = len(DIL_PATTERNS)
DIL_HEADS_PER_GROUP = 4
DIL_WIDTH = DIL_HEADS_PER_GROUP * HEAD_DIM
DIL_BLOCK = 128

NSA_Q_COLS = NSA_HEADS * HEAD_DIM
NSA_KV_COLS = NSA_KV_GROUPS * HEAD_DIM
NSA_GATE_COLS = 3 * NSA_HEADS
DIL_COLS = DIL_GROUPS * 3 * DIL_WIDTH
MERGE_COLS = 2 * D_MODEL
IN_COLS = NSA_Q_COLS + 6 * NSA_KV_COLS + NSA_GATE_COLS + DIL_COLS + MERGE_COLS

PEER_HEADS = 8
PEER_NKEYS = 128
PEER_TOPK = 16
PEER_QDIM = 128
PEER_N_EXPERTS = PEER_NKEYS ** 2
PEER_CHUNK = 128


def rms_norm(z, g):
    zf = z.astype(jnp.float32)
    zf = zf * lax.rsqrt(jnp.mean(zf * zf, axis=-1, keepdims=True) + NORM_EPS)
    return (zf * g.astype(jnp.float32)).astype(z.dtype)

def rope(z, pos):
    half = ROPE_DIMS // 2
    inv = ROPE_THETA_2 ** (-(jnp.arange(half, dtype=jnp.float32) * 2.0 / ROPE_DIMS))
    ang = pos.astype(jnp.float32)[:, None] * inv[None, :]
    cos = jnp.cos(ang)[None, :, None, :]
    sin = jnp.sin(ang)[None, :, None, :]
    zf = z.astype(jnp.float32)
    z1 = zf[..., :half]
    z2 = zf[..., half:ROPE_DIMS]
    out = jnp.concatenate([z1 * cos - z2 * sin, z1 * sin + z2 * cos, zf[..., ROPE_DIMS:]], axis=-1)
    return out.astype(z.dtype)

def compress_blocks(z, idx, pe, w1, w2):
    B, _, G, dh = z.shape
    blk = z[:, idx] + pe[None, None, :, None, :]
    n_cmp = idx.shape[0]
    flat = blk.transpose(0, 1, 3, 2, 4).reshape(B, n_cmp, G, CMP_BLOCK * dh)
    return jax.nn.gelu(flat @ w1) @ w2

def nsa_attention(q, k_c, v_c, k_s, v_s, k_w, v_w, gate_logits, q_norm, k_norm,
                  cmp_pe_k, cmp_w1_k, cmp_w2_k, cmp_pe_v, cmp_w1_v, cmp_w2_v):
    B, S, _ = q.shape
    G, HG, dh = NSA_KV_GROUPS, NSA_Q_PER_KV, HEAD_DIM
    scale = HEAD_DIM ** -0.5
    dtype = q.dtype
    pos = jnp.arange(S, dtype=jnp.int32)
    q = rope(rms_norm(q.reshape(B, S, NSA_HEADS, dh), q_norm), pos)
    shp = (B, S, G, dh)
    k_s = rope(rms_norm(k_s.reshape(shp), k_norm[1]), pos)
    k_w = rope(rms_norm(k_w.reshape(shp), k_norm[2]), pos)
    v_s = v_s.reshape(shp)
    v_w = v_w.reshape(shp)

    n_cmp = (S - CMP_BLOCK) // CMP_STRIDE + 1
    starts = jnp.arange(n_cmp, dtype=jnp.int32) * CMP_STRIDE
    idx = starts[:, None] + jnp.arange(CMP_BLOCK, dtype=jnp.int32)[None, :]
    cmp_end = starts + CMP_BLOCK - 1
    k_cmp = compress_blocks(k_c.reshape(shp), idx, cmp_pe_k, cmp_w1_k, cmp_w2_k)
    v_cmp = compress_blocks(v_c.reshape(shp), idx, cmp_pe_v, cmp_w1_v, cmp_w2_v)
    k_cmp = rope(rms_norm(k_cmp, k_norm[0]), cmp_end)

    n_slc = S // SLC_BLOCK
    n_sel = min(SLC_TOPN, n_slc)
    s0 = np.arange(n_cmp) * CMP_STRIDE
    s1 = s0 + CMP_BLOCK
    b0 = np.arange(n_slc) * SLC_BLOCK
    b1 = b0 + SLC_BLOCK
    ov = np.clip(np.minimum(s1[:, None], b1[None, :]) - np.maximum(s0[:, None], b0[None, :]), 0, None) / CMP_BLOCK
    overlap = jnp.asarray(ov, dtype=jnp.float32)

    ks_blk = k_s.reshape(B, n_slc, SLC_BLOCK, G, dh).transpose(0, 3, 1, 2, 4)
    vs_blk = v_s.reshape(B, n_slc, SLC_BLOCK, G, dh).transpose(0, 3, 1, 2, 4)
    kw_pad = jnp.pad(k_w, ((0, 0), (WIN, 0), (0, 0), (0, 0)))
    vw_pad = jnp.pad(v_w, ((0, 0), (WIN, 0), (0, 0), (0, 0)))
    gates = jax.nn.sigmoid(gate_logits.astype(jnp.float32)).reshape(B, S, NSA_HEADS, 3)
    bi = jnp.arange(B)[:, None, None, None]
    gi = jnp.arange(G)[None, :, None, None]
    blk_ids = jnp.arange(n_slc, dtype=jnp.int32)
    QB = NSA_QBLOCK

    def body(n):
        t0 = n * QB
        t = t0 + jnp.arange(QB, dtype=jnp.int32)
        qb = lax.dynamic_slice_in_dim(q, t0, QB, axis=1).reshape(B, QB, G, HG, dh)
        sc = jnp.einsum('bqgjd,bcgd->bgjqc', qb, k_cmp).astype(jnp.float32) * scale
        valid_c = cmp_end[None, :] <= t[:, None]
        pc = jax.nn.softmax(jnp.where(valid_c, sc, NEG_INF), axis=-1)
        pc = jnp.where(valid_c, pc, 0.0)
        o_c = jnp.einsum('bgjqc,bcgd->bqgjd', pc.astype(dtype), v_cmp)
        imp = jnp.einsum('bgjqc,cn->bgqn', pc, overlap)
        cur = t // SLC_BLOCK
        forced = (blk_ids[None, :] == 0) | (blk_ids[None, :] == cur[:, None]) | (blk_ids[None, :] == cur[:, None] - 1)
        causal_b = blk_ids[None, :] * SLC_BLOCK <= t[:, None]
        score = jnp.where(forced, FORCE_SCORE, jnp.where(causal_b, imp, -1.0))
        _, sel = lax.top_k(score, n_sel)
        kg = ks_blk[bi, gi, sel]
        vg = vs_blk[bi, gi, sel]
        ss = jnp.einsum('bqgjd,bgqnkd->bgjqnk', qb, kg).astype(jnp.float32) * scale
        kpos = sel[..., None] * SLC_BLOCK + jnp.arange(SLC_BLOCK, dtype=jnp.int32)
        valid_s = kpos <= t[None, None, :, None, None]
        ss = jnp.where(valid_s[:, :, None], ss, NEG_INF).reshape(B, G, HG, QB, n_sel * SLC_BLOCK)
        ps = jax.nn.softmax(ss, axis=-1).reshape(B, G, HG, QB, n_sel, SLC_BLOCK)
        o_s = jnp.einsum('bgjqnk,bgqnkd->bqgjd', ps.astype(dtype), vg)
        kwb = lax.dynamic_slice_in_dim(kw_pad, t0, QB + WIN, axis=1)
        vwb = lax.dynamic_slice_in_dim(vw_pad, t0, QB + WIN, axis=1)
        kp = t0 - WIN + jnp.arange(QB + WIN, dtype=jnp.int32)
        dist = t[:, None] - kp[None, :]
        valid_w = (dist >= 0) & (dist < WIN) & (kp[None, :] >= 0)
        sw = jnp.einsum('bqgjd,bkgd->bgjqk', qb, kwb).astype(jnp.float32) * scale
        pw = jax.nn.softmax(jnp.where(valid_w, sw, NEG_INF), axis=-1)
        o_w = jnp.einsum('bgjqk,bkgd->bqgjd', pw.astype(dtype), vwb)
        gb = lax.dynamic_slice_in_dim(gates, t0, QB, axis=1).reshape(B, QB, G, HG, 3)
        o = gb[..., 0:1] * o_c + gb[..., 1:2] * o_s + gb[..., 2:3] * o_w
        return o.reshape(B, QB, NSA_HEADS * dh).astype(dtype)

    out = lax.map(body, jnp.arange(S // QB, dtype=jnp.int32))
    return out.transpose(1, 0, 2, 3).reshape(B, S, NSA_HEADS * dh)

def dilated_group(q, k, v, window, dilation):
    B, S, H, dh = q.shape
    scale = HEAD_DIM ** -0.5
    n_back = window // dilation
    L = -(-S // dilation)
    L = -(-L // DIL_BLOCK) * DIL_BLOCK
    Sp = L * dilation
    nb = L // DIL_BLOCK
    pad = ((0, 0), (0, Sp - S), (0, 0), (0, 0))

    def to_blocks(z):
        z = jnp.pad(z, pad).reshape(B, L, dilation, H, dh).transpose(0, 2, 3, 1, 4)
        return z.reshape(B, dilation, H, nb, DIL_BLOCK, dh)

    def with_prev(z):
        prev = jnp.pad(z[:, :, :, :-1], ((0, 0), (0, 0), (0, 0), (1, 0), (0, 0), (0, 0)))
        return jnp.concatenate([prev, z], axis=4)

    qb = to_blocks(q)
    kk = with_prev(to_blocks(k))
    vv = with_prev(to_blocks(v))
    s = jnp.einsum('brhnqd,brhnkd->brhnqk', qb, kk).astype(jnp.float32) * scale
    blk = jnp.arange(nb, dtype=jnp.int32)[:, None]
    pq = blk * DIL_BLOCK + jnp.arange(DIL_BLOCK, dtype=jnp.int32)[None, :]
    pk = (blk - 1) * DIL_BLOCK + jnp.arange(2 * DIL_BLOCK, dtype=jnp.int32)[None, :]
    dist = pq[:, :, None] - pk[:, None, :]
    valid = (dist >= 0) & (dist <= n_back) & (pk[:, None, :] >= 0)
    s = jnp.where(valid, s, NEG_INF)
    m = jnp.max(s, axis=-1, keepdims=True)
    e = jnp.exp(s - m)
    den = jnp.sum(e, axis=-1)
    o = jnp.einsum('brhnqk,brhnkd->brhnqd', e, vv.astype(jnp.float32)) / den[..., None]
    lse = m[..., 0] + jnp.log(den)
    o = o.reshape(B, dilation, H, L, dh).transpose(0, 3, 1, 2, 4).reshape(B, Sp, H, dh)[:, :S]
    lse = lse.reshape(B, dilation, H, L).transpose(0, 3, 1, 2).reshape(B, Sp, H)[:, :S]
    return o, lse

def dilated_attention(d_cols, q_norm, k_norm):
    B, S, _ = d_cols.shape
    pos = jnp.arange(S, dtype=jnp.int32)
    d = d_cols.reshape(B, S, DIL_GROUPS, 3, DIL_HEADS_PER_GROUP, HEAD_DIM)
    outs, lses = [], []
    for g, (window, dilation) in enumerate(DIL_PATTERNS):
        qg = rope(rms_norm(d[:, :, g, 0], q_norm[g]), pos)
        kg = rope(rms_norm(d[:, :, g, 1], k_norm[g]), pos)
        o, lse = dilated_group(qg, kg, d[:, :, g, 2], window, dilation)
        outs.append(o)
        lses.append(lse)
    alpha = jax.nn.softmax(jnp.stack(lses, axis=0), axis=0)
    o = jnp.sum(alpha[..., None] * jnp.stack(outs, axis=0), axis=0)
    return o.reshape(B, S, DIL_WIDTH).astype(d_cols.dtype)

def peer(hn, w_q, subkeys, u, v):
    B, S, D = hn.shape
    T = B * S
    H, K = PEER_HEADS, PEER_TOPK
    xt = hn.reshape(T, D)
    q = (xt @ w_q).reshape(T, H, 2, PEER_QDIM // 2)
    s = jnp.einsum('thcd,cnd->thcn', q, subkeys).astype(jnp.float32)
    s1, i1 = lax.top_k(s[:, :, 0], K)
    s2, i2 = lax.top_k(s[:, :, 1], K)
    cand = (s1[..., :, None] + s2[..., None, :]).reshape(T, H, K * K)
    sc, ci = lax.top_k(cand, K)
    e1 = jnp.take_along_axis(i1, ci // K, axis=-1)
    e2 = jnp.take_along_axis(i2, ci % K, axis=-1)
    idx = e1 * PEER_NKEYS + e2
    g = jax.nn.softmax(sc, axis=-1)
    C = PEER_CHUNK
    nc = T // C

    def body(args):
        xc, ic, gc = args
        a = jnp.einsum('cd,chkd->chk', xc, u[ic])
        act = (jax.nn.gelu(a.astype(jnp.float32)) * gc).astype(xc.dtype)
        return jnp.einsum('chk,chkd->cd', act, v[ic])

    out = lax.map(body, (xt.reshape(nc, C, D), idx.reshape(nc, C, H, K), g.reshape(nc, C, H, K)))
    return out.reshape(B, S, D)

def second_inputs(seed: int = 0) -> dict:
    key = jax.random.key(seed)
    ks = jax.random.split(key, 24)
    f32 = jnp.float32

    def nrm(k, shape, scale):
        return jax.random.normal(k, shape, f32) * scale

    def gain(k, shape):
        return 1.0 + 0.02 * jax.random.normal(k, shape, f32)

    flat = CMP_BLOCK * HEAD_DIM
    nsa_w = NSA_HEADS * HEAD_DIM
    return {
        "x": nrm(ks[0], (BATCH, SEQ, D_MODEL), 1.0),
        "norm1_g": gain(ks[1], (D_MODEL,)),
        "w_in": nrm(ks[2], (D_MODEL, IN_COLS), D_MODEL ** -0.5),
        "nsa_q_norm": gain(ks[3], (HEAD_DIM,)),
        "nsa_k_norm": gain(ks[4], (3, HEAD_DIM)),
        "cmp_pe_k": nrm(ks[5], (CMP_BLOCK, HEAD_DIM), 0.1),
        "cmp_w1_k": nrm(ks[6], (flat, CMP_HIDDEN), flat ** -0.5),
        "cmp_w2_k": nrm(ks[7], (CMP_HIDDEN, HEAD_DIM), CMP_HIDDEN ** -0.5),
        "cmp_pe_v": nrm(ks[8], (CMP_BLOCK, HEAD_DIM), 0.1),
        "cmp_w1_v": nrm(ks[9], (flat, CMP_HIDDEN), flat ** -0.5),
        "cmp_w2_v": nrm(ks[10], (CMP_HIDDEN, HEAD_DIM), CMP_HIDDEN ** -0.5),
        "dil_q_norm": gain(ks[11], (DIL_GROUPS, HEAD_DIM)),
        "dil_k_norm": gain(ks[12], (DIL_GROUPS, HEAD_DIM)),
        "w_up_nsa": nrm(ks[13], (nsa_w, D_MODEL), nsa_w ** -0.5),
        "w_up_dil": nrm(ks[14], (DIL_WIDTH, D_MODEL), DIL_WIDTH ** -0.5),
        "w_o": nrm(ks[15], (D_MODEL, D_MODEL), D_MODEL ** -0.5),
        "norm2_g": gain(ks[16], (D_MODEL,)),
        "peer_wq": nrm(ks[17], (D_MODEL, PEER_HEADS * PEER_QDIM), D_MODEL ** -0.5),
        "peer_subkeys": nrm(ks[18], (2, PEER_NKEYS, PEER_QDIM // 2), (PEER_QDIM // 2) ** -0.5),
        "peer_u": nrm(ks[19], (PEER_N_EXPERTS, D_MODEL), D_MODEL ** -0.5),
        "peer_v": nrm(ks[20], (PEER_N_EXPERTS, D_MODEL), PEER_HEADS ** -0.5),
    }

def second_block(x, norm1_g, w_in, nsa_q_norm, nsa_k_norm, cmp_pe_k, cmp_w1_k, cmp_w2_k,
              cmp_pe_v, cmp_w1_v, cmp_w2_v, dil_q_norm, dil_k_norm, w_up_nsa, w_up_dil,
              w_o, norm2_g, peer_wq, peer_subkeys, peer_u, peer_v):
    B, S, D = x.shape
    sizes = [NSA_Q_COLS] + [NSA_KV_COLS] * 6 + [NSA_GATE_COLS, DIL_COLS, MERGE_COLS]
    splits = [int(c) for c in np.cumsum(sizes)[:-1]]
    for _ in range(DEPTH_2):
        h = rms_norm(x, norm1_g)
        z = jnp.einsum('bsd,dc->bsc', h, w_in)
        q_n, kc, vc, ksl, vsl, kwn, vwn, g_nsa, dil, mg = jnp.split(z, splits, axis=-1)
        y_nsa = nsa_attention(q_n, kc, vc, ksl, vsl, kwn, vwn, g_nsa, nsa_q_norm, nsa_k_norm,
                              cmp_pe_k, cmp_w1_k, cmp_w2_k, cmp_pe_v, cmp_w1_v, cmp_w2_v)
        y_dil = dilated_attention(dil, dil_q_norm, dil_k_norm)
        gm = jax.nn.sigmoid(mg.astype(jnp.float32)).reshape(B, S, 2, D)
        merged = gm[:, :, 0] * (y_nsa @ w_up_nsa) + gm[:, :, 1] * (y_dil @ w_up_dil)
        x = x + merged.astype(x.dtype) @ w_o
        x = x + peer(rms_norm(x, norm2_g), peer_wq, peer_subkeys, peer_u, peer_v)
    return x


def setup_inputs(seed=0):
    out = dict(first_inputs(seed))
    for name, value in second_inputs(seed + 1).items():
        if name != "x":
            out[name + "_2"] = value
    return out


def reference(
    x, c, ctx, c_ctx, w_mod, b_mod, g_pre_mix, g_post_mix, g_pre_mlp, g_post_mlp, w_in, g_q,
    w_q_b, g_kv, w_kv_b, conf_dw_w, conf_dw_b, conf_ln_g, conf_ln_b, sc_dw_w, g_branch, w_o,
    w_mlp_in, w_mlp_out, norm1_g_2, w_in_2, nsa_q_norm_2, nsa_k_norm_2, cmp_pe_k_2, cmp_w1_k_2,
    cmp_w2_k_2, cmp_pe_v_2, cmp_w1_v_2, cmp_w2_v_2, dil_q_norm_2, dil_k_norm_2, w_up_nsa_2,
    w_up_dil_2, w_o_2, norm2_g_2, peer_wq_2, peer_subkeys_2, peer_u_2, peer_v_2,
):
    x = first_block(
        x, c, ctx, c_ctx, w_mod, b_mod, g_pre_mix, g_post_mix, g_pre_mlp, g_post_mlp, w_in, g_q,
        w_q_b, g_kv, w_kv_b, conf_dw_w, conf_dw_b, conf_ln_g, conf_ln_b, sc_dw_w, g_branch, w_o,
        w_mlp_in, w_mlp_out,
    )
    return second_block(
        x, norm1_g_2, w_in_2, nsa_q_norm_2, nsa_k_norm_2, cmp_pe_k_2, cmp_w1_k_2, cmp_w2_k_2,
        cmp_pe_v_2, cmp_w1_v_2, cmp_w2_v_2, dil_q_norm_2, dil_k_norm_2, w_up_nsa_2, w_up_dil_2,
        w_o_2, norm2_g_2, peer_wq_2, peer_subkeys_2, peer_u_2, peer_v_2,
    )


_drawn_inputs = setup_inputs


def setup_inputs(seed=0):
    import zlib

    import numpy as np

    out = dict(_drawn_inputs(seed))
    spreads = {}
    factors = {'g_q': 4.124,
     'conf_dw_b': 3.534,
     'conf_ln_b': 4.733,
     'norm1_g_2': 4.546,
     'nsa_q_norm_2': 8.0,
     'nsa_k_norm_2': 8.0,
     'cmp_pe_k_2': 6.522,
     'dil_q_norm_2': 8.0,
     'dil_k_norm_2': 8.0,
     'cmp_pe_v_2': 6.922,
     'norm2_g_2': 8.0}
    for name, (base, spread) in spreads.items():
        noise = np.random.default_rng([zlib.crc32(name.encode()), seed]).standard_normal(out[name].shape)
        drawn = base * np.exp(spread * noise) if base else spread * noise
        out[name] = __import__('jax').numpy.asarray(drawn.astype(out[name].dtype))
    for name, factor in factors.items():
        out[name] = (out[name] * factor).astype(out[name].dtype)
    return out
```

```python
from contextlib import ExitStack

import numpy as np
import concourse.bass as bass
from concourse import mybir

ALU = mybir.AluOpType
ACT = mybir.ActivationFunctionType
AX = mybir.AxisListType
F32 = mybir.dt.float32
FR = mybir.dt.float32r
U32 = mybir.dt.uint32

EPS = 1e-6
NEG = -1e30
LAT = (0, 512)
CTX = (512, 256)
SLAB = 2048


class Engine:

    def __init__(self, engine, sem):
        self.e, self.sem, self.n, self.seen = engine, sem, 0, {}

    def wait(self, *after):
        for t in after:
            if t is None:
                continue
            if isinstance(t, list):
                self.wait(*t)
                continue
            sem, value = t
            if self.seen.get(id(sem), 0) < value:
                self.seen[id(sem)] = value
                self.e.wait_ge(sem, value)

    def put(self, fn, *after, count=True):
        self.wait(*after)
        ins = fn(self.e)
        if not count:
            return None
        self.n += 1
        ins.then_inc(self.sem, 1)
        return (self.sem, self.n)

    def dma(self, out, in_, sem, value, *after):
        self.wait(*after)
        self.e.dma_start(out, in_).then_inc(sem, 16)
        return (sem, value)


class Ring:

    def __init__(self, bufs):
        self.bufs, self.free = bufs, [(i, []) for i in range(len(bufs))]

    def take(self):
        i, after = self.free.pop(0)
        return i, self.bufs[i], after

    def give(self, i, *after):
        self.free.append((i, list(after)))


def build(nc, io):
    out_d = io["out"]
    with ExitStack() as top:
        names = [0]

        def sb(stack, shape, dt=F32):
            names[0] += 1
            return stack.enter_context(nc.sbuf_tensor(f"sb{names[0]}", shape, dt))

        def sem():
            names[0] += 1
            return top.enter_context(nc.semaphore(f"sem{names[0]}"))

        PE, DVE, AC, PO, SP = (Engine(e, sem()) for e in (nc.tensor, nc.vector, nc.scalar, nc.gpsimd, nc.sync))
        dma_sems = {}

        def load(eng, out, in_, name, *after):
            s, n = dma_sems.get(name, (None, 0))
            s = s or sem()
            dma_sems[name] = (s, n + 16)
            return eng.dma(out, in_, s, n + 16, *after)

        X = sb(top, [128, 8, 768])
        Y = sb(top, [128, 8, 768])
        ps = [top.enter_context(nc.psum_tensor(f"ps{i}", [128, 1024], F32)) for i in range(4)]
        PS = Ring(ps)
        stage = [sb(top, [128, SLAB]) for _ in range(2)]
        WHb = [sb(top, [128, SLAB], FR) for _ in range(2)]
        WLb = [sb(top, [128, SLAB], FR) for _ in range(2)]
        T = Ring([sb(top, [128, 768]) for _ in range(2)])
        RS = Ring([sb(top, [128, 768]) for _ in range(1)])
        epsc = sb(top, [128, 1])
        ident = sb(top, [128, 128])
        ones = sb(top, [128, 128])
        cols = [sb(top, [128, 165]) for _ in range(2)]
        cols2 = sb(top, [128, 32])
        MOD = sb(top, [128, 48, 2])
        AB = sb(top, [128, 6, 8, 2])

        t_x = load(SP, X[:, :, 0:512], io["xT"], "x0")
        t_xc = load(SP, X[:, :, 512:768], io["ctxT"], "x1")
        t_id = load(PO, ident[:, :], io["ident"], "c0")
        t_ones = load(PO, ones[:, :], io["ones"], "c1")
        t_cols = [load(PO, cols[i][:, :], io["cols"][i], f"c{2 + i}") for i in range(2)]
        t_cols2 = load(PO, cols2[:, :], io["cols2"], "c4")
        t_eps = DVE.put(lambda e: e.memset(epsc[:, :], EPS))
        AC.wait(t_eps, t_cols)
        DVE.wait(t_cols, t_cols2, t_eps)
        PE.wait(t_id, t_ones)

        plan = []
        for l in range(2):
            plan += [("raw", io["w_mod"][l, s]) for s in range(24)]
            plan += [("split", io["w_in"][l, s]) for s in range(7)]
            plan += [("split", io["w_o"][l, s]) for s in range(4)]
            for g in range(8):
                plan += [("split", io["w1"][l, 2 * g + s]) for s in range(2)]
                plan += [("split", io["w2"][l, 2 * g + s]) for s in range(2)]
        plan += [("split", io["win2"][s]) for s in range(5)]
        plan += [("split", io["gate2"])]
        for hp in range(2):
            plan += [("split", io[f"dqk{hp}"][s]) for s in range(3)]
            plan += [("split", io[f"dva{hp}"]), ("split", io[f"dvb{hp}"])]
        plan += [("split", io["up_nsa"][s]) for s in range(2)]
        plan += [("split", io["up_dil"])]
        plan += [("split", io["wmg"][s]) for s in range(8)]
        plan += [("split", io["w_o2"][s]) for s in range(4)]
        plan += [("split", io["wq2"][s]) for s in range(4)]
        for g in range(32):
            plan += [("split", io["u2"][2 * g + s]) for s in range(2)]
            plan += [("split", io["v2"][2 * g + s]) for s in range(2)]
        landed = {}
        stage_free = [None, None]
        w_ready = {}
        w_free = [None, None]
        nsplit = [0]
        sent = [0]
        split_no = {}

        def send(n):
            while sent[0] <= min(n, len(plan) - 1):
                m = sent[0]
                src = plan[m][1]
                landed[m] = load(SP, stage[m % 2][:, 0:src.shape[-1]], src, f"w{m % 2}", stage_free[m % 2])
                sent[0] += 1

        def split(n):
            if n >= len(plan) or plan[n][0] == "raw" or n in w_ready:
                return
            send(n)
            k = nsplit[0] % 2
            nsplit[0] += 1
            w = plan[n][1].shape[-1]
            st = stage[n % 2][:, 0:w]
            th = AC.put(lambda e: e.activation(WHb[k][:, 0:w], st, ACT.Copy), landed[n], w_free[k])
            tl = DVE.put(lambda e: e.tensor_tensor(WLb[k][:, 0:w], st, WHb[k][:, 0:w].bitcast(F32), ALU.subtract),
                         landed[n], th, w_free[k])
            stage_free[n % 2] = [tl]
            w_ready[n] = [th, tl]
            split_no[n] = k

        cur = [0]

        def take_raw():
            n = cur[0]
            cur[0] += 1
            send(n + 1)
            return n, stage[n % 2], landed[n]

        def give_raw(n, *after):
            stage_free[n % 2] = list(after)
            send(n + 2)

        def take_slab():
            n = cur[0]
            cur[0] += 1
            send(n)
            split(n)
            send(n + 2)
            if n + 1 < len(plan) and plan[n + 1][0] == "split":
                split(n + 1)
                send(n + 3)
            k = split_no[n]
            return k, WHb[k], WLb[k], w_ready[n]

        def give_slab(k, *after):
            w_free[k] = list(after)

        background = []

        def idle(n=1):
            for _ in range(n):
                if background:
                    background.pop(0)()

        def three(out, ah, al, bh, bl, first, last):
            PE.put(lambda e: e.matmul(out, ah, bh, start=first, stop=False), count=False)
            PE.put(lambda e: e.matmul(out, ah, bl, start=False, stop=False), count=False)
            return PE.put(lambda e: e.matmul(out, al, bh, start=False, stop=last), count=last)

        def linear(nslab, K, ncol, segs, HH, HL, ready, emit, chunks=None):
            c = 0
            for _ in range(nslab):
                k, wh, wl, wr = take_slab()
                wh = wh[:, 0:K * ncol].rearrange("p (k n) -> p k n", k=K)
                wl = wl[:, 0:K * ncol].rearrange("p (k n) -> p k n", k=K)
                last = None
                for j in range(ncol // 128):
                    if chunks is not None and not chunks(c):
                        c += 1
                        continue
                    sg = segs(c) if callable(segs) else segs
                    i, p, free = PS.take()
                    PE.wait(free, wr, ready)
                    cs = slice(128 * j, 128 * j + 128)
                    for (s0, sn) in sg:
                        for kk in range(K):
                            last = three(p[:, s0:s0 + sn], wh[:, kk, cs], wl[:, kk, cs],
                                         HH[:, kk, s0:s0 + sn], HL[:, kk, s0:s0 + sn], kk == 0, kk == K - 1) or last
                    PS.give(i, *emit(c, p, last, sg))
                    c += 1
                    idle()
                give_slab(k, last)
            return last

        def span(segs):
            return min(s for s, _ in segs), max(s + n for s, n in segs)

        def rstd(src, segs, D, lhs, ready):
            a, b = span(segs)
            i, p, free = PS.take()
            PE.wait(free)
            for c, s in enumerate(src):
                ti, t, tf = T.take()
                tq = AC.put(lambda e: e.activation(t[:, a:b], s[:, a:b], ACT.Square), tf, ready)
                for (s0, sn) in segs:
                    tm = PE.put(lambda e: e.matmul(p[:, s0:s0 + sn], lhs, t[:, s0:s0 + sn], start=(c == 0),
                                                   stop=(c == len(src) - 1)), tq)
                T.give(ti, tm)
            ri, r, rf = RS.take()
            t1 = AC.put(lambda e: e.activation(r[:, a:b], p[:, a:b], ACT.Ln, bias=epsc[:, 0:1], scale=1.0 / D), tm, rf)
            t2 = AC.put(lambda e: e.activation(r[:, a:b], r[:, a:b], ACT.Exp, scale=-0.5), t1)
            PS.give(i, t1)
            return ri, r, t2

        def norm_split(src, segs, D, scale, shift, HH, HL, c0, ready, hfree):
            ri, r, tr = rstd(src, segs, D, ones[:, :], ready)
            done = []
            for c, s in enumerate(src):
                ti, t, tf = T.take()
                for si, (s0, sn) in enumerate(segs):
                    z = slice(s0, s0 + sn)
                    hh, hl = HH[:, c0 + c, z], HL[:, c0 + c, z]
                    tm = DVE.put(lambda e: e.scalar_tensor_tensor(t[:, z], s[:, z], scale(c, s0), r[:, z],
                                                                  ALU.mult, ALU.mult), tr, tf)
                    b = shift(c, s0) if shift else 0.0
                    if shift:
                        th = AC.put(lambda e: e.activation(hh, t[:, z], ACT.Identity, bias=b), tm, hfree)
                    else:
                        th = AC.put(lambda e: e.activation(hh, t[:, z], ACT.Copy), tm, hfree)
                    tl = DVE.put(lambda e: e.scalar_tensor_tensor(hl, t[:, z], b, hh.bitcast(F32),
                                                                  ALU.add, ALU.subtract), th, hfree)
                    done = [th, tl]
                T.give(ti, *done)
            RS.give(ri, *done)
            return done

        def add_normed(segs, D, scale, ready):
            ri, r, tr = rstd([Y[:, c, :] for c in range(8)], segs, D, ones[:, :], ready)
            for c in range(8):
                ti, t, tf = T.take()
                for (s0, sn) in segs:
                    z = slice(s0, s0 + sn)
                    tm = DVE.put(lambda e: e.scalar_tensor_tensor(t[:, z], Y[:, c, z], scale(c, s0), r[:, z],
                                                                  ALU.mult, ALU.mult), tr, tf)
                    ta = DVE.put(lambda e: e.tensor_tensor(X[:, c, z], X[:, c, z], t[:, z], ALU.add), tm)
                T.give(ti, ta)
            RS.give(ri, ta)
            return ta

        def mlp(groups, segs, HH, HL, A, ready, activate, yfree):
            a, b = span(segs)
            last_y = [None] * 8
            afree = [None, None]
            for g in range(groups):
                AH, AL = A[g % len(A)]
                done = []

                def up(c, p, tm, sg):
                    d = activate(g, c, p, tm, AH[:, c, :], AL[:, c, :], afree[g % len(A)])
                    done.append(d[0])
                    return d[1]

                linear(2, 8, 256, segs, HH, HL, ready, up)

                def down(c, p, tm, sg):
                    if g == 0:
                        t = AC.put(lambda e: e.activation(Y[:, c, a:b], p[:, a:b], ACT.Copy), tm, yfree)
                    else:
                        t = DVE.put(lambda e: e.tensor_tensor(Y[:, c, a:b], Y[:, c, a:b], p[:, a:b], ALU.add),
                                    tm, last_y[c])
                    last_y[c] = t
                    return [t]

                last = linear(2, 4, 512, segs, AH, AL, [done[-1]] + done, down)
                afree[g % len(A)] = [last]
            return last_y

        first = ExitStack()
        cT = sb(first, [128, 8, 2])
        sc = sb(first, [128, 8, 2])
        rotM = sb(first, [96, 96])
        cosM = sb(first, [96, 512])
        sinM = sb(first, [96, 512])
        t_c = load(PO, cT[:, :, :], io["cT"], "k0")
        t_tab = [load(PO, rotM[:, :], io["rotM"], "k1"), load(PO, cosM[:, :], io["cosM"], "k2"),
                 load(PO, sinM[:, :], io["sinM"], "k3")]
        t_sc = AC.put(lambda e: e.activation(sc[:, :, :], cT[:, :, :], ACT.Silu), t_c)
        x_ready = [t_x, t_xc]
        mod_read = None

        for l in range(2):
            both = [LAT, CTX] if l == 0 else [LAT]
            col = cols[l]
            G_PRE, G_POST, G_PRE2, G_POST2, G_Q, G_KV, DW_B, LN_G, LN_B, G_BR, CW, SW, B_MOD = (
                0, 8, 16, 24, 32, 34, 35, 37, 39, 41, 49, 111, 117)
            i, p, free = PS.take()
            PE.wait(free, t_sc)
            for s in range(24):
                n, w, tw = take_raw()
                w = w[:, :].rearrange("p (k n) -> p k n", k=8)
                for j in range(2):
                    o = p[:, 4 * s + 2 * j:4 * s + 2 * j + 2]
                    for k in range(8):
                        tm = PE.put(lambda e, k=k, o=o, j=j, w=w: e.matmul(o, w[:, k, 128 * j:128 * j + 128], sc[:, k, :],
                                                                      start=(k == 0), stop=(k == 7)),
                                    tw, count=(k == 7))
                give_raw(n, tm)
            t1 = DVE.put(lambda e: e.tensor_tensor(
                MOD[:, :, :], p[:, 0:96].rearrange("p (c v) -> p c v", v=2),
                col[:, B_MOD:B_MOD + 48].rearrange("p (c v) -> p c v", v=1).broadcast_to([128, 48, 2]), ALU.add),
                tm, mod_read)
            PS.give(i, t1)
            md = MOD[:, :, :].rearrange("p (m c) v -> p m c v", m=6)
            for dst, m, g, plus in ((0, 1, G_PRE, 1.0), (1, 2, G_POST, 0.0), (2, 4, G_PRE2, 1.0), (3, 5, G_POST2, 0.0)):
                for v in range(2):
                    t_ab = DVE.put(lambda e: e.scalar_tensor_tensor(AB[:, dst, :, v], md[:, m, :, v], plus,
                                                                    col[:, g:g + 8], ALU.add, ALU.mult), t1, mod_read)
            t_mod = [t1, t_ab]
            which = lambda s0: 0 if s0 < 512 else 1
            A_ = lambda d: (lambda c, s0: AB[:, d, c, which(s0):which(s0) + 1])
            B_ = lambda m: (lambda c, s0: md[:, m, c, which(s0):which(s0) + 1])

            z = ExitStack()
            ZQ = sb(z, [128, 2, 768])
            ZKV = sb(z, [128, 768])
            KR = sb(z, [96, 768])
            UW = 16 + 512 + 16 + 256 + 16
            U = sb(z, [128, 2, UW])
            CH = sb(z, [128, 2, UW])
            G2 = Ring([sb(z, [128, 768]) for _ in range(2)])
            HHs = ExitStack()
            HH, HL = sb(HHs, [128, 8, 768], FR), sb(HHs, [128, 8, 768], FR)
            h_free = [] if l == 0 else t_phase
            t_z0 = [DVE.put(lambda e: e.memset(U[:, :, :], 0.0), h_free),
                    DVE.put(lambda e: e.memset(CH[:, :, :], 0.0), h_free)]
            xs = [X[:, c, :] for c in range(8)]
            t_h = norm_split(xs, [LAT, CTX], 1024, A_(0), B_(0), HH, HL, 0, x_ready + t_mod, h_free)

            def padded(buf, c, s0, sn, shift=0):
                o = 16 + s0 if s0 == 0 else 16 + 512 + 16
                return buf[:, c, o + shift:o + shift + sn]

            z_done = []
            sigs = {}
            ORDER = ["kv", "kr", "q0", "q1", "g0", "a0", "g1", "a1", "h0", "c0", "h1", "c1", "b0", "b1"]

            def z_out(c, p, tm, sg):
                a, b = span(sg)
                kind = ORDER[c]
                if kind == "kv":
                    t = AC.put(lambda e: e.activation(ZKV[:, a:b], p[:, a:b], ACT.Copy), tm, h_free)
                elif kind == "kr":
                    t = AC.put(lambda e: e.activation(KR[:, a:b], p[0:96, a:b], ACT.Copy), tm, h_free)
                elif kind[0] == "q":
                    j = int(kind[1])
                    t = AC.put(lambda e: e.activation(ZQ[:, j, a:b], p[:, a:b], ACT.Copy), tm, h_free)
                elif kind[0] in "gh":
                    gi, g, gf = G2.take()
                    t = AC.put(lambda e: e.activation(g[:, a:b], p[:, a:b], ACT.Sigmoid if kind[0] == "g" else ACT.Copy),
                               tm, gf, h_free)
                    sigs[kind] = (gi, g, t)
                elif kind[0] in "ac":
                    j = int(kind[1])
                    gi, g, tg = sigs[("g" if kind[0] == "a" else "h") + kind[1]]
                    dst = U if kind[0] == "a" else CH
                    for (s0, sn) in sg:
                        t = DVE.put(lambda e: e.tensor_tensor(padded(dst, j, s0, sn), p[:, s0:s0 + sn],
                                                              g[:, s0:s0 + sn], ALU.mult), tm, tg, t_z0)
                    G2.give(gi, t)
                else:
                    j = int(kind[1])
                    t = AC.put(lambda e: e.activation(Y[:, 6 + j, a:b], p[:, a:b], ACT.Copy), tm, y_free)
                z_done.append(t)
                return [t]

            y_free = [] if l == 0 else t_phase
            in_segs = lambda c: [LAT, CTX] if ORDER[c] in ("kv", "kr") else both
            last = linear(7, 8, 256, in_segs, HH, HL, t_h, z_out)
            t_zdone = z_done
            t_hh = [last] + t_h
            HHs.close()

            att = ExitStack()
            WQ = sb(att, [128, 2, 768])
            WKV = sb(att, [128, 1024])
            V = sb(att, [128, 6, 512])
            QR = Ring([sb(att, [96, 768]) for _ in range(2)])
            KRr = Ring([sb(att, [96, 768]) for _ in range(2)])
            Pb = Ring([sb(att, [128, 768]) for _ in range(2)])
            PTb = Ring([sb(att, [128, 768]) for _ in range(2)])
            sm = Ring([sb(att, [128, 4]) for _ in range(4)])
            ACC = sb(att, [128, UW])
            t_wq = load(PO, WQ[:, :, :], io["w_q_b"][l], "q0", t_hh)
            t_wkv = load(PO, WKV[:, :], io["w_kv_b"][l], "q1", t_hh)

            def conv(buf, j, taps, half, w0, bias, acc, after, free):
                n = UW - 32
                last = [None]

                def tap(k):
                    def go():
                        src = buf[:, j, 16 + k - half:16 + k - half + n]
                        w = col[:, w0 + taps * j + k:w0 + taps * j + k + 1]
                        if k == 0:
                            if bias is None:
                                last[0] = DVE.put(lambda e: e.tensor_scalar(acc[:, 0:n], src, w, None, ALU.mult),
                                                  after, free)
                            else:
                                last[0] = DVE.put(lambda e: e.tensor_scalar(acc[:, 0:n], src, w, bias, ALU.mult,
                                                                            ALU.add), after, free)
                        else:
                            last[0] = DVE.put(lambda e: e.scalar_tensor_tensor(acc[:, 0:n], src, w, acc[:, 0:n],
                                                                               ALU.mult, ALU.add), last[0])
                    return go
                return [tap(k) for k in range(taps)], last

            conv_tok = {}
            acc_free = [t_hh]

            def close_conf(j, last):
                def go():
                    for (s0, sn) in both:
                        o = s0 if s0 == 0 else 528
                        t = DVE.put(lambda e: e.tensor_copy(Y[:, 4 + j, s0:s0 + sn], ACC[:, o:o + sn]), last[0], y_free)
                    conv_tok[4 + j] = t
                    acc_free[0] = [t]
                return go

            def close_sc(j, last):
                def go():
                    for (s0, sn) in both:
                        o = s0 if s0 == 0 else 528
                        t = DVE.put(lambda e: e.tensor_tensor(Y[:, 6 + j, s0:s0 + sn], Y[:, 6 + j, s0:s0 + sn],
                                                              ACC[:, o:o + sn], ALU.mult), last[0], t_zdone)
                    conv_tok[6 + j] = t
                    acc_free[0] = [t]
                return go

            for j in range(2):
                fs, last_c = conv(U, j, 31, 15, CW, col[:, DW_B + j:DW_B + j + 1], ACC, t_zdone, acc_free)
                background.extend(fs + [close_conf(j, last_c)])
            for j in range(2):
                fs, last_c = conv(CH, j, 3, 1, SW, None, ACC, t_zdone, acc_free)
                background.extend(fs + [close_sc(j, last_c)])

            def norm_in_place(src, segs, D, g, ready):
                ri, r, tr = rstd(src, segs, D, ones[:, :], ready)
                a, b = span(segs)
                for c, s in enumerate(src):
                    t = DVE.put(lambda e: e.scalar_tensor_tensor(s[:, a:b], s[:, a:b], col[:, g + c:g + c + 1],
                                                                 r[:, a:b], ALU.mult, ALU.mult), tr)
                RS.give(ri, t)
                return t

            t_kvn = norm_in_place([ZKV[:, :]], [LAT, CTX], 128, G_KV, t_zdone)
            t_qn = norm_in_place([ZQ[:, j, :] for j in range(2)], both, 256, G_Q, t_zdone)

            def rope(buf, ready):
                i, p, free = PS.take()
                tm = PE.put(lambda e: e.matmul(p[0:96, 0:512], rotM[:, :], buf[:, 0:512], start=True, stop=True),
                            free, ready, t_tab)
                ti, t, tf = T.take()
                ta = DVE.put(lambda e: e.tensor_tensor(t[0:96, 0:512], p[0:96, 0:512], sinM[:, :], ALU.mult), tm, tf,
                             t_tab)
                PS.give(i, ta)
                tb = DVE.put(lambda e: e.tensor_tensor(buf[:, 0:512], buf[:, 0:512], cosM[:, :], ALU.mult), ready, tm)
                tc = DVE.put(lambda e: e.tensor_tensor(buf[:, 0:512], buf[:, 0:512], t[0:96, 0:512], ALU.add), ta, tb)
                T.give(ti, tc)
                return tc

            t_kr = rope(KR, t_zdone)
            for i, buf in enumerate(KRr.bufs):
                t_kc = DVE.put(lambda e: e.tensor_copy(buf[64:96, :], KR[64:96, :]), t_kr, t_hh)
            t_v = []
            for tt in range(6):
                i, p, free = PS.take()
                tm = PE.put(lambda e: e.matmul(p[:, 0:512], ZKV[:, 128 * tt:128 * tt + 128],
                                               WKV[:, :].rearrange("p (h a d) -> p h a d", h=8, a=2)[:, :, 1, :],
                                               start=True, stop=True), free, t_kvn, t_wkv)
                tc = AC.put(lambda e: e.activation(V[:, tt, :], p[:, 0:512], ACT.Copy), tm, t_hh)
                PS.give(i, tc)
                t_v.append(tc)

            SM = 1.0 / float(np.sqrt(np.float64(96)))

            def head_in(h):
                ki, kb, kf = KRr.take()
                qi, qb, qf = QR.take()
                i, p, free = PS.take()
                PE.wait(free, t_kvn, t_wkv)
                for (s0, sn) in (LAT, CTX):
                    tm = PE.put(lambda e: e.matmul(p[:, s0:s0 + sn], WKV[:, 128 * h:128 * h + 128],
                                                   ZKV[:, s0:s0 + sn], start=True, stop=True))
                tk = AC.put(lambda e: e.activation(kb[0:64, :], p[0:64, 0:768], ACT.Copy), tm, kf, t_kc)
                PS.give(i, tk)
                a, b = span(both)
                i, p, free = PS.take()
                PE.wait(free, t_qn, t_wq)
                for (s0, sn) in both:
                    for k in range(2):
                        tm = PE.put(lambda e: e.matmul(p[0:96, s0:s0 + sn], WQ[:, k, 96 * h:96 * h + 96],
                                                       ZQ[:, k, s0:s0 + sn], start=(k == 0), stop=(k == 1)))
                tq = AC.put(lambda e: e.activation(qb[:, a:b], p[0:96, a:b], ACT.Copy, scale=SM), tm, qf, t_hh)
                PS.give(i, tq)
                tq2 = rope(qb, tq)
                return (ki, kb, [tk, t_kc]), (qi, qb, [tq, tq2])

            class Unit:
                pass

            units = []
            for h in range(8):
                for qt in range(4):
                    units.append((h, 128 * qt, 0, 768, qt == 0))
                if l == 0:
                    for qt in range(2):
                        units.append((h, 512 + 128 * qt, 512, 256, False))
            heads = {0: head_in(0)}
            O = {}

            def scores(h, q0, k0, kn):
                (ki, kb, tk), (qi, qb, tq) = heads[h]
                i, p, free = PS.take()
                PE.wait(free, tk, tq)
                for (s0, sn) in ([LAT, CTX] if kn == 768 else [(0, 256)]):
                    tm = PE.put(lambda e: e.matmul(p[:, s0:s0 + sn], qb[:, q0:q0 + 128], kb[:, k0 + s0:k0 + s0 + sn],
                                                   start=True, stop=True))
                pi, pb, pf = Pb.take()
                mi, m, mf = sm.take()
                t1 = DVE.put(lambda e: e.tensor_reduce(m[:, 0:1], p[:, 0:kn], AX.X, ALU.max, negate=True), tm, mf, t_hh)
                t2 = AC.put(lambda e: e.activation(pb[:, 0:kn], p[:, 0:kn], ACT.Exp, bias=m[:, 0:1],
                                                   accum_out=m[:, 1:2]), t1, pf, t_hh)
                PS.give(i, t2)
                t3 = DVE.put(lambda e: e.reciprocal(m[:, 2:3], m[:, 1:2]), t2)
                t4 = DVE.put(lambda e: e.tensor_scalar(pb[:, 0:kn], pb[:, 0:kn], m[:, 2:3], None, ALU.mult), t3, t2)
                sm.give(mi, t4)
                return tm, pi, pb, t4

            def values(h, q0, k0, kn, s):
                tm, pi, pb, tp = s
                nb = kn // 128
                i, p, free = PS.take()
                PE.wait(free, tp)
                for b in range(nb):
                    tt = PE.put(lambda e: e.transpose(p[:, 128 * b:128 * b + 128], pb[:, 128 * b:128 * b + 128],
                                                      ident[:, :]), count=(b == nb - 1))
                Pb.give(pi, tt)
                ti, ptb, ptf = PTb.take()
                tc = AC.put(lambda e: e.activation(ptb[:, 0:kn], p[:, 0:kn], ACT.Copy), tt, ptf, t_hh)
                PS.give(i, tc)
                if h not in O:
                    O[h] = PS.take()
                oi, o, of = O[h]
                PE.wait(of, tc, t_v)
                hp = 128 * (h // 2)
                for b in range(nb):
                    tv = PE.put(lambda e: e.matmul(o[:, q0:q0 + 128], V[:, k0 // 128 + b, hp:hp + 128],
                                                   ptb[:, 128 * b:128 * b + 128], start=(b == 0), stop=(b == nb - 1)),
                                count=(b == nb - 1))
                PTb.give(ti, tv)
                return tv

            pending = None
            a, b_ = span(both)
            t_att = []
            qend = units and [u for u in units if u[0] == 0][-1][1]

            def finish(u, s):
                h = u[0]
                tv = values(*u[:4], s)
                if u[1] == qend:
                    r0 = 64 * (h % 2)
                    oi, o, _ = O.pop(h)
                    tc = AC.put(lambda e: e.activation(Y[r0:r0 + 64, h // 2, a:b_], o[r0:r0 + 64, a:b_], ACT.Copy),
                                tv, y_free)
                    PS.give(oi, tc)
                    t_att.append(tc)
                    (ki, _, _), (qi, _, _) = heads[h]
                    KRr.give(ki, tv)
                    QR.give(qi, tv)

            for u in units:
                s = scores(*u[:4])
                if pending:
                    finish(*pending)
                if u[1] == 256 and u[0] + 1 < 8:
                    heads[u[0] + 1] = head_in(u[0] + 1)
                pending = (u, s)
                idle(2)
            finish(*pending)
            idle(len(background))

            i, p, free = PS.take()
            PE.wait(free, conv_tok[4], conv_tok[5])
            for (s0, sn) in both:
                for j in range(2):
                    tm = PE.put(lambda e: e.matmul(p[:, s0:s0 + sn], ones[:, :], Y[:, 4 + j, s0:s0 + sn],
                                                   start=(j == 0), stop=(j == 1)))
            for j in range(2):
                td = DVE.put(lambda e: e.scalar_tensor_tensor(Y[:, 4 + j, a:b_], p[:, a:b_], -1.0 / 256,
                                                              Y[:, 4 + j, a:b_], ALU.mult, ALU.add), tm, conv_tok[4 + j])
            PS.give(i, td)
            ri, r, tr = rstd([Y[:, 4 + j, :] for j in range(2)], both, 256, ones[:, :], td)
            for j in range(2):
                tn = DVE.put(lambda e: e.scalar_tensor_tensor(Y[:, 4 + j, a:b_], Y[:, 4 + j, a:b_],
                                                              col[:, LN_G + j:LN_G + j + 1], r[:, a:b_],
                                                              ALU.mult, ALU.mult), tr)
                ts = AC.put(lambda e: e.activation(Y[:, 4 + j, a:b_], Y[:, 4 + j, a:b_], ACT.Silu,
                                                   bias=col[:, LN_B + j:LN_B + j + 1]), tn)
            RS.give(ri, tn)

            att.close()
            z.close()
            HHs = ExitStack()
            HH, HL = sb(HHs, [128, 8, 768], FR), sb(HHs, [128, 8, 768], FR)
            t_free = t_att + [(PE.sem, PE.n), (DVE.sem, DVE.n), (AC.sem, AC.n)]
            gb = lambda c0: (lambda c, s0: col[:, G_BR + c0 + c:G_BR + c0 + c + 1])
            t_m = []
            for c0, n, rdy in ((0, 4, t_att), (4, 2, [ts]), (6, 2, [conv_tok[6], conv_tok[7]])):
                t_m += norm_split([Y[:, c0 + c, :] for c in range(n)], both, 128 * n, gb(c0), None, HH, HL, c0,
                                  rdy, t_free)

            def y_out(c, p, tm, sg):
                t = AC.put(lambda e: e.activation(Y[:, c, a:b_], p[:, a:b_], ACT.Copy), tm, t_m)
                yt.append(t)
                return [t]

            yt = []
            last = linear(4, 8, 256, both, HH, HL, t_m, y_out)
            t_x1 = add_normed(both, 1024, A_(1), yt)
            t_h = norm_split(xs, both, 1024, A_(2), B_(3), HH, HL, 0, [t_x1], [last])
            mm = ExitStack()
            A = [(sb(mm, [128, 4, 768], FR), sb(mm, [128, 4, 768], FR))]

            def sqrelu(g, c, p, tm, ah, al, afree):
                ti, t, tf = T.take()
                t1 = AC.put(lambda e: e.activation(t[:, a:b_], p[:, a:b_], ACT.Relu), tm, tf)
                t2 = DVE.put(lambda e: e.tensor_tensor(t[:, a:b_], t[:, a:b_], t[:, a:b_], ALU.mult), t1)
                t3 = AC.put(lambda e: e.activation(ah[:, a:b_], t[:, a:b_], ACT.Copy), t2, afree)
                t4 = DVE.put(lambda e: e.tensor_tensor(al[:, a:b_], t[:, a:b_], ah[:, a:b_].bitcast(F32),
                                                       ALU.subtract), t3, afree)
                T.give(ti, t4)
                return t4, [t1]

            yl = mlp(8, both, HH, HL, A, t_h, sqrelu, [t_x1])
            t_x2 = add_normed(both, 1024, A_(3), yl)
            mod_read = [t_x2]
            x_ready = [t_x2]
            mm.close()
            HHs.close()
            t_phase = [(PE.sem, PE.n), (DVE.sem, DVE.n), (AC.sem, AC.n)]
        first.close()

        L = [LAT]
        C_N1, C_N2, C_QN, C_KN, C_DQ, C_DK = 0, 8, 16, 17, 20, 23
        second = ExitStack()
        xs = [X[:, c, :] for c in range(8)]
        HHs = ExitStack()
        cosN = sb(second, [128, 512])
        sinN = sb(second, [128, 512])
        rotN = sb(second, [128, 128])
        bones = sb(second, [128, 128])
        t_t2 = [load(PO, cosN[:, :], io["cosN"], "k0", t_phase), load(PO, sinN[:, :], io["sinN"], "k1", t_phase),
                load(PO, rotN[:, :], io["rotN"], "k2", t_phase), load(PO, bones[:, :], io["bones"], "k3", t_phase)]
        HH, HL = sb(HHs, [128, 8, 512], FR), sb(HHs, [128, 8, 512], FR)
        c2 = lambda b0: (lambda c, s0: cols2[:, b0 + c:b0 + c + 1])
        t_h = norm_split(xs, L, 1024, c2(C_N1), None, HH, HL, 0, x_ready, t_phase)
        t_c8 = DVE.put(lambda e: e.tensor_scalar(cols2[:, C_QN:C_QN + 1], cols2[:, C_QN:C_QN + 1], 0.125, None, ALU.mult))
        t_c8 = DVE.put(lambda e: e.tensor_scalar(cols2[:, C_DQ:C_DQ + 3], cols2[:, C_DQ:C_DQ + 3], 0.125, None, ALU.mult))

        def head_norm_rope(zsrc, ready, g, n, dsts, cos, sin, free):
            ri, r, tr = rstd([zsrc], [(0, n)], 64, bones[:, :], ready + t_t2)
            ti, t, tf = T.take()
            t1 = DVE.put(lambda e: e.scalar_tensor_tensor(t[:, 0:n], zsrc[:, 0:n], cols2[:, g:g + 1], r[:, 0:n],
                                                          ALU.mult, ALU.mult), tr, tf, t_c8)
            i, p, pf = PS.take()
            tm = PE.put(lambda e: e.matmul(p[:, 0:n], rotN[:, :], t[:, 0:n], start=True, stop=True), pf, t1, t_t2)
            t2 = DVE.put(lambda e: e.tensor_tensor(r[:, 0:n], p[:, 0:n], sin, ALU.mult), tm, t1)
            PS.give(i, t2)
            t3 = DVE.put(lambda e: e.tensor_tensor(t[:, 0:n], t[:, 0:n], cos, ALU.mult), tm, t1)
            for (r0, r1, ap) in dsts:
                t4 = DVE.put(lambda e: e.tensor_tensor(ap, t[r0:r1, 0:n], r[r0:r1, 0:n], ALU.add), t2, t3, free)
            T.give(ti, t4)
            RS.give(ri, t4)
            return t1, t4

        nsa = ExitStack()
        QN = sb(nsa, [128, 4, 512])
        KS = sb(nsa, [128, 2, 512])
        KW = sb(nsa, [128, 2, 512])
        VSW = sb(nsa, [128, 4, 256])
        KCM = sb(nsa, [128, 2, 32])
        VCM = sb(nsa, [128, 128])
        GT = sb(nsa, [128, 4, 24])
        cmpS = ExitStack()
        KVC = sb(cmpS, [128, 2, 512])
        BLK = Y[:, :, :].rearrange("p c t -> p (c t)")[:, 0:2048].rearrange("p (t c) -> p t c", c=64)
        W1 = sb(cmpS, [128, 32, 256])
        W2 = sb(cmpS, [128, 2, 2, 128])
        PEt = sb(cmpS, [128, 32])
        HID = sb(cmpS, [128, 2, 2, 64])
        cosC = sb(cmpS, [128, 32])
        sinC = sb(cmpS, [128, 32])
        t_cw = [load(PO, W1[:, :, :], io["cmp_w1"], "q0", t_phase), load(PO, W2[:, :, :, :], io["cmp_w2"], "q1", t_phase),
                load(PO, PEt[:, :], io["cmp_pe"], "q2", t_phase), load(PO, cosC[:, :], io["cosC"], "q3", t_phase),
                load(PO, sinC[:, :], io["sinC"], "q4", t_phase)]
        t_ms = [DVE.put(lambda e: e.memset(KS[:, :, :], 0.0), t_phase), DVE.put(lambda e: e.memset(KW[:, :, :], 0.0), t_phase),
                DVE.put(lambda e: e.memset(KCM[:, :, :], 0.0), t_phase), DVE.put(lambda e: e.memset(VCM[:, :], 0.0), t_phase)]
        ORD2 = ["kvc0", "kvc1", "q0", "q1", "q2", "q3", "ks", "kw"]
        zt = {}

        def z2(c, p, tm, sg):
            kind = ORD2[c]
            if kind[0:3] == "kvc":
                j = int(kind[3])
                zt[kind] = AC.put(lambda e: e.activation(KVC[:, j, :], p[:, 0:512], ACT.Copy), tm, t_phase)
                return [zt[kind]]
            if kind[0] == "q":
                j = int(kind[1])
                t1, zt[kind] = head_norm_rope(p, [tm], C_QN, 512, [(0, 128, QN[:, j, :])], cosN[:, :], sinN[:, :], t_phase)
                return [t1]
            dst = KS if kind == "ks" else KW
            t1, zt[kind] = head_norm_rope(p, [tm], C_KN + (1 if kind == "ks" else 2), 512,
                                          [(0, 64, dst[0:64, 0, :]), (64, 128, dst[64:128, 1, :])], cosN[:, :], sinN[:, :],
                                          t_ms)
            return [t1]

        linear(4, 8, 256, L, HH, HL, t_h, z2)

        def token_major(k, wh, wl, wr, ncol, tiles, emit):
            wh = wh[:, 0:8 * ncol].rearrange("p (k n) -> p k n", k=8)
            wl = wl[:, 0:8 * ncol].rearrange("p (k n) -> p k n", k=8)
            for tt, tok in enumerate(tiles):
                i, p, free = PS.take()
                PE.wait(free, wr, t_h)
                for kk in range(8):
                    last = three(p[:, 0:ncol], HH[:, kk, tok], HL[:, kk, tok], wh[:, kk, :], wl[:, kk, :],
                                 kk == 0, kk == 7)
                PS.give(i, *emit(tt, p, last))
            give_slab(k, last)

        nat = [slice(128 * i, 128 * i + 128) for i in range(4)]
        k, wh, wl, wr = take_slab()
        zv = []

        def v_out(tt, p, tm):
            zv.append(AC.put(lambda e: e.activation(VSW[:, tt, :], p[:, 0:256], ACT.Copy), tm, t_phase))
            return [zv[-1]]

        token_major(k, wh, wl, wr, 256, nat, v_out)
        kv4 = KVC[:, :, :]
        for g in range(2):
            src = KVC[:, g, 0:496].rearrange("p (c t) -> p c t", t=16)
            for hf in range(2):
                s = KVC[:, g, 16 * hf:16 * hf + 496].rearrange("p (c t) -> p t c", t=16)
                pe = PEt[:, 16 * hf:16 * hf + 16].rearrange("p (t c) -> p t c", c=1).broadcast_to([128, 16, 31])
                t_blk = DVE.put(lambda e: e.tensor_tensor(BLK[:, 16 * hf:16 * hf + 16, 31 * g:31 * g + 31], s, pe, ALU.add),
                                zt[f"kvc{g}"], t_cw, t_phase)
        for kv in range(2):
            rows = slice(64 * kv, 64 * kv + 64)
            i, p, free = PS.take()
            PE.wait(free, t_blk, t_cw)
            for hc in range(2):
                for tp in range(32):
                    tm = PE.put(lambda e: e.matmul(p[:, 64 * hc:64 * hc + 62], W1[rows, tp, 128 * hc:128 * hc + 128],
                                                   BLK[rows, tp, 0:62], start=(tp == 0), stop=(tp == 31)),
                                count=(tp == 31))
            t_hid = AC.put(lambda e: e.activation(HID[:, kv, :, 0:62], p[:, 0:128].rearrange("p (a b) -> p a b", a=2)[:, :, 0:62],
                                                  ACT.Gelu_apprx_tanh), tm, t_phase)
            PS.give(i, t_hid)
            i, p, free = PS.take()
            PE.wait(free, t_hid, t_cw)
            if kv == 0:
                for hc in range(2):
                    tm = PE.put(lambda e: e.matmul(p[:, 0:62], W2[:, 0, hc, :], HID[:, 0, hc, 0:62], start=(hc == 0),
                                                   stop=(hc == 1)))
                kz = sb(cmpS, [128, 32])
                ta = AC.put(lambda e: e.activation(kz[0:64, 0:31], p[0:64, 0:31], ACT.Copy), tm, t_phase)
                tb = AC.put(lambda e: e.activation(kz[64:128, 0:31], p[64:128, 31:62], ACT.Copy), tm, t_phase)
                PS.give(i, tb)
                _, t_kcm = head_norm_rope(kz, [ta, tb], C_KN, 31, [(0, 64, KCM[0:64, 0, 0:31]), (64, 128, KCM[64:128, 1, 0:31])],
                                          cosC[:, 0:31], sinC[:, 0:31], t_ms)
            else:
                for g in range(2):
                    for hc in range(2):
                        tm = PE.put(lambda e: e.matmul(p[0:31, 64 * g:64 * g + 64], HID[:, 1, hc, 31 * g:31 * g + 31],
                                                       W2[:, 1, hc, 0:64], start=(hc == 0), stop=(hc == 1)))
                t_vcm = AC.put(lambda e: e.activation(VCM[0:31, :], p[0:31, 0:128], ACT.Copy), tm, t_ms)
                PS.give(i, t_vcm)
        cmpS.close()
        k, wh, wl, wr = take_slab()

        def g_out(tt, p, tm):
            zv.append(AC.put(lambda e: e.activation(GT[:, tt, :], p[:, 0:24], ACT.Sigmoid), tm, t_phase))
            return [zv[-1]]

        token_major(k, wh, wl, wr, 24, nat, g_out)
        attS = ExitStack()
        t_free = [(PE.sem, PE.n), (DVE.sem, DVE.n), (AC.sem, AC.n)]
        CM = sb(attS, [128, 2, 4, 32])
        SL = sb(attS, [128, 896])
        PC = Ring([sb(attS, [128, 8, 128])])
        PTC = Ring([sb(attS, [128, 8, 128])])
        Pb = Ring([sb(attS, [128, 1024]) for _ in range(2)])
        PTb = Ring([sb(attS, [128, 1024]) for _ in range(2)])
        sm = Ring([sb(attS, [128, 8]) for _ in range(4)])
        cs = Ring([sb(attS, [128, 4, 8]) for _ in range(2)])
        t_mk = [load(PO, CM[:, :, :, :], io["cmask"], "q0", t_free), load(PO, SL[:, :], io["slide"], "q1", t_free)]
        t_pc0 = DVE.put(lambda e: e.memset(PC.bufs[0][:, :, :], 0.0), t_free)
        t_yn = []
        bc3 = lambda ap, sh: ap.broadcast_to(sh)
        for qt in range(4):
            qs = slice(128 * qt, 128 * qt + 128)
            Lk = 128 * (qt + 1)
            i, p, free = PS.take()
            PE.wait(free, zt["q3"], t_kcm, zt["kw"])
            for h in range(8):
                tm = PE.put(lambda e: e.matmul(p[:, 32 * h:32 * h + 32], QN[:, h % 4, qs], KCM[:, h // 4, :],
                                               start=True, stop=True), count=(h == 7))
            pi, pc, pcf = PC.take()
            ci, cst, cf = cs.take()
            pcv = pc[:, :, 0:31]
            pv3 = p[:, 0:256].rearrange("p (h c) -> p h c", h=8)[:, :, 0:31]
            msk = CM[:, 0, qt, 0:31].rearrange("p (o c) -> p o c", o=1).broadcast_to([128, 8, 31])
            val = CM[:, 1, qt, 0:31].rearrange("p (o c) -> p o c", o=1).broadcast_to([128, 8, 31])
            vec = lambda j: cst[:, j, :].rearrange("p (h o) -> p h o", o=1)
            b8 = lambda j: vec(j).broadcast_to([128, 8, 31])
            t1 = DVE.put(lambda e: e.tensor_tensor(pcv, pv3, msk, ALU.add), tm, pcf, t_mk, t_pc0)
            PS.give(i, t1)
            t2 = DVE.put(lambda e: e.tensor_reduce(cst[:, 0, :], pcv, AX.X, ALU.max), t1, cf, t_free)
            t3 = DVE.put(lambda e: e.tensor_tensor(pcv, pcv, b8(0), ALU.subtract), t2)
            t4 = AC.put(lambda e: e.activation(pcv, pcv, ACT.Exp), t3)
            t5 = DVE.put(lambda e: e.tensor_reduce(cst[:, 1, :], pcv, AX.X, ALU.add), t4)
            t6 = DVE.put(lambda e: e.reciprocal(cst[:, 2, :], cst[:, 1, :]), t5)
            gates = GT[:, qt, :].rearrange("p (h b) -> p h b", b=3)
            t7 = DVE.put(lambda e: e.tensor_tensor(cst[:, 3, :], cst[:, 2, :], gates[:, :, 0], ALU.mult), t6, zv)
            t8 = DVE.put(lambda e: e.tensor_tensor(pcv, pcv, b8(3), ALU.mult), t7)
            t9 = DVE.put(lambda e: e.tensor_tensor(pcv, pcv, val, ALU.mult), t8)
            cs.give(ci, t9)
            i, p, free = PS.take()
            PE.wait(free, t9)
            for h in range(8):
                tm = PE.put(lambda e: e.transpose(p[:, 128 * h:128 * h + 128], pc[:, h, :], ident[:, :]), count=(h == 7))
            PC.give(pi, tm)
            ti, ptc, tf = PTC.take()
            t_ptc = AC.put(lambda e: e.activation(ptc[:, :, :], p[:, :].rearrange("p (h q) -> p h q", h=8), ACT.Copy), tm, tf,
                           t_free)
            PS.give(i, t_ptc)
            pend = None
            O = {}

            def nsa_scores(h):
                g, c = h // 4, h % 4
                i, p, free = PS.take()
                PE.wait(free, zt["q3"], zt["ks"], zt["kw"])
                for j, kk in enumerate((KS, KW)):
                    tm = PE.put(lambda e: e.matmul(p[:, 512 * j:512 * j + Lk], QN[:, c, qs], kk[:, g, 0:Lk],
                                                   start=True, stop=True))
                pi, pb, pf = Pb.take()
                mi, m, mf = sm.take()
                off = 384 - 128 * qt
                te = []
                for j in range(2):
                    pp = pb[:, Lk * j:Lk * j + Lk]
                    t1 = DVE.put(lambda e: e.tensor_tensor_reduce(pp, p[:, 512 * j:512 * j + Lk], SL[:, off:off + Lk], 1.0,
                                                                  -3e38, ALU.add, ALU.max, m[:, j:j + 1]),
                                 tm, pf, mf, t_mk, t_free)
                t1 = DVE.put(lambda e: e.tensor_scalar(m[:, 2:4], m[:, 0:2], -1.0, None, ALU.mult), t1)
                PS.give(i, t1)
                for j in range(2):
                    pp = pb[:, Lk * j:Lk * j + Lk]
                    t2 = AC.put(lambda e: e.activation(pp, pp, ACT.Exp, bias=m[:, 2 + j:3 + j], accum_out=m[:, 4 + j:5 + j]),
                                t1)
                t3 = DVE.put(lambda e: e.reciprocal(m[:, 6:8], m[:, 4:6]), t2)
                t4 = DVE.put(lambda e: e.tensor_tensor(m[:, 6:8], m[:, 6:8], GT[:, qt, 3 * h + 1:3 * h + 3], ALU.mult), t3, zv)
                for j in range(2):
                    pp = pb[:, Lk * j:Lk * j + Lk]
                    t5 = DVE.put(lambda e: e.tensor_scalar(pp, pp, m[:, 6 + j:7 + j], None, ALU.mult), t4)
                sm.give(mi, t5)
                return h, pi, pb, t5

            def nsa_values(h, pi, pb, tp):
                g, c = h // 4, h % 4
                nb = qt + 1
                i, p, free = PS.take()
                PE.wait(free, tp)
                for b in range(2 * nb):
                    tt = PE.put(lambda e: e.transpose(p[:, 128 * b:128 * b + 128], pb[:, 128 * b:128 * b + 128], ident[:, :]),
                                count=(b == 2 * nb - 1))
                Pb.give(pi, tt)
                ti2, ptb, ptf = PTb.take()
                tc = AC.put(lambda e: e.activation(ptb[:, 0:256 * nb], p[:, 0:256 * nb], ACT.Copy), tt, ptf, t_free)
                PS.give(i, tc)
                oi, o, of = PS.take()
                PE.wait(of, t_ptc, t_vcm, zv)
                oo = o[:, 0:128]
                PE.put(lambda e: e.matmul(oo, VCM[:, :], ptc[:, h, :], start=True, stop=False), count=False)
                PE.wait(tc)
                for j in range(2):
                    for b in range(nb):
                        end = j == 1 and b == nb - 1
                        tv = PE.put(lambda e: e.matmul(oo, VSW[:, b, 128 * j:128 * j + 128],
                                                       ptb[:, 128 * (nb * j + b):128 * (nb * j + b) + 128],
                                                       start=False, stop=end), count=end)
                PTb.give(ti2, tv)
                r0 = 64 * g
                ty = AC.put(lambda e: e.activation(Y[r0:r0 + 64, c, qs], o[r0:r0 + 64, 0:128], ACT.Copy), tv, t_phase)
                PS.give(oi, ty)
                t_yn.append(ty)
                return tv

            for h in range(8):
                s = nsa_scores(h)
                if pend:
                    nsa_values(*pend)
                pend = s
            tv = nsa_values(*pend)
            PTC.give(ti, tv)
        attS.close()
        nsa.close()

        dil = ExitStack()
        t_free = [(PE.sem, PE.n), (DVE.sem, DVE.n), (AC.sem, AC.n)]
        QD = sb(dil, [128, 3, 512])
        KD = sb(dil, [128, 3, 2, 512])
        VD = sb(dil, [128, 3, 4, 128])
        MK = sb(dil, [128, 4, 768])
        Pb = Ring([sb(dil, [128, 768]) for _ in range(2)])
        PTb = Ring([sb(dil, [128, 768]) for _ in range(2)])
        sm = Ring([sb(dil, [128, 4]) for _ in range(4)])
        t_mk = load(PO, MK[:, :, :], io["dmask"], "q0", t_free)
        t_ms = DVE.put(lambda e: e.memset(KD[:, :, :, :], 0.0), t_free)
        strided = [slice(a, 512, 4) for a in range(4)]
        d_free = t_free
        t_yd = []
        for hp in range(2):
            dq, dk, dv = {}, {}, []

            def d_out(c, p, tm, sg):
                g = c // 2
                if c % 2 == 0:
                    t1, dq[g] = head_norm_rope(p, [tm], C_DQ + g, 512, [(0, 128, QD[:, g, :])], cosN[:, :], sinN[:, :], d_free)
                else:
                    t1, dk[g] = head_norm_rope(p, [tm], C_DK + g, 512, [(0, 64, KD[0:64, g, 0, :]), (64, 128, KD[64:128, g, 1, :])],
                                               cosN[:, :], sinN[:, :], [t_ms] + d_free)
                return [t1]

            linear(3, 8, 256, L, HH, HL, t_h, d_out)
            for g, tiles in ((0, nat), (1, strided), (2, strided)):
                if g < 2:
                    if g == 0:
                        k, wh, wl, wr = take_slab()
                    w0 = 128 * g
                else:
                    give_slab(k, tl)
                    k, wh, wl, wr = take_slab()
                    w0 = 0
                nc_ = 256 if g < 2 else 128
                whv = wh[:, 0:8 * nc_].rearrange("p (k n) -> p k n", k=8)
                wlv = wl[:, 0:8 * nc_].rearrange("p (k n) -> p k n", k=8)
                for tt, tok in enumerate(tiles):
                    i, p, free = PS.take()
                    PE.wait(free, wr, t_h)
                    for kk in range(8):
                        tl = three(p[:, 0:128], HH[:, kk, tok], HL[:, kk, tok], whv[:, kk, w0:w0 + 128],
                                   wlv[:, kk, w0:w0 + 128], kk == 0, kk == 7)
                    tc = AC.put(lambda e: e.activation(VD[:, g, tt, :], p[:, 0:128], ACT.Copy), tl, d_free)
                    PS.give(i, tc)
                    dv.append(tc)
            give_slab(k, tl)

            def d_scores(a, j):
                i, p, free = PS.take()
                PE.wait(free, [dq[g] for g in range(3)], [dk[g] for g in range(3)])
                for g in range(3):
                    o = p[:, 0:512] if g == 0 else p[:, 384 + 128 * g:512 + 128 * g]
                    kk = KD[:, g, j, :] if g == 0 else KD[:, g, j, strided[a]]
                    tm = PE.put(lambda e: e.matmul(o, QD[:, g, strided[a]], kk, start=True, stop=True), count=(g == 2))
                pi, pb, pf = Pb.take()
                mi, m, mf = sm.take()
                t1 = DVE.put(lambda e: e.tensor_tensor_reduce(pb[:, :], p[:, 0:768], MK[:, a, :], 1.0, -3e38, ALU.add,
                                                              ALU.max, m[:, 0:1]), tm, pf, mf, t_mk, t_free)
                PS.give(i, t1)
                t2 = DVE.put(lambda e: e.tensor_scalar(m[:, 3:4], m[:, 0:1], -1.0, None, ALU.mult), t1)
                t3 = AC.put(lambda e: e.activation(pb[:, :], pb[:, :], ACT.Exp, bias=m[:, 3:4], accum_out=m[:, 1:2]), t2, t1)
                t4 = DVE.put(lambda e: e.reciprocal(m[:, 2:3], m[:, 1:2]), t3)
                t5 = DVE.put(lambda e: e.tensor_scalar(pb[:, :], pb[:, :], m[:, 2:3], None, ALU.mult), t4)
                sm.give(mi, t5)
                return a, j, pi, pb, t5

            def d_values(a, j, pi, pb, tp):
                i, p, free = PS.take()
                PE.wait(free, tp)
                for b in range(6):
                    tt = PE.put(lambda e: e.transpose(p[:, 128 * b:128 * b + 128], pb[:, 128 * b:128 * b + 128], ident[:, :]),
                                count=(b == 5))
                Pb.give(pi, tt)
                ti, ptb, ptf = PTb.take()
                tc = AC.put(lambda e: e.activation(ptb[:, :], p[:, 0:768], ACT.Copy), tt, ptf, t_free)
                PS.give(i, tc)
                oi, o, of = PS.take()
                PE.wait(of, tc, dv)
                for b in range(6):
                    vv = VD[:, 0, b, :] if b < 4 else VD[:, b - 3, a, :]
                    tv = PE.put(lambda e: e.matmul(o[:, 0:128], vv, ptb[:, 128 * b:128 * b + 128], start=(b == 0), stop=(b == 5)),
                                count=(b == 5))
                PTb.give(ti, tv)
                r0 = 64 * j
                ty = AC.put(lambda e: e.activation(Y[r0:r0 + 64, 4 + hp, strided[a]], o[r0:r0 + 64, 0:128], ACT.Copy), tv, t_phase)
                PS.give(oi, ty)
                t_yd.append(ty)
                return tv

            pend = None
            for a in range(4):
                for j in range(2):
                    s = d_scores(a, j)
                    if pend:
                        d_values(*pend)
                    pend = s
            tv = d_values(*pend)
            d_free = [tv]
        dil.close()

        t_free = [(PE.sem, PE.n), (DVE.sem, DVE.n), (AC.sem, AC.n)]
        mg = ExitStack()
        YH, YL = sb(mg, [128, 6, 512], FR), sb(mg, [128, 6, 512], FR)
        UP = sb(mg, [128, 16, 512])
        t_y = []
        for c in range(6):
            th = AC.put(lambda e: e.activation(YH[:, c, :], Y[:, c, 0:512], ACT.Copy), t_yn, t_yd, t_free)
            tl = DVE.put(lambda e: e.tensor_tensor(YL[:, c, :], Y[:, c, 0:512], YH[:, c, :].bitcast(F32), ALU.subtract), th, t_free)
            t_y = [th, tl]
        ups = []

        def up_out(base):
            def f(c, p, tm, sg):
                t = AC.put(lambda e: e.activation(UP[:, base + c, :], p[:, 0:512], ACT.Copy), tm, t_free)
                ups.append(t)
                return [t]
            return f

        linear(2, 4, 512, L, YH, YL, t_y, up_out(0))
        linear(1, 2, 1024, L, YH[:, 4:6, :], YL[:, 4:6, :], t_y, up_out(8))
        mt = {}
        t_mg = []

        def mg_out(c, p, tm, sg):
            j, b = c // 2, c % 2
            ti, t, tf = T.take()
            t1 = AC.put(lambda e: e.activation(t[:, 0:512], p[:, 0:512], ACT.Sigmoid), tm, tf)
            u = UP[:, 8 * b + j, :]
            t2 = DVE.put(lambda e: e.tensor_tensor(u, u, t[:, 0:512], ALU.mult), t1, ups)
            T.give(ti, t2)
            if b == 1:
                t3 = DVE.put(lambda e: e.tensor_tensor(UP[:, j, :], UP[:, j, :], UP[:, 8 + j, :], ALU.add), t2)
                t_mg.append(t3)
            return [t1]

        last = linear(8, 8, 256, L, HH, HL, t_h, mg_out)
        t_m = []
        for c in range(8):
            th = AC.put(lambda e: e.activation(HH[:, c, :], UP[:, c, :], ACT.Copy), t_mg, last)
            tl = DVE.put(lambda e: e.tensor_tensor(HL[:, c, :], UP[:, c, :], HH[:, c, :].bitcast(F32), ALU.subtract), th)
            t_m = [th, tl]
        t_xx = []

        def x_out(c, p, tm, sg):
            t = DVE.put(lambda e: e.tensor_tensor(X[:, c, 0:512], X[:, c, 0:512], p[:, 0:512], ALU.add), tm)
            t_xx.append(t)
            return [t]

        last = linear(4, 8, 256, L, HH, HL, t_m, x_out)
        mg.close()

        t_h = norm_split(xs, L, 1024, c2(C_N2), None, HH, HL, 0, t_xx, [last])
        t_free = [(PE.sem, PE.n), (DVE.sem, DVE.n), (AC.sem, AC.n)]
        pr = ExitStack()
        E1 = sb(pr, [128, 512])
        E2 = sb(pr, [128, 512])
        GG = sb(pr, [128, 512])
        IO = sb(pr, [128, 128])
        t_io = load(PO, IO[:, :], io["iota"], "q0", t_free)
        tk = ExitStack()
        QP = sb(tk, [128, 8, 512])
        SK = sb(tk, [128, 256])
        S = sb(tk, [128, 16, 128])
        S2 = sb(tk, [128, 2048])
        M1 = sb(tk, [128, 16, 16])
        I1 = sb(tk, [128, 16, 16], U32)
        F1 = sb(tk, [128, 16, 16])
        M2 = sb(tk, [128, 8, 16])
        I2 = sb(tk, [128, 8, 16], U32)
        AB2 = sb(tk, [128, 2, 128], U32)
        AF = sb(tk, [128, 2, 128])
        EE = sb(tk, [128, 3, 128])
        sg_ = sb(tk, [128, 3, 8])
        CAND = sb(tk, [128, 8, 16, 16])
        t_sk = load(PO, SK[:, :], io["subk"], "q1", t_free)
        tq = []

        def q_out(c, p, tm, sg):
            t = AC.put(lambda e: e.activation(QP[:, c, :], p[:, 0:512], ACT.Copy), tm, t_free)
            tq.append(t)
            return [t]

        linear(4, 8, 256, L, HH, HL, t_h, q_out)
        t_S = None
        t_e = []
        for tt in range(4):
            ts = slice(128 * tt, 128 * tt + 128)
            tS = []
            for hf in range(2):
                i, p, free = PS.take()
                PE.wait(free, tq, t_sk)
                for h in range(4):
                    tm = PE.put(lambda e: e.matmul(p[:, 256 * h:256 * h + 256], QP[:, 4 * hf + h, ts], SK[:, :],
                                                   start=True, stop=True), count=(h == 3))
                tS.append(AC.put(lambda e: e.activation(S[:, 8 * hf:8 * hf + 8, :],
                                                        p[:, :].rearrange("p (a b) -> p a b", a=8), ACT.Copy),
                                 tm, t_S, t_free))
                PS.give(i, tS[-1])

            def top16(src, tmp, mx, ix, after):
                ta = DVE.put(lambda e: e.max(mx[:, 0:8], src), after)
                tb = DVE.put(lambda e: e.max_index(ix[:, 0:8], mx[:, 0:8], src), ta)
                tc = DVE.put(lambda e: e.match_replace(tmp, mx[:, 0:8], src, -3e38), ta)
                td = DVE.put(lambda e: e.max(mx[:, 8:16], tmp), tc)
                return DVE.put(lambda e: e.max_index(ix[:, 8:16], mx[:, 8:16], tmp), td)

            for j in range(16):
                t1 = top16(S[:, j, :], S2[:, 128 * j:128 * j + 128], M1[:, j, :], I1[:, j, :], [tS, t_e])
            t_S = t1
            m4 = M1[:, :, :].rearrange("p (h c) k -> p h c k", c=2)
            tcd = []
            for h in range(8):
                sa = M1[:, 2 * h, :].rearrange("p (k o) -> p k o", o=1).broadcast_to([128, 16, 16])
                sbb = M1[:, 2 * h + 1, :].rearrange("p (o k) -> p o k", o=1).broadcast_to([128, 16, 16])
                t2 = DVE.put(lambda e: e.tensor_tensor(CAND[:, h, :, :], sa, sbb, ALU.add), t1, t_free)
                t3 = top16(CAND[:, h, :, :].rearrange("p a b -> p (a b)"), S2[:, 256 * h:256 * h + 256], M2[:, h, :], I2[:, h, :],
                           [t2])
            vec = lambda j: sg_[:, j, :].rearrange("p (h o) -> p h o", o=1).broadcast_to([128, 8, 16])
            gv = EE[:, 2, :].rearrange("p (h k) -> p h k", h=8)
            t4 = DVE.put(lambda e: e.tensor_tensor(gv, M2[:, :, :], M2[:, :, 0:1].broadcast_to([128, 8, 16]), ALU.subtract),
                         t3, t_e)
            t5 = AC.put(lambda e: e.activation(gv, gv, ACT.Exp), t4)
            t6 = DVE.put(lambda e: e.tensor_reduce(sg_[:, 0, :], gv, AX.X, ALU.add), t5)
            t7 = DVE.put(lambda e: e.reciprocal(sg_[:, 1, :], sg_[:, 0, :]), t6)
            t8 = DVE.put(lambda e: e.tensor_tensor(gv, gv, vec(1), ALU.mult), t7)
            ix = I2[:, :, :].rearrange("p h k -> p (h k)")
            t9 = DVE.put(lambda e: e.tensor_scalar(AB2[:, 0, :], ix, 4, None, ALU.logical_shift_right), t3)
            t10 = DVE.put(lambda e: e.tensor_scalar(AB2[:, 1, :], ix, 15, None, ALU.bitwise_and), t3)
            t11 = DVE.put(lambda e: e.tensor_copy(AF[:, :, :], AB2[:, :, :]), t9, t10)
            t12 = DVE.put(lambda e: e.tensor_copy(F1[:, :, :], I1[:, :, :]), t1, t11)
            f4 = F1[:, :, :].rearrange("p (h c) k -> p h c k", c=2)
            for c in range(2):
                cm = CAND[:, :, :, :].rearrange("p h a b -> p (h a) b")
                t13 = DVE.put(lambda e: e.tensor_tensor(
                    cm, AF[:, c, :].rearrange("p (k o) -> p k o", o=1).broadcast_to([128, 128, 16]),
                    IO[:, 0:16].rearrange("p (o k) -> p o k", o=1).broadcast_to([128, 128, 16]), ALU.is_equal), t12, t_io)
                for h in range(8):
                    t14 = DVE.put(lambda e: e.tensor_tensor(
                        CAND[:, h, :, :], CAND[:, h, :, :],
                        F1[:, 2 * h + c, :].rearrange("p (o k) -> p o k", o=1).broadcast_to([128, 16, 16]), ALU.mult), t13)
                t12 = DVE.put(lambda e: e.tensor_reduce(EE[:, c, :], cm, AX.X, ALU.add), t14, t_e)
            i, p, free = PS.take()
            PE.wait(free, t12, t8)
            for c in range(3):
                tm = PE.put(lambda e: e.transpose(p[:, 128 * c:128 * c + 128], EE[:, c, :], ident[:, :]))
            for c, dst in enumerate((E1, E2, GG)):
                te = AC.put(lambda e: e.activation(dst[:, ts], p[:, 128 * c:128 * c + 128], ACT.Copy), tm, t_free)
            PS.give(i, te)
            t_e = [tm]
            t_ee = te
        tk.close()
        t_free = [(PE.sem, PE.n), (DVE.sem, DVE.n), (AC.sem, AC.n)]
        gs = ExitStack()
        GST = Ring([sb(gs, [128, 128, 32]) for _ in range(3)])
        yf = Y[:, :, :].rearrange("p c t -> p (c t)")
        OH = Ring([yf[:, 2048 * i:2048 * i + 2048].rearrange("p (c t n) -> p c t n", c=2, t=8) for i in range(3)])
        t_gw = []
        for blk in range(16):
            gi, gst, gf = GST.take()
            for o8 in range(4):
                oi, oh, of = OH.take()
                i, p, free = PS.take()
                PE.wait(free)
                for t in range(8):
                    tok = 32 * blk + 8 * o8 + t
                    ta = DVE.put(lambda e: e.tensor_scalar(oh[:, 0, t, :], IO[:, :], E1[:, tok:tok + 1], GG[:, tok:tok + 1],
                                                           ALU.is_equal, ALU.mult), of, t_ee, t_free, count=False)
                    tb = DVE.put(lambda e: e.tensor_scalar(oh[:, 1, t, :], IO[:, :], E2[:, tok:tok + 1], None, ALU.is_equal))
                    tm = PE.put(lambda e: e.matmul(p[:, 128 * t:128 * t + 128], oh[:, 1, t, :], oh[:, 0, t, :],
                                                   start=True, stop=True), tb, count=(t == 7))
                OH.give(oi, tm)
                tg = AC.put(lambda e: e.activation(gst[:, :, 8 * o8:8 * o8 + 8].rearrange("p n t -> p t n"),
                                                   p[:, :].rearrange("p (t n) -> p t n", t=8), ACT.Copy), tm, gf, t_free)
                PS.give(i, tg)
            tw = load(SP, io["gdram"][blk].rearrange("n p c -> p n c"),
                      gst[:, :, :].rearrange("p (n c) t -> p n (c t)", n=32), f"g{blk % 3}", tg)
            GST.give(gi, tw)
            t_gw.append(tw)
        gs.close()
        pr.close()
        ex = ExitStack()
        t_free = [(PE.sem, PE.n), (DVE.sem, DVE.n), (AC.sem, AC.n)] + t_gw[-3:]
        A = [(sb(ex, [128, 4, 512], FR), sb(ex, [128, 4, 512], FR)) for _ in range(1)]
        GR = [sb(ex, [128, 16, 4, 32]) for _ in range(2)]
        g_free = [None, None]
        g_tok = {}

        def fetch(g):
            if g < 32:
                g_tok[g] = load(PO, GR[g % 2][:, :, :, :].rearrange("p b c t -> p b (c t)"),
                                io["gdram"][:, g].rearrange("b p c -> p b c"), f"r{g % 2}", t_free, g_free[g % 2])

        fetch(0)
        fetch(1)

        def expert(g, c, p, tm, ah, al, afree):
            ti, t, tf = T.take()
            t1 = AC.put(lambda e: e.activation(t[:, 0:512], p[:, 0:512], ACT.Gelu_apprx_tanh), tm, tf)
            tv = t[:, 0:512].rearrange("p (b t) -> p b t", b=16)
            t2 = DVE.put(lambda e: e.tensor_tensor(tv, tv, GR[g % 2][:, :, c, :], ALU.mult), t1, g_tok[g])
            if c == 3:
                g_free[g % 2] = [t2]
                fetch(g + 2)
            t3 = AC.put(lambda e: e.activation(ah, t[:, 0:512], ACT.Copy), t2, afree, t_free)
            t4 = DVE.put(lambda e: e.tensor_tensor(al, t[:, 0:512], ah.bitcast(F32), ALU.subtract), t3, afree, t_free)
            T.give(ti, t4)
            return t4, [t1]

        yl = mlp(32, L, HH, HL, A, t_h, expert, t_free)
        for c in range(8):
            t = DVE.put(lambda e: e.tensor_tensor(X[:, c, 0:512], X[:, c, 0:512], Y[:, c, 0:512], ALU.add), yl[c])
            t_o = load(SP, out_d[:, c, :], X[:, c, 0:512], "o", t)
        SP.wait(t_o, t_gw[-3:])
        ex.close()
        HHs.close()
        second.close()
        assert cur[0] == len(plan), (cur[0], len(plan))



def slabs(w, kc, ncol):
    k, n = w.shape
    w = w.reshape(k // (128 * kc), kc, 128, n // ncol, ncol)
    return np.ascontiguousarray(w.transpose(0, 3, 2, 1, 4)).reshape(k // (128 * kc), n // ncol, 128, kc * ncol)


def columns(v):
    return np.ascontiguousarray(np.asarray(v).reshape(-1, 128).T)


def tables():
    f = np.float32
    t = np.arange(512)
    inv = (f(1.0) / (f(10000.0) ** (np.arange(0, 16, 2, dtype=f) / f(16)))).astype(f)
    ar, ac = (t // 64).astype(f)[:, None] * inv, (t % 64).astype(f)[:, None] * inv
    ang = np.concatenate([ar, ar, ac, ac], -1).astype(f)
    cosM, sinM = np.ones((96, 512), f), np.zeros((96, 512), f)
    cosM[64:], sinM[64:] = np.cos(ang).T, np.sin(ang).T
    rotM = np.zeros((96, 96), f)
    for o in (64, 80):
        for i in range(8):
            rotM[o + 8 + i, o + i] = -1
            rotM[o + i, o + 8 + i] = 1
    inv2 = (f(500000.0) ** (-(np.arange(8, dtype=f) * f(2.0) / f(16)))).astype(f)

    def rope2(pos):
        a = (pos.astype(f)[:, None] * inv2[None, :]).astype(f)
        c, s = np.ones((128, len(pos)), f), np.zeros((128, len(pos)), f)
        for o in (0, 8, 64, 72):
            c[o:o + 8], s[o:o + 8] = np.cos(a).T, np.sin(a).T
        return c, s

    cosN, sinN = rope2(t)
    end = np.arange(31) * 16 + 31
    cc, ss = rope2(end)
    cosC, sinC = np.ones((128, 32), f), np.zeros((128, 32), f)
    cosC[:, 0:31], sinC[:, 0:31] = cc, ss
    rotN = np.zeros((128, 128), f)
    for o in (0, 64):
        for i in range(8):
            rotN[o + 8 + i, o + i] = -1
            rotN[o + i, o + 8 + i] = 1
    bones = np.zeros((128, 128), f)
    bones[:64, :64] = 1
    bones[64:, 64:] = 1
    valid = end[None, :] <= t[:, None]
    cmask = np.zeros((128, 2, 4, 32), f)
    cmask[:, 0, :, 0:31] = np.where(valid, 0, NEG).reshape(4, 128, 31).transpose(1, 0, 2)
    cmask[:, 1, :, 0:31] = valid.reshape(4, 128, 31).transpose(1, 0, 2)
    p = np.arange(128)
    slide = np.where(np.arange(896)[None, :] <= p[:, None] + 384, 0, NEG).astype(f)
    dmask = np.zeros((128, 4, 768), f)
    for a in range(4):
        q = 4 * p + a
        d = q[:, None] - t[None, :]
        dmask[:, a, 0:512] = np.where((d >= 0) & (d <= 128), 0, NEG)
        d = p[:, None] - p[None, :]
        dmask[:, a, 512:640] = np.where(d >= 0, 0, NEG)
        dmask[:, a, 640:768] = np.where((d >= 0) & (d % 4 == 0), 0, NEG)
    iota = np.tile(np.arange(128, dtype=f), (128, 1))
    return dict(cosM=cosM, sinM=sinM, rotM=rotM, cosN=cosN, sinN=sinN, cosC=cosC, sinC=sinC, rotN=rotN, bones=bones,
                cmask=cmask, slide=slide, dmask=dmask, iota=iota, ident=np.eye(128, dtype=f), ones=np.ones((128, 128), f))


def lay_out(a):
    a = {k: np.asarray(v) for k, v in a.items()}
    f = np.float32
    d = dict(tables())
    rows3 = lambda x: np.ascontiguousarray(x.T.reshape(8, 128, -1).transpose(1, 0, 2))
    d["xT"] = rows3(a["x"][0])
    d["ctxT"] = rows3(a["ctx"][0])
    d["cT"] = np.ascontiguousarray(np.stack([a["c"][0].reshape(8, 128).T, a["c_ctx"].reshape(8, 128).T], -1))
    cols = []
    for l in range(2):
        cw = a["conf_dw_w"][l].reshape(31, 2, 128).transpose(2, 1, 0).reshape(128, 62)
        sw = a["sc_dw_w"][l].reshape(3, 2, 128).transpose(2, 1, 0).reshape(128, 6)
        cols.append(np.concatenate([columns(a[n][l]) for n in ("g_pre_mix", "g_post_mix", "g_pre_mlp", "g_post_mlp", "g_q", "g_kv",
                                                              "conf_dw_b", "conf_ln_g", "conf_ln_b", "g_branch")]
                                   + [cw, sw, columns(a["b_mod"][l])], 1))
    d["cols"] = np.ascontiguousarray(np.stack(cols))
    two = lambda v: np.concatenate([v, v])[:, None]
    c2 = [columns(a["norm1_g_2"]), columns(a["norm2_g_2"]), two(a["nsa_q_norm_2"])]
    c2 += [two(a["nsa_k_norm_2"][i]) for i in range(3)]
    c2 += [two(a["dil_q_norm_2"][i]) for i in range(3)] + [two(a["dil_k_norm_2"][i]) for i in range(3)]
    c2 = np.concatenate(c2, 1)
    d["cols2"] = np.ascontiguousarray(np.concatenate([c2, np.zeros((128, 32 - c2.shape[1]), f)], 1))
    d["w_mod"] = np.stack([slabs(a["w_mod"][l], 8, 256)[0] for l in range(2)])
    w = a["w_in"]
    ch = lambda s: list(range(s, s + 128))
    order = (ch(256) + list(range(320, 416)) + list(range(320, 352)) + ch(0) + ch(128)
             + ch(672) + ch(416) + ch(800) + ch(544)
             + ch(1440) + ch(1184) + ch(1568) + ch(1312) + ch(928) + ch(1056))
    d["w_in"] = np.stack([slabs(w[l][:, order], 8, 256)[0] for l in range(2)])
    d["w_o"] = np.stack([slabs(a["w_o"][l], 8, 256)[0] for l in range(2)])
    d["w1"] = np.stack([slabs(a["w_mlp_in"][l], 8, 256)[0] for l in range(2)])
    d["w2"] = np.stack([slabs(a["w_mlp_out"][l], 4, 512).reshape(16, 128, 2048) for l in range(2)])
    d["w_q_b"] = np.ascontiguousarray(a["w_q_b"].reshape(2, 2, 128, 768).transpose(0, 2, 1, 3))
    d["w_kv_b"] = a["w_kv_b"]
    w = a["w_in_2"]
    half = lambda s: list(range(s, s + 64))
    order = half(512) + half(640) + half(576) + half(704)
    for c in range(4):
        order += half(64 * c) + half(64 * (c + 4))
    order += ch(768) + ch(1024)
    order += ch(896) + ch(1152)
    D0 = 1304
    dil = lambda g, kind, hp: ch(D0 + 768 * g + 256 * kind + 128 * hp)
    heads = slabs(w[:, order], 8, 256)[0]
    d["win2"] = heads
    d["gate2"] = slabs(w[:, 1280:1304], 8, 24)[0, 0]
    for hp in range(2):
        o = []
        for g in range(3):
            o += dil(g, 0, hp) + dil(g, 1, hp)
        d[f"dqk{hp}"] = slabs(w[:, o], 8, 256)[0]
        d[f"dva{hp}"] = slabs(w[:, dil(0, 2, hp) + dil(1, 2, hp)], 8, 256)[0, 0]
        d[f"dvb{hp}"] = slabs(w[:, dil(2, 2, hp)], 8, 128)[0, 0]
    o = []
    for j in range(8):
        o += ch(3608 + 128 * j) + ch(4632 + 128 * j)
    d["wmg"] = slabs(w[:, o], 8, 256)[0]
    o = []
    for c in range(4):
        o += half(64 * c) + half(64 * (c + 4))
    d["up_nsa"] = slabs(a["w_up_nsa_2"][o], 4, 512)[0]
    d["up_dil"] = slabs(a["w_up_dil_2"], 2, 1024)[0, 0]
    d["w_o2"] = slabs(a["w_o_2"], 8, 256)[0]
    d["wq2"] = slabs(a["peer_wq_2"], 8, 256)[0]
    d["cmp_w1"] = np.concatenate([a["cmp_w1_k_2"].reshape(32, 64, 256).transpose(1, 0, 2),
                                  a["cmp_w1_v_2"].reshape(32, 64, 256).transpose(1, 0, 2)], 0)
    w2 = [a[n].reshape(2, 128, 64).transpose(1, 0, 2) for n in ("cmp_w2_k_2", "cmp_w2_v_2")]
    d["cmp_w2"] = np.ascontiguousarray(np.stack([np.concatenate([x, x], -1) for x in w2], 1))
    d["cmp_pe"] = np.ascontiguousarray(np.concatenate([a["cmp_pe_k_2"].T, a["cmp_pe_v_2"].T], 0))
    sk = np.zeros((128, 256), f)
    sk[0:64, 0:128], sk[64:128, 128:256] = a["peer_subkeys_2"][0].T, a["peer_subkeys_2"][1].T
    d["subk"] = sk
    d["u2"] = slabs(np.ascontiguousarray(a["peer_u_2"].T), 8, 256)[0]
    d["v2"] = slabs(a["peer_v_2"], 4, 512).reshape(64, 128, 2048)
    return {k: np.ascontiguousarray(v) for k, v in d.items()}


def program(nc, arrays):
    io = {n: nc.dram_tensor(f"in_{n}", v.shape, F32, kind="ExternalInput").ap() for n, v in arrays.items()}
    io["gdram"] = nc.dram_tensor("gdram", (16, 32, 128, 128), F32, kind="Internal").ap()
    io["out"] = nc.dram_tensor("out_0", (128, 8, 512), F32, kind="ExternalOutput").ap()
    build(nc, io)


def kernel(**inputs):
    import concourse.bacc as bacc
    from concourse.bass_utils import run_bass_kernel_spmd as run

    arrays = lay_out(inputs)
    nc = bacc.Bacc("TRN2", target_bir_lowering=False, num_devices=1)
    program(nc, arrays)
    r = run(nc, [{f"in_{n}": v for n, v in arrays.items()}], core_ids=[0])
    o = np.asarray(r.results[0]["out_0"])
    return np.ascontiguousarray(o.transpose(1, 0, 2).reshape(1024, 512).T).reshape(1, 512, 1024)
```

```python
from contextlib import ExitStack

import numpy as np
import concourse.bass as bass
from concourse import mybir

ALU = mybir.AluOpType
ACT = mybir.ActivationFunctionType
AX = mybir.AxisListType
F32 = mybir.dt.float32
FR = mybir.dt.float32r
U32 = mybir.dt.uint32

EPS = 1e-6
NEG = -1e30
LAT = (0, 512)
CTX = (512, 256)
SLAB = 2048
NPRE = 20


class Engine:

    def __init__(self, engine, sem):
        self.e, self.sem, self.n, self.seen = engine, sem, 0, {}

    def wait(self, *after):
        for t in after:
            if t is None:
                continue
            if isinstance(t, list):
                self.wait(*t)
                continue
            sem, value = t
            if self.seen.get(id(sem), 0) < value:
                self.seen[id(sem)] = value
                self.e.wait_ge(sem, value)

    def put(self, fn, *after, count=True):
        self.wait(*after)
        ins = fn(self.e)
        if not count:
            return None
        self.n += 1
        ins.then_inc(self.sem, 1)
        return (self.sem, self.n)

    def dma(self, out, in_, sem, value, *after):
        self.wait(*after)
        self.e.dma_start(out, in_).then_inc(sem, 16)
        return (sem, value)


class Ring:

    def __init__(self, bufs):
        self.bufs, self.free = bufs, [(i, []) for i in range(len(bufs))]

    def take(self):
        i, after = self.free.pop(0)
        return i, self.bufs[i], after

    def give(self, i, *after):
        self.free.append((i, list(after)))


def build(nc, io):
    out_d = io["out"]
    with ExitStack() as top:
        names = [0]

        def sb(stack, shape, dt=F32):
            names[0] += 1
            return stack.enter_context(nc.sbuf_tensor(f"sb{names[0]}", shape, dt))

        def sem():
            names[0] += 1
            return top.enter_context(nc.semaphore(f"sem{names[0]}"))

        PE, DVE, AC, PO, SP = (Engine(e, sem()) for e in (nc.tensor, nc.vector, nc.scalar, nc.gpsimd, nc.sync))
        dma_sems = {}

        def load(eng, out, in_, name, *after):
            s, n = dma_sems.get(name, (None, 0))
            s = s or sem()
            dma_sems[name] = (s, n + 16)
            return eng.dma(out, in_, s, n + 16, *after)

        X = sb(top, [128, 8, 768])
        Y = sb(top, [128, 8, 768])
        ps = [top.enter_context(nc.psum_tensor(f"ps{i}", [128, 1024], F32)) for i in range(4)]
        PS = Ring(ps)
        stage = [sb(top, [128, SLAB]) for _ in range(2)]
        WHb = [sb(top, [128, SLAB], FR) for _ in range(2)]
        WLb = [sb(top, [128, SLAB], FR) for _ in range(2)]
        T = Ring([sb(top, [128, 768]) for _ in range(3)])
        RS = Ring([sb(top, [128, 768]) for _ in range(2)])
        epsc = sb(top, [128, 1])
        ident = sb(top, [128, 128])
        ones = sb(top, [128, 128])
        cols = [sb(top, [128, 165]) for _ in range(2)]
        cols2 = sb(top, [128, 32])
        MODs = [sb(top, [128, 48, 2]) for _ in range(2)]
        mrow = [sb(top, [2, 256]) for _ in range(2)]
        csil = sb(top, [128, 8, 2])
        AB = sb(top, [128, 6, 8, 2])

        t_x = load(SP, X[:, :, 0:512], io["xT"], "x0")
        t_xc = load(SP, X[:, :, 512:768], io["ctxT"], "x1")
        t_id = load(PO, ident[:, :], io["ident"], "c0")
        t_ones = load(PO, ones[:, :], io["ones"], "c1")
        t_cols = [load(PO, cols[i][:, :], io["cols"][i], f"c{2 + i}") for i in range(2)]
        t_cols2 = load(PO, cols2[:, :], io["cols2"], "c4")
        t_eps = DVE.put(lambda e: e.memset(epsc[:, :], EPS))
        AC.wait(t_eps, t_cols)
        DVE.wait(t_cols, t_cols2, t_eps)
        PE.wait(t_id, t_ones)

        plan = []

        def weave(slabs, mods):
            return [x for w, m in zip(slabs, mods) for x in [("split", w)] + [("raw", v) for v in m]]

        mod_slabs = [[io["w_mod"][l, s] for s in range(24)] for l in range(2)]
        IN_MODS = [2] * 7
        OUT_MODS = [1, 1, 0, 0]
        plan += [("raw", v) for v in mod_slabs[0][0:8]]
        for l in range(2):
            rest = mod_slabs[0][8:] if l == 0 else []
            plan += weave([io["w_in"][l, s] for s in range(7)], [[rest.pop(0) for _ in range(2 * (l == 0))] for _ in range(7)])
            plan += weave([io["w_o"][l, s] for s in range(4)], [[rest.pop(0)] if rest else [] for _ in range(4)])
            ff = []
            for g in range(8):
                ff += [io["w1"][l, 2 * g + s] for s in range(2)] + [io["w2"][l, 2 * g + s] for s in range(2)]
            plan += weave(ff, [[mod_slabs[1][i]] if l == 0 and i < 24 else [] for i in range(32)])
        plan += [("split", io["win2"][s]) for s in range(5)]
        plan += [("split", io["gate2"])]
        for hp in range(2):
            plan += [("split", io[f"dqk{hp}"][s]) for s in range(3)]
            plan += [("split", io[f"dva{hp}"]), ("split", io[f"dvb{hp}"])]
        plan += [("split", io["up_nsa"][s]) for s in range(2)]
        plan += [("split", io["up_dil"])]
        plan += [("split", io["wmg"][s]) for s in range(8)]
        plan += [("split", io["w_o2"][s]) for s in range(4)]
        plan += [("split", io["wq2"][s]) for s in range(4)]
        for g in range(NPRE):
            plan += [("split", io["u2"][2 * g + s]) for s in range(2)]
        for g in range(32):
            if g >= NPRE:
                plan += [("split", io["u2"][2 * g + s]) for s in range(2)]
            plan += [("split", io["v2"][2 * g + s]) for s in range(2)]
        landed = {}
        stage_free = [None, None]
        w_ready = {}
        w_free = [None, None]
        nsplit = [0]
        sent = [0]
        split_no = {}

        def send(n):
            while sent[0] <= min(n, len(plan) - 1):
                m = sent[0]
                src = plan[m][1]
                landed[m] = load(SP, stage[m % 2][:, 0:src.shape[-1]], src, f"w{m % 2}", stage_free[m % 2])
                sent[0] += 1

        def split(n):
            if n >= len(plan) or plan[n][0] == "raw" or n in w_ready:
                return
            send(n)
            k = nsplit[0] % 2
            nsplit[0] += 1
            w = plan[n][1].shape[-1]
            st = stage[n % 2][:, 0:w]
            th = AC.put(lambda e: e.activation(WHb[k][:, 0:w], st, ACT.Copy), landed[n], w_free[k])
            tl = DVE.put(lambda e: e.tensor_tensor(WLb[k][:, 0:w], st, WHb[k][:, 0:w].bitcast(F32), ALU.subtract),
                         landed[n], th, w_free[k])
            stage_free[n % 2] = [tl]
            w_ready[n] = [th, tl]
            split_no[n] = k

        cur = [0]

        def take_raw():
            n = cur[0]
            cur[0] += 1
            send(n + 1)
            if plan[n + 1][0] == "split":
                split(n + 1)
            return n, stage[n % 2], landed[n]

        def give_raw(n, *after):
            stage_free[n % 2] = list(after)
            send(n + 2)

        def take_slab():
            n = cur[0]
            cur[0] += 1
            send(n)
            split(n)
            send(n + 2)
            if n + 1 < len(plan) and plan[n + 1][0] == "split":
                split(n + 1)
                send(n + 3)
            k = split_no[n]
            return k, WHb[k], WLb[k], w_ready[n]

        def give_slab(k, *after):
            w_free[k] = list(after)

        background = []

        def idle(n=1):
            for _ in range(n):
                if background:
                    background.pop(0)()

        def three(out, ah, al, bh, bl, first, last):
            PE.put(lambda e: e.matmul(out, ah, bh, start=first, stop=False), count=False)
            PE.put(lambda e: e.matmul(out, ah, bl, start=False, stop=False), count=False)
            return PE.put(lambda e: e.matmul(out, al, bh, start=False, stop=last), count=last)

        extra = []

        def linear(nslab, K, ncol, segs, HH, HL, ready, emit, mods=0):
            c = 0
            last = None
            for _ in range(nslab):
                k, wh, wl, wr = take_slab()
                wh = wh[:, 0:K * ncol].rearrange("p (k n) -> p k n", k=K)
                wl = wl[:, 0:K * ncol].rearrange("p (k n) -> p k n", k=K)
                nj = ncol // 128
                j = 0
                while j < nj:
                    pair = [j, j + 1] if (K == 4 and c == 0) else [j]
                    held = []
                    for jj in pair:
                        i, p, free = PS.take()
                        held.append((i, p, free, jj, c + jj - j))
                    parts = [range(K)] if len(pair) == 1 else [range(K - 1), range(K - 1, K)]
                    ends = {}
                    for part in parts:
                        for (i, p, free, jj, cc) in held:
                            sg = segs(cc) if callable(segs) else segs
                            PE.wait(free, wr)
                            cs = slice(128 * jj, 128 * jj + 128)
                            for kk in part:
                                PE.wait(ready[kk])
                                for (s0, sn) in sg:
                                    t = three(p[:, s0:s0 + sn], wh[:, kk, cs], wl[:, kk, cs],
                                              HH[:, kk, s0:s0 + sn], HL[:, kk, s0:s0 + sn], kk == 0, kk == K - 1)
                                    ends[cc] = t or ends.get(cc)
                    for (i, p, free, jj, cc) in held:
                        sg = segs(cc) if callable(segs) else segs
                        last = ends[cc]
                        PS.give(i, *emit(cc, p, last, sg))
                        idle()
                    j += len(pair)
                    c += len(pair)
                give_slab(k, last)
                for _ in range(mods):
                    if extra:
                        extra.pop(0)()
            return last

        def span(segs):
            return min(s for s, _ in segs), max(s + n for s, n in segs)

        class Stats:

            def __init__(self, n, segs, D, lhs=None):
                self.n, self.segs, self.D, self.lhs = n, segs, D, lhs if lhs is not None else ones[:, :]
                self.c, self.held, self.tile = 0, None, None

            def flush(self):
                if self.held is None:
                    return
                c, ti, t, tq = self.held
                i, p, free = self.tile
                PE.wait(free)
                for (s0, sn) in self.segs:
                    tm = PE.put(lambda e: e.matmul(p[:, s0:s0 + sn], self.lhs, t[:, s0:s0 + sn], start=(c == 0),
                                                   stop=(c == self.n - 1)), tq)
                T.give(ti, tm)
                self.held, self.tm = None, tm

            def add(self, s, *ready):
                a, b = span(self.segs)
                self.flush()
                if self.tile is None:
                    self.tile = PS.take()
                ti, t, tf = T.take()
                tq = AC.put(lambda e: e.activation(t[:, a:b], s[:, a:b], ACT.Square), tf, list(ready))
                self.held = (self.c, ti, t, tq)
                self.c += 1
                return self

            def finish(self):
                self.flush()
                a, b = span(self.segs)
                i, p, free = self.tile
                ri, r, rf = RS.take()
                t1 = AC.put(lambda e: e.activation(r[:, a:b], p[:, a:b], ACT.Ln, bias=epsc[:, 0:1], scale=1.0 / self.D),
                            self.tm, rf)
                t2 = AC.put(lambda e: e.activation(r[:, a:b], r[:, a:b], ACT.Exp, scale=-0.5), t1)
                PS.give(i, t1)
                return ri, r, t2

        def stats_of(src, segs, D, ready, lhs=None):
            st = Stats(len(src), segs, D, lhs)
            for s in src:
                st.add(s, ready)
            return st

        def norm_split(src, segs, stats, scale, shift, HH, HL, c0, hfree):
            ri, r, tr = stats.finish()
            done = []
            late = []

            def low():
                c, ti, t, ths = late.pop(0)
                for (s0, sn), th in zip(segs, ths):
                    z = slice(s0, s0 + sn)
                    b = shift(c, s0) if shift else 0.0
                    tl = DVE.put(lambda e: e.scalar_tensor_tensor(HL[:, c0 + c, z], t[:, z], b, HH[:, c0 + c, z].bitcast(F32),
                                                                  ALU.add, ALU.subtract), th, hfree)
                T.give(ti, th, tl)
                done.append([ths[-1], tl])

            for c, s in enumerate(src):
                ti, t, tf = T.take()
                ths = []
                tms = [DVE.put(lambda e: e.scalar_tensor_tensor(t[:, s0:s0 + sn], s[:, s0:s0 + sn], scale(c, s0),
                                                                r[:, s0:s0 + sn], ALU.mult, ALU.mult), tr, tf)
                       for (s0, sn) in segs]
                for (s0, sn), tm in zip(segs, tms):
                    z = slice(s0, s0 + sn)
                    if shift:
                        b = shift(c, s0)
                        th = AC.put(lambda e: e.activation(HH[:, c0 + c, z], t[:, z], ACT.Identity, bias=b), tm, hfree)
                    else:
                        th = AC.put(lambda e: e.activation(HH[:, c0 + c, z], t[:, z], ACT.Copy), tm, hfree)
                    ths.append(th)
                late.append((c, ti, t, ths))
                if c > 0:
                    low()
            low()
            RS.give(ri, tms[-1])
            return done

        def add_normed(segs, stats, scale, after):
            ri, r, tr = stats.finish()
            late = []

            def add():
                c, ti, t, tm = late.pop(0)
                a, b = span(segs)
                ta = DVE.put(lambda e: e.tensor_tensor(X[:, c, a:b], X[:, c, a:b], t[:, a:b], ALU.add), tm)
                T.give(ti, ta)
                after(c, ta)
                return ta

            for c in range(8):
                ti, t, tf = T.take()
                for (s0, sn) in segs:
                    z = slice(s0, s0 + sn)
                    tm = DVE.put(lambda e: e.scalar_tensor_tensor(t[:, z], Y[:, c, z], scale(c, s0), r[:, z],
                                                                  ALU.mult, ALU.mult), tr, tf)
                late.append((c, ti, t, tm))
                if c > 0:
                    add()
            ta = add()
            RS.give(ri, tm)
            return ta

        def mlp(groups, segs, HH, HL, AH, AL, ready, activate, yfree, ystats, mods=0):
            a, b = span(segs)
            last_y = [None] * 8
            afree = []
            for g in range(groups):
                done = []

                def up(c, p, tm, sg):
                    d = activate(g, c, p, tm, AH[:, c, :], AL[:, c, :], afree)
                    done.append(d[0])
                    return d[1]

                linear(2, 8, 256, segs, HH, HL, ready, up, mods)

                def down(c, p, tm, sg):
                    if g == 0:
                        t = AC.put(lambda e: e.activation(Y[:, c, a:b], p[:, a:b], ACT.Copy), tm, yfree)
                    else:
                        t = DVE.put(lambda e: e.tensor_tensor(Y[:, c, a:b], Y[:, c, a:b], p[:, a:b], ALU.add),
                                    tm, last_y[c])
                    last_y[c] = t
                    if g == groups - 1:
                        ystats.add(Y[:, c, :], t)
                    return [t]

                last = linear(2, 4, 512, segs, AH, AL, done, down, mods)
                afree = [last]
            return last_y

        first = ExitStack()
        cT = sb(first, [128, 8, 2])
        rotM = sb(first, [96, 96])
        cosM = sb(first, [96, 512])
        sinM = sb(first, [96, 512])
        t_c = load(PO, cT[:, :, :], io["cT"], "k0")
        t_tab = [load(PO, rotM[:, :], io["rotM"], "k1"), load(PO, cosM[:, :], io["cosM"], "k2"),
                 load(PO, sinM[:, :], io["sinM"], "k3")]
        t_sc = AC.put(lambda e: e.activation(csil[:, :, :], cT[:, :, :], ACT.Silu), t_c)
        x_ready = [t_x, t_xc]
        G_PRE, G_POST, G_PRE2, G_POST2, G_Q, G_KV, DW_B, LN_G, LN_B, G_BR, CW, SW, B_MOD = (
            0, 8, 16, 24, 32, 34, 35, 37, 39, 41, 49, 111, 117)
        t_m48 = [[None] * 24 for _ in range(2)]
        mod_late = []
        row_free = [None, None]

        def mod_close():
            l, s, i, p, te = mod_late.pop(0)
            for j in range(2):
                tm = PE.put(lambda e: e.matmul(p[:, 512 + 2 * j:514 + 2 * j], mrow[s % 2][:, 128 * j:128 * j + 128],
                                               ident[0:2, 0:2], start=True, stop=True), te, count=(j == 1))
            row_free[s % 2] = tm
            o = B_MOD + 2 * s
            t = DVE.put(lambda e: e.tensor_tensor(
                MODs[l][:, 2 * s:2 * s + 2, :], p[:, 512:516].rearrange("p (c v) -> p c v", v=2),
                cols[l][:, o:o + 2].rearrange("p (c v) -> p c v", v=1).broadcast_to([128, 2, 2]), ALU.add), tm)
            PS.give(i, t)
            t_m48[l][s] = t

        def mod_slab(l, s):
            i, p, free = PS.take()
            PE.wait(free, t_sc)
            n, w, tw = take_raw()
            w = w[:, :].rearrange("p (k n) -> p k n", k=8)
            for k in range(8):
                tm = PE.put(lambda e: e.matmul(p[0:2, 0:256], csil[:, k, :], w[:, k, :], start=(k == 0), stop=(k == 7)),
                            tw, count=(k == 7))
            give_raw(n, tm)
            te = AC.put(lambda e: e.activation(mrow[s % 2][:, :], p[0:2, 0:256], ACT.Copy), tm, row_free[s % 2])
            if mod_late:
                mod_close()
            mod_late.append((l, s, i, p, te))
            if s in (7, 23):
                mod_close()

        for s in range(8):
            mod_slab(0, s)
        extra.extend([lambda s=s: mod_slab(0, s) for s in range(8, 24)])

        def scales(l, dst, m, g, plus, after):
            for v in range(2):
                t = DVE.put(lambda e: e.scalar_tensor_tensor(AB[:, dst, :, v],
                                                             MODs[l][:, 8 * m:8 * m + 8, v], plus, cols[l][:, g:g + 8],
                                                             ALU.add, ALU.mult), t_m48[l][4 * m:4 * m + 4], after)
            return [t] + t_m48[l]

        for l in range(2):
            both = [LAT, CTX] if l == 0 else [LAT]
            col = cols[l]
            md = MODs[l][:, :, :].rearrange("p (m c) v -> p m c v", m=6)
            which = lambda s0: 0 if s0 < 512 else 1
            A_ = lambda d: (lambda c, s0: AB[:, d, c, which(s0):which(s0) + 1])
            B_ = lambda m: (lambda c, s0: md[:, m, c, which(s0):which(s0) + 1])
            t_pre = scales(l, 0, 1, G_PRE, 1.0, x_ready)

            z = ExitStack()
            ZQ = sb(z, [128, 2, 768])
            ZKV = sb(z, [128, 768])
            KR = sb(z, [96, 768])
            UW = 16 + 512 + 16 + 256 + 16
            U = sb(z, [128, 2, UW])
            CH = sb(z, [128, 2, UW])
            G2 = Ring([sb(z, [128, 768]) for _ in range(2)])
            HHs = ExitStack()
            HH, HL = sb(HHs, [128, 8, 768], FR), sb(HHs, [128, 8, 768], FR)
            h_free = [] if l == 0 else t_phase
            t_z0 = [DVE.put(lambda e: e.memset(U[:, :, :], 0.0), h_free),
                    DVE.put(lambda e: e.memset(CH[:, :, :], 0.0), h_free)]
            xs = [X[:, c, :] for c in range(8)]
            st = stats_of(xs, [LAT, CTX], 1024, x_ready) if l == 0 else x_stats
            DVE.wait(t_pre)
            AC.wait(t_pre)
            t_h = norm_split(xs, [LAT, CTX], st, A_(0), B_(0), HH, HL, 0, h_free)

            def padded(buf, c, s0, sn, shift=0):
                o = 16 + s0 if s0 == 0 else 16 + 512 + 16
                return buf[:, c, o + shift:o + shift + sn]

            z_done = []
            sigs = {}
            ORDER = ["kv", "kr", "q0", "q1", "g0", "a0", "g1", "a1", "h0", "c0", "h1", "c1", "b0", "b1"]

            def z_out(c, p, tm, sg):
                a, b = span(sg)
                kind = ORDER[c]
                if kind == "kv":
                    t = AC.put(lambda e: e.activation(ZKV[:, a:b], p[:, a:b], ACT.Copy), tm, h_free)
                elif kind == "kr":
                    t = AC.put(lambda e: e.activation(KR[:, a:b], p[0:96, a:b], ACT.Copy), tm, h_free)
                elif kind[0] == "q":
                    j = int(kind[1])
                    t = AC.put(lambda e: e.activation(ZQ[:, j, a:b], p[:, a:b], ACT.Copy), tm, h_free)
                elif kind[0] in "gh":
                    gi, g, gf = G2.take()
                    t = AC.put(lambda e: e.activation(g[:, a:b], p[:, a:b], ACT.Sigmoid if kind[0] == "g" else ACT.Copy),
                               tm, gf, h_free)
                    sigs[kind] = (gi, g, t)
                elif kind[0] in "ac":
                    j = int(kind[1])
                    gi, g, tg = sigs[("g" if kind[0] == "a" else "h") + kind[1]]
                    dst = U if kind[0] == "a" else CH
                    for (s0, sn) in sg:
                        t = DVE.put(lambda e: e.tensor_tensor(padded(dst, j, s0, sn), p[:, s0:s0 + sn],
                                                              g[:, s0:s0 + sn], ALU.mult), tm, tg, t_z0)
                    G2.give(gi, t)
                else:
                    j = int(kind[1])
                    t = AC.put(lambda e: e.activation(Y[:, 6 + j, a:b], p[:, a:b], ACT.Copy), tm, y_free)
                z_done.append(t)
                return [t]

            y_free = [] if l == 0 else t_phase
            in_segs = lambda c: [LAT, CTX] if ORDER[c] in ("kv", "kr") else both
            last = linear(7, 8, 256, in_segs, HH, HL, t_h, z_out, 2)
            t_zdone = z_done
            t_hh = [last] + t_h[-1]
            HHs.close()

            att = ExitStack()
            WQ = sb(att, [128, 2, 768])
            WKV = sb(att, [128, 1024])
            V = sb(att, [128, 6, 512])
            QR = Ring([sb(att, [96, 768]) for _ in range(2)])
            KRr = Ring([sb(att, [96, 768]) for _ in range(2)])
            Pb = Ring([sb(att, [128, 768]) for _ in range(3)])
            PTb = Ring([sb(att, [128, 768]) for _ in range(2)])
            sm = Ring([sb(att, [128, 4]) for _ in range(4)])
            ACC = sb(att, [128, UW])
            t_wq = load(PO, WQ[:, :, :], io["w_q_b"][l], "q0", t_hh)
            t_wkv = load(PO, WKV[:, :], io["w_kv_b"][l], "q1", t_hh)

            def conv(buf, j, taps, half, w0, bias, acc, after, free):
                n = UW - 32
                last = [None]

                def tap(k):
                    def go():
                        src = buf[:, j, 16 + k - half:16 + k - half + n]
                        w = col[:, w0 + taps * j + k:w0 + taps * j + k + 1]
                        if k == 0:
                            if bias is None:
                                last[0] = DVE.put(lambda e: e.tensor_scalar(acc[:, 0:n], src, w, None, ALU.mult),
                                                  after, free)
                            else:
                                last[0] = DVE.put(lambda e: e.tensor_scalar(acc[:, 0:n], src, w, bias, ALU.mult,
                                                                            ALU.add), after, free)
                        else:
                            last[0] = DVE.put(lambda e: e.scalar_tensor_tensor(acc[:, 0:n], src, w, acc[:, 0:n],
                                                                               ALU.mult, ALU.add), last[0])
                    return go
                return [tap(k) for k in range(taps)], last

            conv_tok = {}
            acc_free = [t_hh]

            def close_conf(j, last):
                def go():
                    for (s0, sn) in both:
                        o = s0 if s0 == 0 else 528
                        t = DVE.put(lambda e: e.tensor_copy(Y[:, 4 + j, s0:s0 + sn], ACC[:, o:o + sn]), last[0], y_free)
                    conv_tok[4 + j] = t
                    acc_free[0] = [t]
                return go

            def close_sc(j, last):
                def go():
                    for (s0, sn) in both:
                        o = s0 if s0 == 0 else 528
                        t = DVE.put(lambda e: e.tensor_tensor(Y[:, 6 + j, s0:s0 + sn], Y[:, 6 + j, s0:s0 + sn],
                                                              ACC[:, o:o + sn], ALU.mult), last[0], t_zdone)
                    conv_tok[6 + j] = t
                    acc_free[0] = [t]
                return go

            for j in range(2):
                fs, last_c = conv(U, j, 31, 15, CW, col[:, DW_B + j:DW_B + j + 1], ACC, t_zdone, acc_free)
                background.extend(fs + [close_conf(j, last_c)])
            for j in range(2):
                fs, last_c = conv(CH, j, 3, 1, SW, None, ACC, t_zdone, acc_free)
                background.extend(fs + [close_sc(j, last_c)])

            def norm_in_place(src, segs, D, g, ready):
                ri, r, tr = stats_of(src, segs, D, ready).finish()
                a, b = span(segs)
                for c, s in enumerate(src):
                    t = DVE.put(lambda e: e.scalar_tensor_tensor(s[:, a:b], s[:, a:b], col[:, g + c:g + c + 1],
                                                                 r[:, a:b], ALU.mult, ALU.mult), tr)
                RS.give(ri, t)
                return t

            t_kvn = norm_in_place([ZKV[:, :]], [LAT, CTX], 128, G_KV, t_zdone)
            t_qn = norm_in_place([ZQ[:, j, :] for j in range(2)], both, 256, G_Q, t_zdone)

            def rope(buf, ready):
                i, p, free = PS.take()
                tm = PE.put(lambda e: e.matmul(p[0:96, 0:512], rotM[:, :], buf[:, 0:512], start=True, stop=True),
                            free, ready, t_tab)
                ti, t, tf = T.take()
                ta = DVE.put(lambda e: e.tensor_tensor(t[0:96, 0:512], p[0:96, 0:512], sinM[:, :], ALU.mult), tm, tf,
                             t_tab)
                PS.give(i, ta)
                tb = DVE.put(lambda e: e.tensor_tensor(buf[:, 0:512], buf[:, 0:512], cosM[:, :], ALU.mult), ready, tm)
                tc = DVE.put(lambda e: e.tensor_tensor(buf[:, 0:512], buf[:, 0:512], t[0:96, 0:512], ALU.add), ta, tb)
                T.give(ti, tc)
                return tc

            t_kr = rope(KR, t_zdone)
            for i, buf in enumerate(KRr.bufs):
                t_kc = DVE.put(lambda e: e.tensor_copy(buf[64:96, :], KR[64:96, :]), t_kr, t_hh)
            t_v = []
            for tt in range(6):
                i, p, free = PS.take()
                tm = PE.put(lambda e: e.matmul(p[:, 0:512], ZKV[:, 128 * tt:128 * tt + 128],
                                               WKV[:, :].rearrange("p (h a d) -> p h a d", h=8, a=2)[:, :, 1, :],
                                               start=True, stop=True), free, t_kvn, t_wkv)
                tc = AC.put(lambda e: e.activation(V[:, tt, :], p[:, 0:512], ACT.Copy), tm, t_hh)
                PS.give(i, tc)
                t_v.append(tc)

            SM = 1.0 / float(np.sqrt(np.float64(96)))

            def head_in(h):
                ki, kb, kf = KRr.take()
                qi, qb, qf = QR.take()
                i, p, free = PS.take()
                PE.wait(free, t_kvn, t_wkv)
                for (s0, sn) in (LAT, CTX):
                    tm = PE.put(lambda e: e.matmul(p[:, s0:s0 + sn], WKV[:, 128 * h:128 * h + 128],
                                                   ZKV[:, s0:s0 + sn], start=True, stop=True))
                tk = AC.put(lambda e: e.activation(kb[0:64, :], p[0:64, 0:768], ACT.Copy), tm, kf, t_kc)
                PS.give(i, tk)
                a, b = span(both)
                i, p, free = PS.take()
                PE.wait(free, t_qn, t_wq)
                for (s0, sn) in both:
                    for k in range(2):
                        tm = PE.put(lambda e: e.matmul(p[0:96, s0:s0 + sn], WQ[:, k, 96 * h:96 * h + 96],
                                                       ZQ[:, k, s0:s0 + sn], start=(k == 0), stop=(k == 1)))
                tq = AC.put(lambda e: e.activation(qb[:, a:b], p[0:96, a:b], ACT.Copy, scale=SM), tm, qf, t_hh)
                PS.give(i, tq)
                tq2 = rope(qb, tq)
                return (ki, kb, [tk, t_kc]), (qi, qb, [tq, tq2])

            units = []
            for h in range(8):
                for qt in range(4):
                    units.append((h, 128 * qt, 0, 768))
                if l == 0:
                    for qt in range(2):
                        units.append((h, 512 + 128 * qt, 512, 256))
            per = len(units) // 8
            heads = {0: head_in(0)}
            O = {}
            a, b_ = span(both)

            def scores(h, q0, k0, kn):
                (ki, kb, tk), (qi, qb, tq) = heads[h]
                i, p, free = PS.take()
                PE.wait(free, tk, tq)
                for (s0, sn) in ([LAT, CTX] if kn == 768 else [(0, 256)]):
                    tm = PE.put(lambda e: e.matmul(p[:, s0:s0 + sn], qb[:, q0:q0 + 128], kb[:, k0 + s0:k0 + s0 + sn],
                                                   start=True, stop=True))
                pi, pb, pf = Pb.take()
                mi, m, mf = sm.take()
                t1 = DVE.put(lambda e: e.tensor_reduce(m[:, 0:1], p[:, 0:kn], AX.X, ALU.max, negate=True), tm, mf, t_hh)
                t2 = AC.put(lambda e: e.activation(pb[:, 0:kn], p[:, 0:kn], ACT.Exp, bias=m[:, 0:1],
                                                   accum_out=m[:, 1:2]), t1, pf, t_hh)
                PS.give(i, t2)
                idle(1)
                t3 = DVE.put(lambda e: e.reciprocal(m[:, 2:3], m[:, 1:2]), t2)
                t4 = DVE.put(lambda e: e.tensor_scalar(pb[:, 0:kn], pb[:, 0:kn], m[:, 2:3], None, ALU.mult), t3, t2)
                sm.give(mi, t4)
                return pi, pb, t4

            def turn(u, s):
                h, q0, k0, kn = u
                pi, pb, tp = s
                nb = kn // 128
                i, p, free = PS.take()
                PE.wait(free, tp)
                for b in range(nb):
                    tt = PE.put(lambda e: e.transpose(p[:, 128 * b:128 * b + 128], pb[:, 128 * b:128 * b + 128],
                                                      ident[:, :]), count=(b == nb - 1))
                Pb.give(pi, tt)
                ti, ptb, ptf = PTb.take()
                tc = AC.put(lambda e: e.activation(ptb[:, 0:kn], p[:, 0:kn], ACT.Copy), tt, ptf, t_hh)
                PS.give(i, tc)
                return ti, ptb, tc

            att_stats = Stats(4, both, 512)
            t_att = []

            def values(u, s):
                h, q0, k0, kn = u
                ti, ptb, tc = s
                if h not in O:
                    O[h] = PS.take()
                oi, o, of = O[h]
                PE.wait(of, tc, t_v)
                hp = 128 * (h // 2)
                nb = kn // 128
                for b in range(nb):
                    tv = PE.put(lambda e: e.matmul(o[:, q0:q0 + 128], V[:, k0 // 128 + b, hp:hp + 128],
                                                   ptb[:, 128 * b:128 * b + 128], start=(b == 0), stop=(b == nb - 1)),
                                count=(b == nb - 1))
                PTb.give(ti, tv)
                if q0 == b_ - 128:
                    r0 = 64 * (h % 2)
                    oi, o, _ = O.pop(h)
                    tc = AC.put(lambda e: e.activation(Y[r0:r0 + 64, h // 2, a:b_], o[r0:r0 + 64, a:b_], ACT.Copy),
                                tv, y_free)
                    PS.give(oi, tc)
                    t_att.append(tc)
                    (ki, _, _), (qi, _, _) = heads[h]
                    KRr.give(ki, tv)
                    QR.give(qi, tv)

            def conf_norm():
                i, p, free = PS.take()
                PE.wait(free, conv_tok[4], conv_tok[5])
                for (s0, sn) in both:
                    for j in range(2):
                        tm = PE.put(lambda e: e.matmul(p[:, s0:s0 + sn], ones[:, :], Y[:, 4 + j, s0:s0 + sn],
                                                       start=(j == 0), stop=(j == 1)))
                for j in range(2):
                    td = DVE.put(lambda e: e.scalar_tensor_tensor(Y[:, 4 + j, a:b_], p[:, a:b_], -1.0 / 256,
                                                                  Y[:, 4 + j, a:b_], ALU.mult, ALU.add), tm, conv_tok[4 + j])
                PS.give(i, td)
                conf["d"] = td
                conf["st"] = stats_of([Y[:, 4 + j, :] for j in range(2)], both, 256, td)

            def conf_norm2():
                ri, r, tr = conf["st"].finish()
                for j in range(2):
                    tn = DVE.put(lambda e: e.scalar_tensor_tensor(Y[:, 4 + j, a:b_], Y[:, 4 + j, a:b_],
                                                                  col[:, LN_G + j:LN_G + j + 1], r[:, a:b_],
                                                                  ALU.mult, ALU.mult), tr)
                    ts = AC.put(lambda e: e.activation(Y[:, 4 + j, a:b_], Y[:, 4 + j, a:b_], ACT.Silu,
                                                       bias=col[:, LN_B + j:LN_B + j + 1]), tn)
                RS.give(ri, tn)
                conf["st"] = stats_of([Y[:, 4 + j, :] for j in range(2)], both, 256, ts)

            def branch_scale(c0):
                def go():
                    ri, r, tr = conf["st"].finish()
                    for j in range(2):
                        g = G_BR + c0 + j
                        t = DVE.put(lambda e: e.scalar_tensor_tensor(Y[:, c0 + j, a:b_], Y[:, c0 + j, a:b_], col[:, g:g + 1],
                                                                     r[:, a:b_], ALU.mult, ALU.mult), tr)
                    RS.give(ri, t)
                    conf[c0] = t
                return go

            def sc_stats():
                conf["st"] = stats_of([Y[:, 6 + j, :] for j in range(2)], both, 256, [conv_tok[6], conv_tok[7]])

            conf = {}
            background.extend([conf_norm, conf_norm2, branch_scale(4), sc_stats, branch_scale(6)])
            scored, turned = [], []
            for n, u in enumerate(units + [None, None, None]):
                if u is not None:
                    scored.append((u, scores(*u)))
                if turned:
                    values(*turned.pop(0))
                if n % per == per - 3 and u is not None and u[0] + 1 < 8:
                    heads[u[0] + 1] = head_in(u[0] + 1)
                if len(scored) > 1 or (u is None and scored):
                    su = scored.pop(0)
                    turned.append((su[0], turn(*su)))
                idle(1 if l == 0 else 2)
            while turned:
                values(*turned.pop(0))
            idle(len(background))
            for c in range(4):
                att_stats.add(Y[:, c, :], t_att)

            att.close()
            z.close()
            HHs = ExitStack()
            HH, HL = sb(HHs, [128, 8, 768], FR), sb(HHs, [128, 8, 768], FR)
            t_free = [(PE.sem, PE.n), (DVE.sem, DVE.n), (AC.sem, AC.n)]
            t_m = [None] * 8
            for c in range(4, 8):
                for (s0, sn) in both:
                    zz = slice(s0, s0 + sn)
                    th = AC.put(lambda e: e.activation(HH[:, c, zz], Y[:, c, zz], ACT.Copy), conf[4], conf[6], t_free)
                    tl = DVE.put(lambda e: e.tensor_tensor(HL[:, c, zz], Y[:, c, zz], HH[:, c, zz].bitcast(F32), ALU.subtract),
                                 th, t_free)
                t_m[c] = [th, tl]
            t_m[0:4] = norm_split([Y[:, c, :] for c in range(4)], both, att_stats,
                                  lambda c, s0: col[:, G_BR + c:G_BR + c + 1], None, HH, HL, 0, t_free)
            ystats = Stats(8, both, 1024)

            def y_out(c, p, tm, sg):
                t = AC.put(lambda e: e.activation(Y[:, c, a:b_], p[:, a:b_], ACT.Copy), tm, t_m)
                ystats.add(Y[:, c, :], t)
                return [t]

            last = linear(4, 8, 256, both, HH, HL, t_m, y_out, 1)
            now = [(DVE.sem, DVE.n)]
            DVE.wait(scales(l, 1, 2, G_POST, 0.0, now), scales(l, 2, 4, G_PRE2, 1.0, now), scales(l, 3, 5, G_POST2, 0.0, now))
            AC.wait(t_m48[l])
            st = Stats(8, both, 1024)
            t_x1 = add_normed(both, ystats, A_(1), lambda c, ta: st.add(X[:, c, :], ta))
            t_h = norm_split(xs, both, st, A_(2), B_(3), HH, HL, 0, [last])
            mm = ExitStack()
            AH, AL = sb(mm, [128, 4, 768], FR), sb(mm, [128, 4, 768], FR)
            if l == 0:
                extra.extend([lambda s=s: mod_slab(1, s) for s in range(24)])

            def sqrelu(g, c, p, tm, ah, al, afree):
                ti, t, tf = T.take()
                t1 = AC.put(lambda e: e.activation(t[:, a:b_], p[:, a:b_], ACT.Relu), tm, tf)
                t2 = DVE.put(lambda e: e.tensor_tensor(t[:, a:b_], t[:, a:b_], t[:, a:b_], ALU.mult), t1)
                t3 = AC.put(lambda e: e.activation(ah[:, a:b_], t[:, a:b_], ACT.Copy), t2, afree)
                t4 = DVE.put(lambda e: e.tensor_tensor(al[:, a:b_], t[:, a:b_], ah[:, a:b_].bitcast(F32),
                                                       ALU.subtract), t3, afree)
                T.give(ti, t4)
                return t4, [t1]

            ystats = Stats(8, both, 1024)
            yl = mlp(8, both, HH, HL, AH, AL, t_h, sqrelu, [t_x1], ystats, 1)
            next_segs = [LAT, CTX] if l == 0 else [LAT]
            x_stats = Stats(8, next_segs, 1024)
            t_x2 = add_normed(both, ystats, A_(3), lambda c, ta: x_stats.add(X[:, c, :], ta))
            x_ready = [t_x2]
            mm.close()
            HHs.close()
            t_phase = [(PE.sem, PE.n), (DVE.sem, DVE.n), (AC.sem, AC.n)]
        first.close()

        L = [LAT]
        C_N1, C_N2, C_QN, C_KN, C_DQ, C_DK = 0, 8, 16, 17, 20, 23
        second = ExitStack()
        xs = [X[:, c, :] for c in range(8)]
        HHs = ExitStack()
        cosN = sb(second, [128, 512])
        sinN = sb(second, [128, 512])
        rotN = sb(second, [128, 128])
        bones = sb(second, [128, 128])
        t_t2 = [load(PO, cosN[:, :], io["cosN"], "k0", t_phase), load(PO, sinN[:, :], io["sinN"], "k1", t_phase),
                load(PO, rotN[:, :], io["rotN"], "k2", t_phase), load(PO, bones[:, :], io["bones"], "k3", t_phase)]
        HH, HL = sb(HHs, [128, 8, 512], FR), sb(HHs, [128, 8, 512], FR)
        c2 = lambda b0: (lambda c, s0: cols2[:, b0 + c:b0 + c + 1])
        t_h = norm_split(xs, L, x_stats, c2(C_N1), None, HH, HL, 0, t_phase)
        t_c8 = DVE.put(lambda e: e.tensor_scalar(cols2[:, C_QN:C_QN + 1], cols2[:, C_QN:C_QN + 1], 0.125, None, ALU.mult))
        t_c8 = DVE.put(lambda e: e.tensor_scalar(cols2[:, C_DQ:C_DQ + 3], cols2[:, C_DQ:C_DQ + 3], 0.125, None, ALU.mult))

        def head_norm_rope(zsrc, ready, g, n, dsts, cos, sin, free):
            ri, r, tr = stats_of([zsrc], [(0, n)], 64, ready + t_t2, bones[:, :]).finish()
            ti, t, tf = T.take()
            t1 = DVE.put(lambda e: e.scalar_tensor_tensor(t[:, 0:n], zsrc[:, 0:n], cols2[:, g:g + 1], r[:, 0:n],
                                                          ALU.mult, ALU.mult), tr, tf, t_c8)
            i, p, pf = PS.take()
            tm = PE.put(lambda e: e.matmul(p[:, 0:n], rotN[:, :], t[:, 0:n], start=True, stop=True), pf, t1, t_t2)
            t2 = DVE.put(lambda e: e.tensor_tensor(r[:, 0:n], p[:, 0:n], sin, ALU.mult), tm, t1)
            PS.give(i, t2)
            t3 = DVE.put(lambda e: e.tensor_tensor(t[:, 0:n], t[:, 0:n], cos, ALU.mult), tm, t1)
            for (r0, r1, ap) in dsts:
                t4 = DVE.put(lambda e: e.tensor_tensor(ap, t[r0:r1, 0:n], r[r0:r1, 0:n], ALU.add), t2, t3, free)
            T.give(ti, t4)
            RS.give(ri, t4)
            return t1, t4

        nsa = ExitStack()
        QN = sb(nsa, [128, 4, 512])
        KS = sb(nsa, [128, 2, 512])
        KW = sb(nsa, [128, 2, 512])
        VSW = sb(nsa, [128, 4, 256])
        KCM = sb(nsa, [128, 2, 32])
        VCM = sb(nsa, [128, 128])
        GT = sb(nsa, [128, 4, 24])
        cmpS = ExitStack()
        KVC = Y[:, :, :].rearrange("p c t -> p (c t)")[:, 2048:3072].rearrange("p (g t) -> p g t", g=2)
        BLK = Y[:, :, :].rearrange("p c t -> p (c t)")[:, 0:2048].rearrange("p (t c) -> p t c", c=64)
        W1 = sb(cmpS, [128, 32, 256])
        W2 = Y[:, :, :].rearrange("p c t -> p (c t)")[:, 3072:3584].rearrange("p (a b c) -> p a b c", a=2, b=2)
        PEt = sb(cmpS, [128, 32])
        HID = Y[:, :, :].rearrange("p c t -> p (c t)")[:, 3584:3840].rearrange("p (a b c) -> p a b c", a=2, b=2)
        cosC = sb(cmpS, [128, 32])
        sinC = sb(cmpS, [128, 32])
        t_cw = [load(PO, W1[:, :, :], io["cmp_w1"], "q0", t_phase), load(PO, W2[:, :, :, :], io["cmp_w2"], "q1", t_phase),
                load(PO, PEt[:, :], io["cmp_pe"], "q2", t_phase), load(PO, cosC[:, :], io["cosC"], "q3", t_phase),
                load(PO, sinC[:, :], io["sinC"], "q4", t_phase)]
        t_ms = [DVE.put(lambda e: e.memset(KS[:, :, :], 0.0), t_phase), DVE.put(lambda e: e.memset(KW[:, :, :], 0.0), t_phase),
                DVE.put(lambda e: e.memset(KCM[:, :, :], 0.0), t_phase), DVE.put(lambda e: e.memset(VCM[:, :], 0.0), t_phase)]
        ORD2 = ["kvc0", "kvc1", "q0", "q1", "q2", "q3", "ks", "kw"]
        zt = {}

        def z2(c, p, tm, sg):
            kind = ORD2[c]
            if kind[0:3] == "kvc":
                j = int(kind[3])
                zt[kind] = AC.put(lambda e: e.activation(KVC[:, j, :], p[:, 0:512], ACT.Copy), tm, t_phase)
                return [zt[kind]]
            if kind[0] == "q":
                j = int(kind[1])
                t1, zt[kind] = head_norm_rope(p, [tm], C_QN, 512, [(0, 128, QN[:, j, :])], cosN[:, :], sinN[:, :], t_phase)
                return [t1]
            dst = KS if kind == "ks" else KW
            t1, zt[kind] = head_norm_rope(p, [tm], C_KN + (1 if kind == "ks" else 2), 512,
                                          [(0, 64, dst[0:64, 0, :]), (64, 128, dst[64:128, 1, :])], cosN[:, :], sinN[:, :],
                                          t_ms)
            return [t1]

        linear(4, 8, 256, L, HH, HL, t_h, z2)

        def token_major(k, wh, wl, wr, ncol, tiles, emit):
            wh = wh[:, 0:8 * ncol].rearrange("p (k n) -> p k n", k=8)
            wl = wl[:, 0:8 * ncol].rearrange("p (k n) -> p k n", k=8)
            for tt, tok in enumerate(tiles):
                i, p, free = PS.take()
                PE.wait(free, wr, t_h)
                for kk in range(8):
                    last = three(p[:, 0:ncol], HH[:, kk, tok], HL[:, kk, tok], wh[:, kk, :], wl[:, kk, :],
                                 kk == 0, kk == 7)
                PS.give(i, *emit(tt, p, last))
            give_slab(k, last)

        nat = [slice(128 * i, 128 * i + 128) for i in range(4)]
        k, wh, wl, wr = take_slab()
        zv = []

        def v_out(tt, p, tm):
            zv.append(AC.put(lambda e: e.activation(VSW[:, tt, :], p[:, 0:256], ACT.Copy), tm, t_phase))
            return [zv[-1]]

        token_major(k, wh, wl, wr, 256, nat, v_out)
        kv4 = KVC[:, :, :]
        for g in range(2):
            src = KVC[:, g, 0:496].rearrange("p (c t) -> p c t", t=16)
            for hf in range(2):
                s = KVC[:, g, 16 * hf:16 * hf + 496].rearrange("p (c t) -> p t c", t=16)
                pe = PEt[:, 16 * hf:16 * hf + 16].rearrange("p (t c) -> p t c", c=1).broadcast_to([128, 16, 31])
                t_blk = DVE.put(lambda e: e.tensor_tensor(BLK[:, 16 * hf:16 * hf + 16, 31 * g:31 * g + 31], s, pe, ALU.add),
                                zt[f"kvc{g}"], t_cw, t_phase)
        for kv in range(2):
            rows = slice(64 * kv, 64 * kv + 64)
            i, p, free = PS.take()
            PE.wait(free, t_blk, t_cw)
            for hc in range(2):
                for tp in range(32):
                    tm = PE.put(lambda e: e.matmul(p[:, 64 * hc:64 * hc + 62], W1[rows, tp, 128 * hc:128 * hc + 128],
                                                   BLK[rows, tp, 0:62], start=(tp == 0), stop=(tp == 31)),
                                count=(tp == 31))
            t_hid = AC.put(lambda e: e.activation(HID[:, kv, :, 0:62], p[:, 0:128].rearrange("p (a b) -> p a b", a=2)[:, :, 0:62],
                                                  ACT.Gelu_apprx_tanh), tm, t_phase)
            PS.give(i, t_hid)
            i, p, free = PS.take()
            PE.wait(free, t_hid, t_cw)
            if kv == 0:
                for hc in range(2):
                    tm = PE.put(lambda e: e.matmul(p[:, 0:62], W2[:, 0, hc, :], HID[:, 0, hc, 0:62], start=(hc == 0),
                                                   stop=(hc == 1)))
                kz = sb(cmpS, [128, 32])
                ta = AC.put(lambda e: e.activation(kz[0:64, 0:31], p[0:64, 0:31], ACT.Copy), tm, t_phase)
                tb = AC.put(lambda e: e.activation(kz[64:128, 0:31], p[64:128, 31:62], ACT.Copy), tm, t_phase)
                PS.give(i, tb)
                _, t_kcm = head_norm_rope(kz, [ta, tb], C_KN, 31, [(0, 64, KCM[0:64, 0, 0:31]), (64, 128, KCM[64:128, 1, 0:31])],
                                          cosC[:, 0:31], sinC[:, 0:31], t_ms)
            else:
                for g in range(2):
                    for hc in range(2):
                        tm = PE.put(lambda e: e.matmul(p[0:31, 64 * g:64 * g + 64], HID[:, 1, hc, 31 * g:31 * g + 31],
                                                       W2[:, 1, hc, 0:64], start=(hc == 0), stop=(hc == 1)))
                t_vcm = AC.put(lambda e: e.activation(VCM[0:31, :], p[0:31, 0:128], ACT.Copy), tm, t_ms)
                PS.give(i, t_vcm)
        cmpS.close()
        k, wh, wl, wr = take_slab()

        def g_out(tt, p, tm):
            zv.append(AC.put(lambda e: e.activation(GT[:, tt, :], p[:, 0:24], ACT.Sigmoid), tm, t_phase))
            return [zv[-1]]

        token_major(k, wh, wl, wr, 24, nat, g_out)
        attS = ExitStack()
        t_free = [(PE.sem, PE.n), (DVE.sem, DVE.n), (AC.sem, AC.n)]
        CM = sb(attS, [128, 2, 4, 32])
        SL = sb(attS, [128, 896])
        PC = Ring([sb(attS, [128, 8, 128])])
        PTC = Ring([sb(attS, [128, 8, 128])])
        Pb = Ring([sb(attS, [128, 1024]) for _ in range(2)])
        PTb = Ring([sb(attS, [128, 1024]) for _ in range(2)])
        sm = Ring([sb(attS, [128, 8]) for _ in range(4)])
        cs = Ring([sb(attS, [128, 4, 8]) for _ in range(2)])
        t_mk = [load(PO, CM[:, :, :, :], io["cmask"], "q0", t_free), load(PO, SL[:, :], io["slide"], "q1", t_free)]
        t_pc0 = DVE.put(lambda e: e.memset(PC.bufs[0][:, :, :], 0.0), t_free)
        t_yn = []
        bc3 = lambda ap, sh: ap.broadcast_to(sh)
        for qt in range(4):
            qs = slice(128 * qt, 128 * qt + 128)
            Lk = 128 * (qt + 1)
            i, p, free = PS.take()
            PE.wait(free, zt["q3"], t_kcm, zt["kw"])
            for h in range(8):
                tm = PE.put(lambda e: e.matmul(p[:, 32 * h:32 * h + 32], QN[:, h % 4, qs], KCM[:, h // 4, :],
                                               start=True, stop=True), count=(h == 7))
            pi, pc, pcf = PC.take()
            ci, cst, cf = cs.take()
            pcv = pc[:, :, 0:31]
            pv3 = p[:, 0:256].rearrange("p (h c) -> p h c", h=8)[:, :, 0:31]
            msk = CM[:, 0, qt, 0:31].rearrange("p (o c) -> p o c", o=1).broadcast_to([128, 8, 31])
            val = CM[:, 1, qt, 0:31].rearrange("p (o c) -> p o c", o=1).broadcast_to([128, 8, 31])
            vec = lambda j: cst[:, j, :].rearrange("p (h o) -> p h o", o=1)
            b8 = lambda j: vec(j).broadcast_to([128, 8, 31])
            t1 = DVE.put(lambda e: e.tensor_tensor(pcv, pv3, msk, ALU.add), tm, pcf, t_mk, t_pc0)
            PS.give(i, t1)
            t2 = DVE.put(lambda e: e.tensor_reduce(cst[:, 0, :], pcv, AX.X, ALU.max), t1, cf, t_free)
            t3 = DVE.put(lambda e: e.tensor_tensor(pcv, pcv, b8(0), ALU.subtract), t2)
            t4 = AC.put(lambda e: e.activation(pcv, pcv, ACT.Exp), t3)
            t5 = DVE.put(lambda e: e.tensor_reduce(cst[:, 1, :], pcv, AX.X, ALU.add), t4)
            t6 = DVE.put(lambda e: e.reciprocal(cst[:, 2, :], cst[:, 1, :]), t5)
            gates = GT[:, qt, :].rearrange("p (h b) -> p h b", b=3)
            t7 = DVE.put(lambda e: e.tensor_tensor(cst[:, 3, :], cst[:, 2, :], gates[:, :, 0], ALU.mult), t6, zv)
            t8 = DVE.put(lambda e: e.tensor_tensor(pcv, pcv, b8(3), ALU.mult), t7)
            t9 = DVE.put(lambda e: e.tensor_tensor(pcv, pcv, val, ALU.mult), t8)
            cs.give(ci, t9)
            i, p, free = PS.take()
            PE.wait(free, t9)
            for h in range(8):
                tm = PE.put(lambda e: e.transpose(p[:, 128 * h:128 * h + 128], pc[:, h, :], ident[:, :]), count=(h == 7))
            PC.give(pi, tm)
            ti, ptc, tf = PTC.take()
            t_ptc = AC.put(lambda e: e.activation(ptc[:, :, :], p[:, :].rearrange("p (h q) -> p h q", h=8), ACT.Copy), tm, tf,
                           t_free)
            PS.give(i, t_ptc)
            pend = None
            O = {}

            def nsa_scores(h):
                g, c = h // 4, h % 4
                i, p, free = PS.take()
                PE.wait(free, zt["q3"], zt["ks"], zt["kw"])
                for j, kk in enumerate((KS, KW)):
                    tm = PE.put(lambda e: e.matmul(p[:, 512 * j:512 * j + Lk], QN[:, c, qs], kk[:, g, 0:Lk],
                                                   start=True, stop=True))
                pi, pb, pf = Pb.take()
                mi, m, mf = sm.take()
                off = 384 - 128 * qt
                te = []
                for j in range(2):
                    pp = pb[:, Lk * j:Lk * j + Lk]
                    t1 = DVE.put(lambda e: e.tensor_tensor_reduce(pp, p[:, 512 * j:512 * j + Lk], SL[:, off:off + Lk], 1.0,
                                                                  -3e38, ALU.add, ALU.max, m[:, j:j + 1]),
                                 tm, pf, mf, t_mk, t_free)
                t1 = DVE.put(lambda e: e.tensor_scalar(m[:, 2:4], m[:, 0:2], -1.0, None, ALU.mult), t1)
                PS.give(i, t1)
                for j in range(2):
                    pp = pb[:, Lk * j:Lk * j + Lk]
                    t2 = AC.put(lambda e: e.activation(pp, pp, ACT.Exp, bias=m[:, 2 + j:3 + j], accum_out=m[:, 4 + j:5 + j]),
                                t1)
                t3 = DVE.put(lambda e: e.reciprocal(m[:, 6:8], m[:, 4:6]), t2)
                t4 = DVE.put(lambda e: e.tensor_tensor(m[:, 6:8], m[:, 6:8], GT[:, qt, 3 * h + 1:3 * h + 3], ALU.mult), t3, zv)
                for j in range(2):
                    pp = pb[:, Lk * j:Lk * j + Lk]
                    t5 = DVE.put(lambda e: e.tensor_scalar(pp, pp, m[:, 6 + j:7 + j], None, ALU.mult), t4)
                sm.give(mi, t5)
                return h, pi, pb, t5

            def nsa_values(h, pi, pb, tp):
                g, c = h // 4, h % 4
                nb = qt + 1
                i, p, free = PS.take()
                PE.wait(free, tp)
                for b in range(2 * nb):
                    tt = PE.put(lambda e: e.transpose(p[:, 128 * b:128 * b + 128], pb[:, 128 * b:128 * b + 128], ident[:, :]),
                                count=(b == 2 * nb - 1))
                Pb.give(pi, tt)
                ti2, ptb, ptf = PTb.take()
                tc = AC.put(lambda e: e.activation(ptb[:, 0:256 * nb], p[:, 0:256 * nb], ACT.Copy), tt, ptf, t_free)
                PS.give(i, tc)
                oi, o, of = PS.take()
                PE.wait(of, t_ptc, t_vcm, zv)
                oo = o[:, 0:128]
                PE.put(lambda e: e.matmul(oo, VCM[:, :], ptc[:, h, :], start=True, stop=False), count=False)
                PE.wait(tc)
                for j in range(2):
                    for b in range(nb):
                        end = j == 1 and b == nb - 1
                        tv = PE.put(lambda e: e.matmul(oo, VSW[:, b, 128 * j:128 * j + 128],
                                                       ptb[:, 128 * (nb * j + b):128 * (nb * j + b) + 128],
                                                       start=False, stop=end), count=end)
                PTb.give(ti2, tv)
                r0 = 64 * g
                ty = AC.put(lambda e: e.activation(Y[r0:r0 + 64, c, qs], o[r0:r0 + 64, 0:128], ACT.Copy), tv, t_phase)
                PS.give(oi, ty)
                t_yn.append(ty)
                return tv

            for h in range(8):
                s = nsa_scores(h)
                if pend:
                    nsa_values(*pend)
                pend = s
            tv = nsa_values(*pend)
            PTC.give(ti, tv)
        attS.close()
        nsa.close()

        dil = ExitStack()
        t_free = [(PE.sem, PE.n), (DVE.sem, DVE.n), (AC.sem, AC.n)]
        QD = sb(dil, [128, 3, 512])
        KD = sb(dil, [128, 3, 2, 512])
        VD = sb(dil, [128, 3, 4, 128])
        MK = sb(dil, [128, 4, 768])
        Pb = Ring([sb(dil, [128, 768]) for _ in range(2)])
        PTb = Ring([sb(dil, [128, 768]) for _ in range(2)])
        sm = Ring([sb(dil, [128, 4]) for _ in range(4)])
        t_mk = load(PO, MK[:, :, :], io["dmask"], "q0", t_free)
        t_ms = DVE.put(lambda e: e.memset(KD[:, :, :, :], 0.0), t_free)
        strided = [slice(a, 512, 4) for a in range(4)]
        d_free = t_free
        t_yd = []
        for hp in range(2):
            dq, dk, dv = {}, {}, []

            def d_out(c, p, tm, sg):
                g = c // 2
                if c % 2 == 0:
                    t1, dq[g] = head_norm_rope(p, [tm], C_DQ + g, 512, [(0, 128, QD[:, g, :])], cosN[:, :], sinN[:, :], d_free)
                else:
                    t1, dk[g] = head_norm_rope(p, [tm], C_DK + g, 512, [(0, 64, KD[0:64, g, 0, :]), (64, 128, KD[64:128, g, 1, :])],
                                               cosN[:, :], sinN[:, :], [t_ms] + d_free)
                return [t1]

            linear(3, 8, 256, L, HH, HL, t_h, d_out)
            for g, tiles in ((0, nat), (1, strided), (2, strided)):
                if g < 2:
                    if g == 0:
                        k, wh, wl, wr = take_slab()
                    w0 = 128 * g
                else:
                    give_slab(k, tl)
                    k, wh, wl, wr = take_slab()
                    w0 = 0
                nc_ = 256 if g < 2 else 128
                whv = wh[:, 0:8 * nc_].rearrange("p (k n) -> p k n", k=8)
                wlv = wl[:, 0:8 * nc_].rearrange("p (k n) -> p k n", k=8)
                for tt, tok in enumerate(tiles):
                    i, p, free = PS.take()
                    PE.wait(free, wr, t_h)
                    for kk in range(8):
                        tl = three(p[:, 0:128], HH[:, kk, tok], HL[:, kk, tok], whv[:, kk, w0:w0 + 128],
                                   wlv[:, kk, w0:w0 + 128], kk == 0, kk == 7)
                    tc = AC.put(lambda e: e.activation(VD[:, g, tt, :], p[:, 0:128], ACT.Copy), tl, d_free)
                    PS.give(i, tc)
                    dv.append(tc)
            give_slab(k, tl)

            def d_scores(a, j):
                i, p, free = PS.take()
                PE.wait(free, [dq[g] for g in range(3)], [dk[g] for g in range(3)])
                for g in range(3):
                    o = p[:, 0:512] if g == 0 else p[:, 384 + 128 * g:512 + 128 * g]
                    kk = KD[:, g, j, :] if g == 0 else KD[:, g, j, strided[a]]
                    tm = PE.put(lambda e: e.matmul(o, QD[:, g, strided[a]], kk, start=True, stop=True), count=(g == 2))
                pi, pb, pf = Pb.take()
                mi, m, mf = sm.take()
                t1 = DVE.put(lambda e: e.tensor_tensor_reduce(pb[:, :], p[:, 0:768], MK[:, a, :], 1.0, -3e38, ALU.add,
                                                              ALU.max, m[:, 0:1]), tm, pf, mf, t_mk, t_free)
                PS.give(i, t1)
                t2 = DVE.put(lambda e: e.tensor_scalar(m[:, 3:4], m[:, 0:1], -1.0, None, ALU.mult), t1)
                t3 = AC.put(lambda e: e.activation(pb[:, :], pb[:, :], ACT.Exp, bias=m[:, 3:4], accum_out=m[:, 1:2]), t2, t1)
                t4 = DVE.put(lambda e: e.reciprocal(m[:, 2:3], m[:, 1:2]), t3)
                t5 = DVE.put(lambda e: e.tensor_scalar(pb[:, :], pb[:, :], m[:, 2:3], None, ALU.mult), t4)
                sm.give(mi, t5)
                return a, j, pi, pb, t5

            def d_values(a, j, pi, pb, tp):
                i, p, free = PS.take()
                PE.wait(free, tp)
                for b in range(6):
                    tt = PE.put(lambda e: e.transpose(p[:, 128 * b:128 * b + 128], pb[:, 128 * b:128 * b + 128], ident[:, :]),
                                count=(b == 5))
                Pb.give(pi, tt)
                ti, ptb, ptf = PTb.take()
                tc = AC.put(lambda e: e.activation(ptb[:, :], p[:, 0:768], ACT.Copy), tt, ptf, t_free)
                PS.give(i, tc)
                oi, o, of = PS.take()
                PE.wait(of, tc, dv)
                for b in range(6):
                    vv = VD[:, 0, b, :] if b < 4 else VD[:, b - 3, a, :]
                    tv = PE.put(lambda e: e.matmul(o[:, 0:128], vv, ptb[:, 128 * b:128 * b + 128], start=(b == 0), stop=(b == 5)),
                                count=(b == 5))
                PTb.give(ti, tv)
                r0 = 64 * j
                ty = AC.put(lambda e: e.activation(Y[r0:r0 + 64, 4 + hp, strided[a]], o[r0:r0 + 64, 0:128], ACT.Copy), tv, t_phase)
                PS.give(oi, ty)
                t_yd.append(ty)
                return tv

            pend = None
            for a in range(4):
                for j in range(2):
                    s = d_scores(a, j)
                    if pend:
                        d_values(*pend)
                    pend = s
            tv = d_values(*pend)
            d_free = [tv]
        dil.close()

        t_free = [(PE.sem, PE.n), (DVE.sem, DVE.n), (AC.sem, AC.n)]
        mg = ExitStack()
        YH, YL = sb(mg, [128, 6, 512], FR), sb(mg, [128, 6, 512], FR)
        UPm = sb(mg, [128, 13, 512])
        up_rest = Y[:, 6:8, :].rearrange("p c t -> p (c t)").rearrange("p (c t) -> p c t", c=3)
        UP = lambda c: UPm[:, c, :] if c < 13 else up_rest[:, c - 13, :]
        t_y = []
        for c in range(6):
            th = AC.put(lambda e: e.activation(YH[:, c, :], Y[:, c, 0:512], ACT.Copy), t_yn, t_yd, t_free)
            tl = DVE.put(lambda e: e.tensor_tensor(YL[:, c, :], Y[:, c, 0:512], YH[:, c, :].bitcast(F32), ALU.subtract), th, t_free)
            t_y.append([th, tl])
        ups = []

        def up_out(base):
            def f(c, p, tm, sg):
                t = AC.put(lambda e: e.activation(UP(base + c), p[:, 0:512], ACT.Copy), tm, t_free)
                ups.append(t)
                return [t]
            return f

        linear(2, 4, 512, L, YH, YL, t_y, up_out(0))
        linear(1, 2, 1024, L, YH[:, 4:6, :], YL[:, 4:6, :], t_y[4:6], up_out(8))
        mt = {}
        t_mg = []

        def mg_out(c, p, tm, sg):
            j, b = c // 2, c % 2
            ti, t, tf = T.take()
            t1 = AC.put(lambda e: e.activation(t[:, 0:512], p[:, 0:512], ACT.Sigmoid), tm, tf)
            u = UP(8 * b + j)
            t2 = DVE.put(lambda e: e.tensor_tensor(u, u, t[:, 0:512], ALU.mult), t1, ups)
            T.give(ti, t2)
            if b == 1:
                t3 = DVE.put(lambda e: e.tensor_tensor(UP(j), UP(j), UP(8 + j), ALU.add), t2)
                t_mg.append(t3)
            return [t1]

        last = linear(8, 8, 256, L, HH, HL, t_h, mg_out)
        t_m = []
        for c in range(8):
            th = AC.put(lambda e: e.activation(HH[:, c, :], UP(c), ACT.Copy), t_mg, last)
            tl = DVE.put(lambda e: e.tensor_tensor(HL[:, c, :], UP(c), HH[:, c, :].bitcast(F32), ALU.subtract), th)
            t_m.append([th, tl])
        t_xx = []
        st = Stats(8, L, 1024)

        def x_out(c, p, tm, sg):
            t = DVE.put(lambda e: e.tensor_tensor(X[:, c, 0:512], X[:, c, 0:512], p[:, 0:512], ALU.add), tm)
            t_xx.append(t)
            st.add(X[:, c, :], t)
            return [t]

        last = linear(4, 8, 256, L, HH, HL, t_m, x_out)
        mg.close()

        t_h = norm_split(xs, L, st, c2(C_N2), None, HH, HL, 0, [last])
        t_free = [(PE.sem, PE.n), (DVE.sem, DVE.n), (AC.sem, AC.n)]
        pr = ExitStack()
        E1, E2, GG = (b[:, 0:512] for b in T.bufs)
        IO = sb(pr, [128, 128])
        QP = sb(pr, [128, 8, 512])
        SK = sb(pr, [128, 256])
        GA = Ring([sb(pr, [128, 4, 512])])
        GST = Ring([sb(pr, [128, 128, 32]) for _ in range(1)])
        M1 = RS.bufs[1][:, 0:256].rearrange("p (a b) -> p a b", a=16)
        I1 = sb(pr, [128, 16, 16], U32)
        F1 = RS.bufs[1][:, 256:512].rearrange("p (a b) -> p a b", a=16)
        M2 = RS.bufs[1][:, 512:640].rearrange("p (a b) -> p a b", a=8)
        I2 = sb(pr, [128, 8, 16], U32)
        AB2 = sb(pr, [128, 2, 128], U32)
        AF = sb(pr, [128, 2, 128])
        EE = RS.bufs[0][:, 0:384].rearrange("p (a b) -> p a b", a=3)
        sg_ = sb(pr, [128, 2, 8])
        SX = X[:, :, 512:768].rearrange("p c (j n) -> p c j n", j=2)
        yf = Y[:, :, :].rearrange("p c t -> p (c t)")
        S2 = yf[:, 0:2048]
        CAND = yf[:, 2048:4096].rearrange("p (h a b) -> p h a b", h=8, a=16)
        OH = Ring([sb(pr, [128, 2, 8, 128]), yf[:, 4096:6144].rearrange("p (c t n) -> p c t n", c=2, t=8)])
        t_io = load(PO, IO[:, :], io["iota"], "q0", t_free)
        t_sk = load(PO, SK[:, :], io["subk"], "q1", t_free)
        tq = []

        def q_out(c, p, tm, sg):
            t = AC.put(lambda e: e.activation(QP[:, c, :], p[:, 0:512], ACT.Copy), tm, t_free)
            tq.append(t)
            return [t]

        linear(4, 8, 256, L, HH, HL, t_h, q_out)
        tok_S, tok_E, tok_M = [None], [None], [None]
        e_ready = {}

        def choose(tt):
            ts = slice(128 * tt, 128 * tt + 128)
            tS = []
            for hf in range(2):
                i, p, free = PS.take()
                PE.wait(free, tq, t_sk)
                for h in range(4):
                    tm = PE.put(lambda e: e.matmul(p[:, 256 * h:256 * h + 256], QP[:, 4 * hf + h, ts], SK[:, :],
                                                   start=True, stop=True), count=(h == 3))
                tS.append(AC.put(lambda e: e.activation(X[:, 4 * hf:4 * hf + 4, 512:768],
                                                        p[:, :].rearrange("p (a b) -> p a b", a=4), ACT.Copy),
                                 tm, tok_S[0], t_free))
                PS.give(i, tS[-1])
            yield

            def top16(src, tmp, mx, ix, after):
                ta = DVE.put(lambda e: e.max(mx[:, 0:8], src), after)
                DVE.put(lambda e: e.max_index(ix[:, 0:8], mx[:, 0:8], src), ta)
                tc = DVE.put(lambda e: e.match_replace(tmp, mx[:, 0:8], src, -3e38), ta)
                td = DVE.put(lambda e: e.max(mx[:, 8:16], tmp), tc)
                return DVE.put(lambda e: e.max_index(ix[:, 8:16], mx[:, 8:16], tmp), td)

            for j in range(16):
                t1 = top16(SX[:, j // 2, j % 2, :], S2[:, 128 * j:128 * j + 128], M1[:, j, :], I1[:, j, :], [tS, tok_M[0], t_free])
                if j % 4 == 3:
                    yield
            tok_S[0] = t1
            for h in range(8):
                sa = M1[:, 2 * h, :].rearrange("p (k o) -> p k o", o=1).broadcast_to([128, 16, 16])
                sbb = M1[:, 2 * h + 1, :].rearrange("p (o k) -> p o k", o=1).broadcast_to([128, 16, 16])
                t2 = DVE.put(lambda e: e.tensor_tensor(CAND[:, h, :, :], sa, sbb, ALU.add), t1)
                t3 = top16(CAND[:, h, :, :].rearrange("p a b -> p (a b)"), S2[:, 256 * h:256 * h + 256], M2[:, h, :],
                           I2[:, h, :], [t2])
                if h % 2 == 1:
                    yield
            vec = lambda j: sg_[:, j, :].rearrange("p (h o) -> p h o", o=1).broadcast_to([128, 8, 16])
            gv = EE[:, 2, :].rearrange("p (h k) -> p h k", h=8)
            t4 = DVE.put(lambda e: e.tensor_tensor(gv, M2[:, :, :], M2[:, :, 0:1].broadcast_to([128, 8, 16]), ALU.subtract),
                         t3, tok_E[0])
            t5 = AC.put(lambda e: e.activation(gv, gv, ACT.Exp), t4)
            ix = I2[:, :, :].rearrange("p h k -> p (h k)")
            t9 = DVE.put(lambda e: e.tensor_scalar(AB2[:, 0, :], ix, 4, None, ALU.logical_shift_right), t3)
            t10 = DVE.put(lambda e: e.tensor_scalar(AB2[:, 1, :], ix, 15, None, ALU.bitwise_and), t3)
            t11 = DVE.put(lambda e: e.tensor_copy(AF[:, :, :], AB2[:, :, :]), t9, t10)
            t12 = DVE.put(lambda e: e.tensor_copy(F1[:, :, :], I1[:, :, :]), t1, t11)
            t6 = DVE.put(lambda e: e.tensor_reduce(sg_[:, 0, :], gv, AX.X, ALU.add), t5)
            t7 = DVE.put(lambda e: e.reciprocal(sg_[:, 1, :], sg_[:, 0, :]), t6)
            t8 = DVE.put(lambda e: e.tensor_tensor(gv, gv, vec(1), ALU.mult), t7)
            yield
            for c in range(2):
                cm = CAND[:, :, :, :].rearrange("p h a b -> p (h a) b")
                t13 = DVE.put(lambda e: e.tensor_tensor(
                    cm, AF[:, c, :].rearrange("p (k o) -> p k o", o=1).broadcast_to([128, 128, 16]),
                    IO[:, 0:16].rearrange("p (o k) -> p o k", o=1).broadcast_to([128, 128, 16]), ALU.is_equal), t12, t_io)
                yield
                for h in range(8):
                    t14 = DVE.put(lambda e: e.tensor_tensor(
                        CAND[:, h, :, :], CAND[:, h, :, :],
                        F1[:, 2 * h + c, :].rearrange("p (o k) -> p o k", o=1).broadcast_to([128, 16, 16]), ALU.mult), t13)
                t12 = DVE.put(lambda e: e.tensor_reduce(EE[:, c, :], cm, AX.X, ALU.add), t14, tok_E[0])
                yield
            tok_M[0] = t12
            i, p, free = PS.take()
            PE.wait(free, t12, t8)
            for c in range(3):
                tm = PE.put(lambda e: e.transpose(p[:, 128 * c:128 * c + 128], EE[:, c, :], ident[:, :]), count=(c == 2))
            for c, dst in enumerate((E1, E2, GG)):
                te = AC.put(lambda e: e.activation(dst[:, ts], p[:, 128 * c:128 * c + 128], ACT.Copy), tm, t_free)
            PS.give(i, te)
            tok_E[0] = tm
            e_ready[tt] = te

        t_gw = []

        def spread(tt):
            late = []

            def finish():
                b, oi, oh, tb = late.pop(0)
                if b % 4 == 0:
                    cur_st.append(GST.take())
                gi, gst, gf = cur_st[-1]
                i, p, free = PS.take()
                PE.wait(free, tb)
                for t in range(8):
                    tm = PE.put(lambda e: e.matmul(p[:, 128 * t:128 * t + 128], oh[:, 1, t, :], oh[:, 0, t, :],
                                                   start=True, stop=True), count=(t == 7))
                OH.give(oi, tm)
                o8 = b % 4
                tg = AC.put(lambda e: e.activation(gst[:, :, 8 * o8:8 * o8 + 8].rearrange("p n t -> p t n"),
                                                   p[:, :].rearrange("p (t n) -> p t n", t=8), ACT.Copy), tm, gf, t_free)
                PS.give(i, tg)
                if o8 == 3:
                    blk = 4 * tt + b // 4
                    tw = load(PO, io["gdram"][blk].rearrange("n p c -> p n c"),
                              gst[:, :, :].rearrange("p (n c) t -> p n (c t)", n=32), "g", tg)
                    GST.give(gi, tw)
                    t_gw.append(tw)

            cur_st = []
            for b in range(16):
                oi, oh, of = OH.take()
                DVE.wait(of, e_ready[tt], t_io, t_free)
                PO.wait(of, e_ready[tt], t_io, t_free)
                for t in range(8):
                    tok = 128 * tt + 8 * b + t
                    ta = DVE.put(lambda e: e.tensor_scalar(oh[:, 0, t, :], IO[:, :], E1[:, tok:tok + 1], GG[:, tok:tok + 1],
                                                           ALU.is_equal, ALU.mult), count=(t == 7))
                    tb = PO.put(lambda e: e.tensor_scalar(oh[:, 1, t, :], IO[:, :], E2[:, tok:tok + 1], None, ALU.is_equal),
                                count=(t == 7))
                late.append((b, oi, oh, [ta, tb]))
                yield
                if len(late) > 1:
                    finish()
            finish()

        def steps(gens):
            live = list(gens)

            def go():
                for g in list(live):
                    if next(g, live) is live:
                        live.remove(g)
                return live
            return go

        phases = [[choose(0)], [spread(0), choose(1)], [spread(1), choose(2)], [spread(2), choose(3)], [spread(3)]]
        runner = [None]

        def route():
            if runner[0] is None:
                if not phases:
                    return
                runner[0] = steps(phases.pop(0))
            if not runner[0]():
                runner[0] = None

        t_aw = {}
        cur_ga = [None]

        def pre(g):
            def emit(c, p, tm, sg):
                if c == 0:
                    cur_ga[0] = GA.take()
                gi, ga, gf = cur_ga[0]
                t = AC.put(lambda e: e.activation(ga[:, c, :], p[:, 0:512], ACT.Gelu_apprx_tanh), tm, gf, t_free)
                if c == 3:
                    t_aw[g] = load(SP, io["adram"][g], ga[:, :, :].rearrange("p c t -> p (c t)"), "aw", t)
                    GA.give(gi, t_aw[g])
                route()
                return [t]
            return emit

        for g in range(NPRE):
            linear(2, 8, 256, L, HH, HL, t_h, pre(g))
        while phases or runner[0] is not None:
            route()
        pr.close()
        ex = ExitStack()
        t_free = [(PE.sem, PE.n), (DVE.sem, DVE.n), (AC.sem, AC.n), (PO.sem, PO.n), t_gw[-1], t_aw[NPRE - 1]]
        AH = [sb(ex, [128, 4, 512], FR) for _ in range(2)]
        AL = [sb(ex, [128, 4, 512], FR) for _ in range(2)]
        GR = [sb(ex, [128, 16, 4, 32]) for _ in range(2)]
        AR = [sb(ex, [128, 512]) for _ in range(3)]
        g_free, a_free, h_used = [None, None], [None] * 3, [None, None]
        g_tok, a_tok = {}, {}

        def fetch(g):
            if g < 32:
                g_tok[g] = load(PO, GR[g % 2][:, :, :, :].rearrange("p b c t -> p b (c t)"),
                                io["gdram"][:, g].rearrange("b p c -> p b c"), f"r{g % 2}", t_free, g_free[g % 2])

        def fetch_a(m):
            if m < 4 * NPRE:
                g, c, k = m // 4, m % 4, m % 3
                a_tok[m] = load(PO, AR[k][:, :], io["adram"][g, :, 512 * c:512 * c + 512], f"s{k}", t_free, a_free[k])

        ready = {}

        def weigh(g, c, tv, after):
            ah, al = AH[g % 2][:, c, :], AL[g % 2][:, c, :]
            flat = tv.rearrange("p b t -> p (b t)")
            t2 = DVE.put(lambda e: e.tensor_tensor(tv, tv, GR[g % 2][:, :, c, :], ALU.mult), after, g_tok[g])
            t3 = AC.put(lambda e: e.activation(ah, flat, ACT.Copy), t2, h_used[g % 2], t_free)
            late.append((g, c, flat, al, ah, t2, t3))

        late = []

        def weigh_low():
            g, c, flat, al, ah, t2, t3 = late.pop(0)
            t4 = DVE.put(lambda e: e.tensor_tensor(al, flat, ah.bitcast(F32), ALU.subtract), t3, h_used[g % 2], t_free)
            ready.setdefault(g, []).append([t3, t4])
            if c == 3:
                g_free[g % 2] = [t4]
                fetch(g + 2)
            if g < NPRE:
                a_free[(4 * g + c) % 3] = [t4]
                fetch_a(4 * g + c + 3)
            return t4

        def prepare(g):
            if g >= 32:
                return
            if g < NPRE:
                for c in range(4):
                    weigh(g, c, AR[(4 * g + c) % 3][:, :].rearrange("p (b t) -> p b t", b=16), a_tok[4 * g + c])
                    if c > 0:
                        weigh_low()
                weigh_low()
                return

            def up(c, p, tm, sg):
                ti, t, tf = T.take()
                t1 = AC.put(lambda e: e.activation(t[:, 0:512], p[:, 0:512], ACT.Gelu_apprx_tanh), tm, tf)
                weigh(g, c, t[:, 0:512].rearrange("p (b t) -> p b t", b=16), t1)
                T.give(ti, weigh_low())
                return [t1]

            linear(2, 8, 256, L, HH, HL, t_h, up)

        last_y = [None] * 8
        fetch(0)
        fetch(1)
        for m in range(3):
            fetch_a(m)
        prepare(0)
        for g in range(32):
            if g + 1 < NPRE:
                prepare(g + 1)
            elif g >= NPRE:
                prepare(g)

            def down(c, p, tm, sg):
                if g == 0:
                    t = AC.put(lambda e: e.activation(Y[:, c, 0:512], p[:, 0:512], ACT.Copy), tm, t_free)
                elif g < 31:
                    t = DVE.put(lambda e: e.tensor_tensor(Y[:, c, 0:512], Y[:, c, 0:512], p[:, 0:512], ALU.add),
                                tm, last_y[c])
                else:
                    t = DVE.put(lambda e: e.tensor_tensor(Y[:, c, 0:512], Y[:, c, 0:512], p[:, 0:512], ALU.add),
                                tm, last_y[c])
                    t2 = DVE.put(lambda e: e.tensor_tensor(X[:, c, 0:512], X[:, c, 0:512], Y[:, c, 0:512], ALU.add), t)
                    t_out.append(load(SP, out_d[:, c, :], X[:, c, 0:512], f"o{c % 4}", t2, t_out[-4] if c >= 4 else None))
                last_y[c] = t
                return [t]

            t_out = []
            h_used[g % 2] = [linear(2, 4, 512, L, AH[g % 2], AL[g % 2], ready[g], down)]
        SP.wait(t_out)
        ex.close()
        HHs.close()
        second.close()
        assert cur[0] == len(plan), (cur[0], len(plan))



def slabs(w, kc, ncol):
    k, n = w.shape
    w = w.reshape(k // (128 * kc), kc, 128, n // ncol, ncol)
    return np.ascontiguousarray(w.transpose(0, 3, 2, 1, 4)).reshape(k // (128 * kc), n // ncol, 128, kc * ncol)


def columns(v):
    return np.ascontiguousarray(np.asarray(v).reshape(-1, 128).T)


def tables():
    f = np.float32
    t = np.arange(512)
    inv = (f(1.0) / (f(10000.0) ** (np.arange(0, 16, 2, dtype=f) / f(16)))).astype(f)
    ar, ac = (t // 64).astype(f)[:, None] * inv, (t % 64).astype(f)[:, None] * inv
    ang = np.concatenate([ar, ar, ac, ac], -1).astype(f)
    cosM, sinM = np.ones((96, 512), f), np.zeros((96, 512), f)
    cosM[64:], sinM[64:] = np.cos(ang).T, np.sin(ang).T
    rotM = np.zeros((96, 96), f)
    for o in (64, 80):
        for i in range(8):
            rotM[o + 8 + i, o + i] = -1
            rotM[o + i, o + 8 + i] = 1
    inv2 = (f(500000.0) ** (-(np.arange(8, dtype=f) * f(2.0) / f(16)))).astype(f)

    def rope2(pos):
        a = (pos.astype(f)[:, None] * inv2[None, :]).astype(f)
        c, s = np.ones((128, len(pos)), f), np.zeros((128, len(pos)), f)
        for o in (0, 8, 64, 72):
            c[o:o + 8], s[o:o + 8] = np.cos(a).T, np.sin(a).T
        return c, s

    cosN, sinN = rope2(t)
    end = np.arange(31) * 16 + 31
    cc, ss = rope2(end)
    cosC, sinC = np.ones((128, 32), f), np.zeros((128, 32), f)
    cosC[:, 0:31], sinC[:, 0:31] = cc, ss
    rotN = np.zeros((128, 128), f)
    for o in (0, 64):
        for i in range(8):
            rotN[o + 8 + i, o + i] = -1
            rotN[o + i, o + 8 + i] = 1
    bones = np.zeros((128, 128), f)
    bones[:64, :64] = 1
    bones[64:, 64:] = 1
    valid = end[None, :] <= t[:, None]
    cmask = np.zeros((128, 2, 4, 32), f)
    cmask[:, 0, :, 0:31] = np.where(valid, 0, NEG).reshape(4, 128, 31).transpose(1, 0, 2)
    cmask[:, 1, :, 0:31] = valid.reshape(4, 128, 31).transpose(1, 0, 2)
    p = np.arange(128)
    slide = np.where(np.arange(896)[None, :] <= p[:, None] + 384, 0, NEG).astype(f)
    dmask = np.zeros((128, 4, 768), f)
    for a in range(4):
        q = 4 * p + a
        d = q[:, None] - t[None, :]
        dmask[:, a, 0:512] = np.where((d >= 0) & (d <= 128), 0, NEG)
        d = p[:, None] - p[None, :]
        dmask[:, a, 512:640] = np.where(d >= 0, 0, NEG)
        dmask[:, a, 640:768] = np.where((d >= 0) & (d % 4 == 0), 0, NEG)
    iota = np.tile(np.arange(128, dtype=f), (128, 1))
    return dict(cosM=cosM, sinM=sinM, rotM=rotM, cosN=cosN, sinN=sinN, cosC=cosC, sinC=sinC, rotN=rotN, bones=bones,
                cmask=cmask, slide=slide, dmask=dmask, iota=iota, ident=np.eye(128, dtype=f), ones=np.ones((128, 128), f))


def lay_out(a):
    a = {k: np.asarray(v) for k, v in a.items()}
    f = np.float32
    d = dict(tables())
    rows3 = lambda x: np.ascontiguousarray(x.T.reshape(8, 128, -1).transpose(1, 0, 2))
    d["xT"] = rows3(a["x"][0])
    d["ctxT"] = rows3(a["ctx"][0])
    d["cT"] = np.ascontiguousarray(np.stack([a["c"][0].reshape(8, 128).T, a["c_ctx"].reshape(8, 128).T], -1))
    cols = []
    for l in range(2):
        cw = a["conf_dw_w"][l].reshape(31, 2, 128).transpose(2, 1, 0).reshape(128, 62)
        sw = a["sc_dw_w"][l].reshape(3, 2, 128).transpose(2, 1, 0).reshape(128, 6)
        cols.append(np.concatenate([columns(a[n][l]) for n in ("g_pre_mix", "g_post_mix", "g_pre_mlp", "g_post_mlp", "g_q", "g_kv",
                                                              "conf_dw_b", "conf_ln_g", "conf_ln_b", "g_branch")]
                                   + [cw, sw, columns(a["b_mod"][l])], 1))
    d["cols"] = np.ascontiguousarray(np.stack(cols))
    two = lambda v: np.concatenate([v, v])[:, None]
    c2 = [columns(a["norm1_g_2"]), columns(a["norm2_g_2"]), two(a["nsa_q_norm_2"])]
    c2 += [two(a["nsa_k_norm_2"][i]) for i in range(3)]
    c2 += [two(a["dil_q_norm_2"][i]) for i in range(3)] + [two(a["dil_k_norm_2"][i]) for i in range(3)]
    c2 = np.concatenate(c2, 1)
    d["cols2"] = np.ascontiguousarray(np.concatenate([c2, np.zeros((128, 32 - c2.shape[1]), f)], 1))
    d["w_mod"] = np.stack([slabs(a["w_mod"][l], 8, 256)[0] for l in range(2)])
    w = a["w_in"]
    ch = lambda s: list(range(s, s + 128))
    order = (ch(256) + list(range(320, 416)) + list(range(320, 352)) + ch(0) + ch(128)
             + ch(672) + ch(416) + ch(800) + ch(544)
             + ch(1440) + ch(1184) + ch(1568) + ch(1312) + ch(928) + ch(1056))
    d["w_in"] = np.stack([slabs(w[l][:, order], 8, 256)[0] for l in range(2)])
    d["w_o"] = np.stack([slabs(a["w_o"][l], 8, 256)[0] for l in range(2)])
    d["w1"] = np.stack([slabs(a["w_mlp_in"][l], 8, 256)[0] for l in range(2)])
    d["w2"] = np.stack([slabs(a["w_mlp_out"][l], 4, 512).reshape(16, 128, 2048) for l in range(2)])
    d["w_q_b"] = np.ascontiguousarray(a["w_q_b"].reshape(2, 2, 128, 768).transpose(0, 2, 1, 3))
    d["w_kv_b"] = a["w_kv_b"]
    w = a["w_in_2"]
    half = lambda s: list(range(s, s + 64))
    order = half(512) + half(640) + half(576) + half(704)
    for c in range(4):
        order += half(64 * c) + half(64 * (c + 4))
    order += ch(768) + ch(1024)
    order += ch(896) + ch(1152)
    D0 = 1304
    dil = lambda g, kind, hp: ch(D0 + 768 * g + 256 * kind + 128 * hp)
    heads = slabs(w[:, order], 8, 256)[0]
    d["win2"] = heads
    d["gate2"] = slabs(w[:, 1280:1304], 8, 24)[0, 0]
    for hp in range(2):
        o = []
        for g in range(3):
            o += dil(g, 0, hp) + dil(g, 1, hp)
        d[f"dqk{hp}"] = slabs(w[:, o], 8, 256)[0]
        d[f"dva{hp}"] = slabs(w[:, dil(0, 2, hp) + dil(1, 2, hp)], 8, 256)[0, 0]
        d[f"dvb{hp}"] = slabs(w[:, dil(2, 2, hp)], 8, 128)[0, 0]
    o = []
    for j in range(8):
        o += ch(3608 + 128 * j) + ch(4632 + 128 * j)
    d["wmg"] = slabs(w[:, o], 8, 256)[0]
    o = []
    for c in range(4):
        o += half(64 * c) + half(64 * (c + 4))
    d["up_nsa"] = slabs(a["w_up_nsa_2"][o], 4, 512)[0]
    d["up_dil"] = slabs(a["w_up_dil_2"], 2, 1024)[0, 0]
    d["w_o2"] = slabs(a["w_o_2"], 8, 256)[0]
    d["wq2"] = slabs(a["peer_wq_2"], 8, 256)[0]
    d["cmp_w1"] = np.concatenate([a["cmp_w1_k_2"].reshape(32, 64, 256).transpose(1, 0, 2),
                                  a["cmp_w1_v_2"].reshape(32, 64, 256).transpose(1, 0, 2)], 0)
    w2 = [a[n].reshape(2, 128, 64).transpose(1, 0, 2) for n in ("cmp_w2_k_2", "cmp_w2_v_2")]
    d["cmp_w2"] = np.ascontiguousarray(np.stack([np.concatenate([x, x], -1) for x in w2], 1))
    d["cmp_pe"] = np.ascontiguousarray(np.concatenate([a["cmp_pe_k_2"].T, a["cmp_pe_v_2"].T], 0))
    sk = np.zeros((128, 256), f)
    sk[0:64, 0:128], sk[64:128, 128:256] = a["peer_subkeys_2"][0].T, a["peer_subkeys_2"][1].T
    d["subk"] = sk
    d["u2"] = slabs(np.ascontiguousarray(a["peer_u_2"].T), 8, 256)[0]
    d["v2"] = slabs(a["peer_v_2"], 4, 512).reshape(64, 128, 2048)
    return {k: np.ascontiguousarray(v) for k, v in d.items()}


def program(nc, arrays):
    io = {n: nc.dram_tensor(f"in_{n}", v.shape, F32, kind="ExternalInput").ap() for n, v in arrays.items()}
    io["gdram"] = nc.dram_tensor("gdram", (16, 32, 128, 128), F32, kind="Internal").ap()
    io["adram"] = nc.dram_tensor("adram", (NPRE, 128, 2048), F32, kind="Internal").ap()
    io["out"] = nc.dram_tensor("out_0", (128, 8, 512), F32, kind="ExternalOutput").ap()
    build(nc, io)


def kernel(**inputs):
    import concourse.bacc as bacc
    from concourse.bass_utils import run_bass_kernel_spmd as run

    arrays = lay_out(inputs)
    nc = bacc.Bacc("TRN2", target_bir_lowering=False, num_devices=1)
    program(nc, arrays)
    r = run(nc, [{f"in_{n}": v for n, v in arrays.items()}], core_ids=[0])
    o = np.asarray(r.results[0]["out_0"])
    return np.ascontiguousarray(o.transpose(1, 0, 2).reshape(1024, 512).T).reshape(1, 512, 1024)
```

```python
from contextlib import ExitStack

import numpy as np
import concourse.bass as bass
from concourse import mybir

ALU = mybir.AluOpType
ACT = mybir.ActivationFunctionType
AX = mybir.AxisListType
F32 = mybir.dt.float32
FR = mybir.dt.float32r
U32 = mybir.dt.uint32

EPS = 1e-6
NEG = -1e30
LAT = (0, 512)
CTX = (512, 256)
SLAB = 2048
NPRE = 22


class Engine:

    def __init__(self, engine, sem):
        self.e, self.sem, self.n, self.seen = engine, sem, 0, {}

    def wait(self, *after):
        for t in after:
            if t is None:
                continue
            if isinstance(t, list):
                self.wait(*t)
                continue
            sem, value = t
            if self.seen.get(id(sem), 0) < value:
                self.seen[id(sem)] = value
                self.e.wait_ge(sem, value)

    def put(self, fn, *after, count=True):
        self.wait(*after)
        ins = fn(self.e)
        if not count:
            return None
        self.n += 1
        ins.then_inc(self.sem, 1)
        return (self.sem, self.n)

    def dma(self, out, in_, sem, value, *after):
        self.wait(*after)
        self.e.dma_start(out, in_).then_inc(sem, 16)
        return (sem, value)


class Ring:

    def __init__(self, bufs):
        self.bufs, self.free = bufs, [(i, []) for i in range(len(bufs))]

    def take(self):
        i, after = self.free.pop(0)
        return i, self.bufs[i], after

    def give(self, i, *after):
        self.free.append((i, list(after)))


def build(nc, io):
    out_d = io["out"]
    with ExitStack() as top:
        names = [0]

        def sb(stack, shape, dt=F32):
            names[0] += 1
            return stack.enter_context(nc.sbuf_tensor(f"sb{names[0]}", shape, dt))

        def sem():
            names[0] += 1
            return top.enter_context(nc.semaphore(f"sem{names[0]}"))

        PE, DVE, AC, PO, SP = (Engine(e, sem()) for e in (nc.tensor, nc.vector, nc.scalar, nc.gpsimd, nc.sync))
        dma_sems = {}

        def load(eng, out, in_, name, *after):
            s, n = dma_sems.get(name, (None, 0))
            s = s or sem()
            dma_sems[name] = (s, n + 16)
            return eng.dma(out, in_, s, n + 16, *after)

        X = sb(top, [128, 8, 768])
        Y = sb(top, [128, 8, 768])
        ps = [top.enter_context(nc.psum_tensor(f"ps{i}", [128, 1024], F32)) for i in range(4)]
        PS = Ring(ps)
        stage = [sb(top, [128, SLAB]) for _ in range(2)]
        WHb = [sb(top, [128, SLAB], FR) for _ in range(2)]
        WLb = [sb(top, [128, SLAB], FR) for _ in range(2)]
        T = Ring([sb(top, [128, 768]) for _ in range(3)])
        RS = Ring([sb(top, [128, 768]) for _ in range(2)])
        epsc = sb(top, [128, 1])
        ident = sb(top, [128, 128])
        ones = sb(top, [128, 128])
        cols = [sb(top, [128, 165]) for _ in range(2)]
        cols2 = sb(top, [128, 32])
        MODs = [sb(top, [128, 48, 2]) for _ in range(2)]
        mrow = [sb(top, [2, 256]) for _ in range(2)]
        csil = sb(top, [128, 8, 2])
        AB = sb(top, [128, 6, 8, 2])

        t_x = load(SP, X[:, :, 0:512], io["xT"], "x0")
        t_xc = load(SP, X[:, :, 512:768], io["ctxT"], "x1")
        t_id = load(PO, ident[:, :], io["ident"], "c0")
        t_ones = load(PO, ones[:, :], io["ones"], "c1")
        t_cols = [load(PO, cols[i][:, :], io["cols"][i], f"c{2 + i}") for i in range(2)]
        t_cols2 = load(PO, cols2[:, :], io["cols2"], "c4")
        t_eps = DVE.put(lambda e: e.memset(epsc[:, :], EPS))
        AC.wait(t_eps, t_cols)
        DVE.wait(t_cols, t_cols2, t_eps)
        PE.wait(t_id, t_ones)

        plan = []

        def weave(slabs, mods):
            return [x for w, m in zip(slabs, mods) for x in [("split", w)] + [("raw", v) for v in m]]

        mod_slabs = [[io["w_mod"][l, s] for s in range(24)] for l in range(2)]
        IN_MODS = [2] * 7
        OUT_MODS = [1, 1, 0, 0]
        plan += [("raw", v) for v in mod_slabs[0][0:8]]
        for l in range(2):
            rest = mod_slabs[0][8:] if l == 0 else []
            plan += weave([io["w_in"][l, s] for s in range(7)], [[rest.pop(0) for _ in range(2 * (l == 0))] for _ in range(7)])
            plan += weave([io["w_o"][l, s] for s in range(4)], [[rest.pop(0)] if rest else [] for _ in range(4)])
            ff = []
            for g in range(8):
                ff += [io["w1"][l, 2 * g + s] for s in range(2)] + [io["w2"][l, 2 * g + s] for s in range(2)]
            plan += weave(ff, [[mod_slabs[1][i]] if l == 0 and i < 24 else [] for i in range(32)])
        plan += [("split", io["win2"][s]) for s in range(5)]
        plan += [("split", io["gate2"])]
        for hp in range(2):
            plan += [("split", io[f"wdqk{hp}"][s]) for s in range(3)]
            plan += [("split", io[f"dva{hp}"]), ("split", io[f"dvb{hp}"])]
        plan += [("split", io["wmg"][s]) for s in range(8)]
        plan += [("split", io["up_nsa"][s]) for s in range(2)]
        plan += [("split", io["up_dil"])]
        plan += [("split", io["w_o2"][s]) for s in range(4)]
        plan += [("split", io["wq2"][s]) for s in range(4)]
        for g in range(NPRE):
            plan += [("split", io["u2"][2 * g + s]) for s in range(2)]
        for g in range(32):
            if g >= NPRE:
                plan += [("split", io["u2"][2 * g + s]) for s in range(2)]
            plan += [("split", io["v2"][2 * g + s]) for s in range(2)]
        landed = {}
        stage_free = [None, None]
        w_ready = {}
        w_free = [None, None]
        nsplit = [0]
        sent = [0]
        split_no = {}

        def send(n):
            while sent[0] <= min(n, len(plan) - 1):
                m = sent[0]
                src = plan[m][1]
                landed[m] = load(SP, stage[m % 2][:, 0:src.shape[-1]], src, f"w{m % 2}", stage_free[m % 2])
                sent[0] += 1

        def split(n):
            if n >= len(plan) or plan[n][0] == "raw" or n in w_ready:
                return
            send(n)
            k = nsplit[0] % 2
            nsplit[0] += 1
            w = plan[n][1].shape[-1]
            st = stage[n % 2][:, 0:w]
            th = AC.put(lambda e: e.activation(WHb[k][:, 0:w], st, ACT.Copy), landed[n], w_free[k])
            tl = DVE.put(lambda e: e.tensor_tensor(WLb[k][:, 0:w], st, WHb[k][:, 0:w].bitcast(F32), ALU.subtract),
                         landed[n], th, w_free[k])
            stage_free[n % 2] = [tl]
            w_ready[n] = [th, tl]
            split_no[n] = k

        cur = [0]

        def take_raw():
            n = cur[0]
            cur[0] += 1
            send(n + 1)
            if plan[n + 1][0] == "split":
                split(n + 1)
            return n, stage[n % 2], landed[n]

        def give_raw(n, *after):
            stage_free[n % 2] = list(after)
            send(n + 2)

        def take_slab():
            n = cur[0]
            cur[0] += 1
            send(n)
            split(n)
            send(n + 2)
            if n + 1 < len(plan) and plan[n + 1][0] == "split":
                split(n + 1)
                send(n + 3)
            k = split_no[n]
            return k, WHb[k], WLb[k], w_ready[n]

        def give_slab(k, *after):
            w_free[k] = list(after)

        background = []

        def idle(n=1):
            for _ in range(n):
                if background:
                    background.pop(0)()

        def three(out, ah, al, bh, bl, first, last):
            PE.put(lambda e: e.matmul(out, ah, bh, start=first, stop=False), count=False)
            PE.put(lambda e: e.matmul(out, ah, bl, start=False, stop=False), count=False)
            return PE.put(lambda e: e.matmul(out, al, bh, start=False, stop=last), count=last)

        extra = []

        def linear(nslab, K, ncol, segs, HH, HL, ready, emit, mods=0, order=None):
            c = 0
            last = None
            for _ in range(nslab):
                k, wh, wl, wr = take_slab()
                wh = wh[:, 0:K * ncol].rearrange("p (k n) -> p k n", k=K)
                wl = wl[:, 0:K * ncol].rearrange("p (k n) -> p k n", k=K)
                nj = ncol // 128
                j = 0
                while j < nj:
                    pair = [j, j + 1] if c == 0 and (K == 4 or order) else [j]
                    held = []
                    for jj in pair:
                        i, p, free = PS.take()
                        held.append((i, p, free, jj, c + jj - j))
                    ks = order or list(range(K))
                    parts = [ks] if len(pair) == 1 else [ks[:-1], ks[-1:]] if K == 4 else [[kk] for kk in ks]
                    ends = {}
                    owed = mods if j == 0 else 0
                    for part in parts:
                        if len(part) == 1 and part[0] == ks[K // 2]:
                            while owed and extra:
                                owed -= 1
                                extra.pop(0)()
                        for (i, p, free, jj, cc) in held:
                            sg = segs(cc) if callable(segs) else segs
                            PE.wait(free, wr)
                            cs = slice(128 * jj, 128 * jj + 128)
                            for kk in part:
                                PE.wait(ready[kk])
                                for (s0, sn) in sg:
                                    t = three(p[:, s0:s0 + sn], wh[:, kk, cs], wl[:, kk, cs],
                                              HH[:, kk, s0:s0 + sn], HL[:, kk, s0:s0 + sn], kk == ks[0], kk == ks[-1])
                                    ends[cc] = t or ends.get(cc)
                    for (i, p, free, jj, cc) in held:
                        sg = segs(cc) if callable(segs) else segs
                        last = ends[cc]
                        PS.give(i, *emit(cc, p, last, sg))
                        idle()
                    j += len(pair)
                    c += len(pair)
                    while owed and extra:
                        owed -= 1
                        extra.pop(0)()
                give_slab(k, last)
            return last

        def span(segs):
            return min(s for s, _ in segs), max(s + n for s, n in segs)

        class Stats:

            def __init__(self, n, segs, D, lhs=None):
                self.n, self.segs, self.D, self.lhs = n, segs, D, lhs if lhs is not None else ones[:, :]
                self.c, self.held, self.tile = 0, None, None

            def flush(self):
                if self.held is None:
                    return
                c, ti, t, tq = self.held
                i, p, free = self.tile
                PE.wait(free)
                for (s0, sn) in self.segs:
                    tm = PE.put(lambda e: e.matmul(p[:, s0:s0 + sn], self.lhs, t[:, s0:s0 + sn], start=(c == 0),
                                                   stop=(c == self.n - 1)), tq)
                T.give(ti, tm)
                self.held, self.tm = None, tm

            def add(self, s, *ready):
                a, b = span(self.segs)
                self.flush()
                if self.tile is None:
                    self.tile = PS.take()
                ti, t, tf = T.take()
                tq = AC.put(lambda e: e.activation(t[:, a:b], s[:, a:b], ACT.Square), tf, list(ready))
                self.held = (self.c, ti, t, tq)
                self.c += 1
                return self

            def finish(self):
                self.flush()
                a, b = span(self.segs)
                i, p, free = self.tile
                ri, r, rf = RS.take()
                t1 = AC.put(lambda e: e.activation(r[:, a:b], p[:, a:b], ACT.Ln, bias=epsc[:, 0:1], scale=1.0 / self.D),
                            self.tm, rf)
                t2 = AC.put(lambda e: e.activation(r[:, a:b], r[:, a:b], ACT.Exp, scale=-0.5), t1)
                PS.give(i, t1)
                return ri, r, t2

        def stats_of(src, segs, D, ready, lhs=None):
            st = Stats(len(src), segs, D, lhs)
            for s in src:
                st.add(s, ready)
            return st

        def norm_split(src, segs, stats, scale, shift, HH, HL, c0, hfree):
            ri, r, tr = stats.finish()
            done = []
            late = []

            def low():
                c, ti, t, ths = late.pop(0)
                for (s0, sn), th in zip(segs, ths):
                    z = slice(s0, s0 + sn)
                    b = shift(c, s0) if shift else 0.0
                    tl = DVE.put(lambda e: e.scalar_tensor_tensor(HL[:, c0 + c, z], t[:, z], b, HH[:, c0 + c, z].bitcast(F32),
                                                                  ALU.add, ALU.subtract), th, hfree)
                T.give(ti, th, tl)
                done.append([ths[-1], tl])

            for c, s in enumerate(src):
                ti, t, tf = T.take()
                ths = []
                tms = [DVE.put(lambda e: e.scalar_tensor_tensor(t[:, s0:s0 + sn], s[:, s0:s0 + sn], scale(c, s0),
                                                                r[:, s0:s0 + sn], ALU.mult, ALU.mult), tr, tf)
                       for (s0, sn) in segs]
                for (s0, sn), tm in zip(segs, tms):
                    z = slice(s0, s0 + sn)
                    if shift:
                        b = shift(c, s0)
                        th = AC.put(lambda e: e.activation(HH[:, c0 + c, z], t[:, z], ACT.Identity, bias=b), tm, hfree)
                    else:
                        th = AC.put(lambda e: e.activation(HH[:, c0 + c, z], t[:, z], ACT.Copy), tm, hfree)
                    ths.append(th)
                late.append((c, ti, t, ths))
                if c > 0:
                    low()
            low()
            RS.give(ri, tms[-1])
            return done

        def add_normed(segs, stats, scale, after):
            ri, r, tr = stats.finish()
            late = []

            def add():
                c, ti, t, tm = late.pop(0)
                a, b = span(segs)
                ta = DVE.put(lambda e: e.tensor_tensor(X[:, c, a:b], X[:, c, a:b], t[:, a:b], ALU.add), tm)
                T.give(ti, ta)
                after(c, ta)
                return ta

            for c in range(8):
                ti, t, tf = T.take()
                for (s0, sn) in segs:
                    z = slice(s0, s0 + sn)
                    tm = DVE.put(lambda e: e.scalar_tensor_tensor(t[:, z], Y[:, c, z], scale(c, s0), r[:, z],
                                                                  ALU.mult, ALU.mult), tr, tf)
                late.append((c, ti, t, tm))
                if c > 0:
                    add()
            ta = add()
            RS.give(ri, tm)
            return ta

        def mlp(groups, segs, HH, HL, AH, AL, ready, activate, yfree, ystats, mods=0):
            a, b = span(segs)
            last_y = [None] * 8
            afree = []
            for g in range(groups):
                done = []

                def up(c, p, tm, sg):
                    d = activate(g, c, p, tm, AH[:, c, :], AL[:, c, :], afree)
                    done.append(d[0])
                    return d[1]

                linear(2, 8, 256, segs, HH, HL, ready, up, mods, list(range(8)) if g == 0 else None)

                def down(c, p, tm, sg):
                    if g == 0:
                        t = AC.put(lambda e: e.activation(Y[:, c, a:b], p[:, a:b], ACT.Copy), tm, yfree)
                    else:
                        t = DVE.put(lambda e: e.tensor_tensor(Y[:, c, a:b], Y[:, c, a:b], p[:, a:b], ALU.add),
                                    tm, last_y[c])
                    last_y[c] = t
                    if g == groups - 1:
                        ystats.add(Y[:, c, :], t)
                    return [t]

                last = linear(2, 4, 512, segs, AH, AL, done, down, mods)
                afree = [last]
            return last_y

        first = ExitStack()
        cT = sb(first, [128, 8, 2])
        rotM = sb(first, [96, 96])
        cosM = sb(first, [96, 512])
        sinM = sb(first, [96, 512])
        t_c = load(PO, cT[:, :, :], io["cT"], "k0")
        t_tab = [load(PO, rotM[:, :], io["rotM"], "k1"), load(PO, cosM[:, :], io["cosM"], "k2"),
                 load(PO, sinM[:, :], io["sinM"], "k3")]
        t_sc = AC.put(lambda e: e.activation(csil[:, :, :], cT[:, :, :], ACT.Silu), t_c)
        x_ready = [t_x, t_xc]
        G_PRE, G_POST, G_PRE2, G_POST2, G_Q, G_KV, DW_B, LN_G, LN_B, G_BR, CW, SW, B_MOD = (
            0, 8, 16, 24, 32, 34, 35, 37, 39, 41, 49, 111, 117)
        t_m48 = [[None] * 24 for _ in range(2)]
        mod_late = []
        row_free = [None, None]

        def mod_close():
            l, s, i, p, te = mod_late.pop(0)
            for j in range(2):
                tm = PE.put(lambda e: e.matmul(p[:, 512 + 2 * j:514 + 2 * j], mrow[s % 2][:, 128 * j:128 * j + 128],
                                               ident[0:2, 0:2], start=True, stop=True), te, count=(j == 1))
            row_free[s % 2] = tm
            o = B_MOD + 2 * s
            t = DVE.put(lambda e: e.tensor_tensor(
                MODs[l][:, 2 * s:2 * s + 2, :], p[:, 512:516].rearrange("p (c v) -> p c v", v=2),
                cols[l][:, o:o + 2].rearrange("p (c v) -> p c v", v=1).broadcast_to([128, 2, 2]), ALU.add), tm)
            PS.give(i, t)
            t_m48[l][s] = t

        def mod_slab(l, s):
            i, p, free = PS.take()
            PE.wait(free, t_sc)
            n, w, tw = take_raw()
            w = w[:, :].rearrange("p (k n) -> p k n", k=8)
            for k in range(8):
                tm = PE.put(lambda e: e.matmul(p[0:2, 0:256], csil[:, k, :], w[:, k, :], start=(k == 0), stop=(k == 7)),
                            tw, count=(k == 7))
            give_raw(n, tm)
            te = AC.put(lambda e: e.activation(mrow[s % 2][:, :], p[0:2, 0:256], ACT.Copy), tm, row_free[s % 2])
            if mod_late:
                mod_close()
            mod_late.append((l, s, i, p, te))
            if s in (7, 23):
                mod_close()

        for s in range(8):
            mod_slab(0, s)
        extra.extend([lambda s=s: mod_slab(0, s) for s in range(8, 24)])

        def scales(l, dst, m, g, plus, after):
            for v in range(2):
                t = DVE.put(lambda e: e.scalar_tensor_tensor(AB[:, dst, :, v],
                                                             MODs[l][:, 8 * m:8 * m + 8, v], plus, cols[l][:, g:g + 8],
                                                             ALU.add, ALU.mult), t_m48[l][4 * m:4 * m + 4], after)
            return [t] + t_m48[l]

        for l in range(2):
            both = [LAT, CTX] if l == 0 else [LAT]
            col = cols[l]
            md = MODs[l][:, :, :].rearrange("p (m c) v -> p m c v", m=6)
            which = lambda s0: 0 if s0 < 512 else 1
            A_ = lambda d: (lambda c, s0: AB[:, d, c, which(s0):which(s0) + 1])
            B_ = lambda m: (lambda c, s0: md[:, m, c, which(s0):which(s0) + 1])
            t_pre = scales(l, 0, 1, G_PRE, 1.0, x_ready)

            z = ExitStack()
            ZQ = sb(z, [128, 2, 768])
            ZKV = sb(z, [128, 768])
            KR = sb(z, [96, 768])
            UW = 16 + 512 + 16 + 256 + 16
            U = sb(z, [128, 2, UW])
            CH = sb(z, [128, 2, UW])
            G2 = Ring([sb(z, [128, 768]) for _ in range(2)])
            HHs = ExitStack()
            HH, HL = sb(HHs, [128, 8, 768], FR), sb(HHs, [128, 8, 768], FR)
            h_free = [] if l == 0 else t_phase
            t_z0 = [DVE.put(lambda e: e.memset(U[:, :, :], 0.0), h_free),
                    DVE.put(lambda e: e.memset(CH[:, :, :], 0.0), h_free)]
            xs = [X[:, c, :] for c in range(8)]
            st = stats_of(xs, [LAT, CTX], 1024, x_ready) if l == 0 else x_stats
            DVE.wait(t_pre)
            AC.wait(t_pre)
            t_h = norm_split(xs, [LAT, CTX], st, A_(0), B_(0), HH, HL, 0, h_free)

            def padded(buf, c, s0, sn, shift=0):
                o = 16 + s0 if s0 == 0 else 16 + 512 + 16
                return buf[:, c, o + shift:o + shift + sn]

            z_done = []
            sigs = {}
            ORDER = ["kv", "kr", "q0", "q1", "g0", "a0", "g1", "a1", "h0", "c0", "h1", "c1", "b0", "b1"]

            def z_out(c, p, tm, sg):
                a, b = span(sg)
                kind = ORDER[c]
                if kind == "kv":
                    t = AC.put(lambda e: e.activation(ZKV[:, a:b], p[:, a:b], ACT.Copy), tm, h_free)
                elif kind == "kr":
                    t = AC.put(lambda e: e.activation(KR[:, a:b], p[0:96, a:b], ACT.Copy), tm, h_free)
                elif kind[0] == "q":
                    j = int(kind[1])
                    t = AC.put(lambda e: e.activation(ZQ[:, j, a:b], p[:, a:b], ACT.Copy), tm, h_free)
                elif kind[0] in "gh":
                    gi, g, gf = G2.take()
                    t = AC.put(lambda e: e.activation(g[:, a:b], p[:, a:b], ACT.Sigmoid if kind[0] == "g" else ACT.Copy),
                               tm, gf, h_free)
                    sigs[kind] = (gi, g, t)
                elif kind[0] in "ac":
                    j = int(kind[1])
                    gi, g, tg = sigs[("g" if kind[0] == "a" else "h") + kind[1]]
                    dst = U if kind[0] == "a" else CH
                    for (s0, sn) in sg:
                        t = DVE.put(lambda e: e.tensor_tensor(padded(dst, j, s0, sn), p[:, s0:s0 + sn],
                                                              g[:, s0:s0 + sn], ALU.mult), tm, tg, t_z0)
                    G2.give(gi, t)
                else:
                    j = int(kind[1])
                    t = AC.put(lambda e: e.activation(Y[:, 6 + j, a:b], p[:, a:b], ACT.Copy), tm, y_free)
                z_done.append(t)
                return [t]

            y_free = [] if l == 0 else t_phase
            in_segs = lambda c: [LAT, CTX] if ORDER[c] in ("kv", "kr") else both
            last = linear(7, 8, 256, in_segs, HH, HL, t_h, z_out, 2, list(range(8)))
            t_zdone = z_done
            t_hh = [last] + t_h[-1]
            HHs.close()

            att = ExitStack()
            WQ = sb(att, [128, 2, 768])
            WKV = sb(att, [128, 1024])
            V = sb(att, [128, 6, 512])
            QR = Ring([sb(att, [96, 768]) for _ in range(2)])
            KRr = Ring([sb(att, [96, 768]) for _ in range(2)])
            Pb = Ring([sb(att, [128, 768])] + G2.bufs)
            PTb = Ring([sb(att, [128, 768]) for _ in range(2)])
            OT = Ring([sb(att, [128, 6, 128]) for _ in range(2)])
            MX = sb(att, [128, 2, 64])
            ACC = sb(att, [128, UW])
            t_wq = load(PO, WQ[:, :, :], io["w_q_b"][l], "q0", t_hh)
            t_wkv = load(PO, WKV[:, :], io["w_kv_b"][l], "q1", t_hh)

            def conv(buf, j, taps, half, w0, bias, acc, after, free):
                n = UW - 32 if l == 0 else 512
                last = [None]

                def tap(k):
                    def go():
                        src = buf[:, j, 16 + k - half:16 + k - half + n]
                        w = col[:, w0 + taps * j + k:w0 + taps * j + k + 1]
                        if k == 0:
                            if bias is None:
                                last[0] = DVE.put(lambda e: e.tensor_scalar(acc[:, 0:n], src, w, None, ALU.mult),
                                                  after, free)
                            else:
                                last[0] = DVE.put(lambda e: e.tensor_scalar(acc[:, 0:n], src, w, bias, ALU.mult,
                                                                            ALU.add), after, free)
                        else:
                            last[0] = DVE.put(lambda e: e.scalar_tensor_tensor(acc[:, 0:n], src, w, acc[:, 0:n],
                                                                               ALU.mult, ALU.add), last[0])
                    return go
                return [tap(k) for k in range(taps)], last

            conv_tok = {}
            acc_free = [t_hh]

            def close_conf(j, last):
                def go():
                    for (s0, sn) in both:
                        o = s0 if s0 == 0 else 528
                        t = DVE.put(lambda e: e.tensor_copy(Y[:, 4 + j, s0:s0 + sn], ACC[:, o:o + sn]), last[0], y_free)
                    conv_tok[4 + j] = t
                    acc_free[0] = [t]
                return go

            def close_sc(j, last):
                def go():
                    for (s0, sn) in both:
                        o = s0 if s0 == 0 else 528
                        t = DVE.put(lambda e: e.tensor_tensor(Y[:, 6 + j, s0:s0 + sn], Y[:, 6 + j, s0:s0 + sn],
                                                              ACC[:, o:o + sn], ALU.mult), last[0], t_zdone)
                    conv_tok[6 + j] = t
                    acc_free[0] = [t]
                return go

            for j in range(2):
                fs, last_c = conv(U, j, 31, 15, CW, col[:, DW_B + j:DW_B + j + 1], ACC, t_zdone, acc_free)
                background.extend(fs + [close_conf(j, last_c)])
            for j in range(2):
                fs, last_c = conv(CH, j, 3, 1, SW, None, ACC, t_zdone, acc_free)
                background.extend(fs + [close_sc(j, last_c)])

            def norm_in_place(src, segs, D, g, ready):
                ri, r, tr = stats_of(src, segs, D, ready).finish()
                a, b = span(segs)
                for c, s in enumerate(src):
                    t = DVE.put(lambda e: e.scalar_tensor_tensor(s[:, a:b], s[:, a:b], col[:, g + c:g + c + 1],
                                                                 r[:, a:b], ALU.mult, ALU.mult), tr)
                RS.give(ri, t)
                return t

            t_kvn = norm_in_place([ZKV[:, :]], [LAT, CTX], 128, G_KV, t_zdone)
            t_qn = norm_in_place([ZQ[:, j, :] for j in range(2)], both, 256, G_Q, t_zdone)

            def rope(buf, ready):
                i, p, free = PS.take()
                tm = PE.put(lambda e: e.matmul(p[0:96, 0:512], rotM[:, :], buf[:, 0:512], start=True, stop=True),
                            free, ready, t_tab)
                ti, t, tf = T.take()
                ta = DVE.put(lambda e: e.tensor_tensor(t[0:96, 0:512], p[0:96, 0:512], sinM[:, :], ALU.mult), tm, tf,
                             t_tab)
                PS.give(i, ta)
                tb = DVE.put(lambda e: e.tensor_tensor(buf[:, 0:512], buf[:, 0:512], cosM[:, :], ALU.mult), ready, tm)
                tc = DVE.put(lambda e: e.tensor_tensor(buf[:, 0:512], buf[:, 0:512], t[0:96, 0:512], ALU.add), ta, tb)
                T.give(ti, tc)
                return tc

            t_kr = rope(KR, t_zdone)
            for i, buf in enumerate(KRr.bufs):
                t_kc = DVE.put(lambda e: e.tensor_copy(buf[64:96, :], KR[64:96, :]), t_kr, t_hh)
            t_v = []
            for tt in range(6):
                i, p, free = PS.take()
                tm = PE.put(lambda e: e.matmul(p[:, 0:512], ZKV[:, 128 * tt:128 * tt + 128],
                                               WKV[:, :].rearrange("p (h a d) -> p h a d", h=8, a=2)[:, :, 1, :],
                                               start=True, stop=True), free, t_kvn, t_wkv)
                tc = AC.put(lambda e: e.activation(V[:, tt, :], p[:, 0:512], ACT.Copy), tm, t_hh)
                PS.give(i, tc)
                t_v.append(tc)

            SM = 1.0 / float(np.sqrt(np.float64(96)))

            def head_in(h):
                ki, kb, kf = KRr.take()
                i, p, free = PS.take()
                PE.wait(free, t_kvn, t_wkv)
                for (s0, sn) in (LAT, CTX):
                    tm = PE.put(lambda e: e.matmul(p[:, s0:s0 + sn], WKV[:, 128 * h:128 * h + 128],
                                                   ZKV[:, s0:s0 + sn], start=True, stop=True))
                tk = AC.put(lambda e: e.activation(kb[0:64, :], p[0:64, 0:768], ACT.Copy), tm, kf, t_kc)
                PS.give(i, tk)
                yield
                qi, qb, qf = QR.take()
                a, b = span(both)
                i, p, free = PS.take()
                PE.wait(free, t_qn, t_wq)
                for (s0, sn) in both:
                    for k in range(2):
                        tm = PE.put(lambda e: e.matmul(p[0:96, s0:s0 + sn], WQ[:, k, 96 * h:96 * h + 96],
                                                       ZQ[:, k, s0:s0 + sn], start=(k == 0), stop=(k == 1)))
                tq = AC.put(lambda e: e.activation(qb[:, a:b], p[0:96, a:b], ACT.Copy, scale=SM), tm, qf, t_hh)
                PS.give(i, tq)
                yield
                heads[h] = (ki, kb, [tk, t_kc]), (qi, qb, [tq, rope(qb, tq)])
                yield

            units = []
            for h in range(8):
                for qt in range(4):
                    units.append((h, 128 * qt, 0, 768))
                if l == 0:
                    for qt in range(2):
                        units.append((h, 512 + 128 * qt, 512, 256))
            per = len(units) // 8
            heads = {}
            for _ in head_in(0):
                pass
            O = {}
            a, b_ = span(both)
            nq = (b_ - a) // 128

            def scores(h, q0, k0, kn):
                (ki, kb, tk), (qi, qb, tq) = heads[h]
                i, p, free = PS.take()
                PE.wait(free, tk, tq)
                for (s0, sn) in ([LAT, CTX] if kn == 768 else [(0, 256)]):
                    tm = PE.put(lambda e: e.matmul(p[:, s0:s0 + sn], qb[:, q0:q0 + 128], kb[:, k0 + s0:k0 + s0 + sn],
                                                   start=True, stop=True))
                if q0 == b_ - 128:
                    KRr.give(ki, tm)
                    QR.give(qi, tm)
                pi, pb, pf = Pb.take()
                u = nq * h + q0 // 128
                t1 = DVE.put(lambda e: e.tensor_reduce(MX[:, 0, u:u + 1], p[:, 0:kn], AX.X, ALU.max, negate=True), tm, t_hh)
                t2 = AC.put(lambda e: e.activation(pb[:, 0:kn], p[:, 0:kn], ACT.Exp, bias=MX[:, 0, u:u + 1],
                                                   accum_out=MX[:, 1, u:u + 1]), t1, pf, t_hh)
                PS.give(i, t2)
                return pi, pb, t2

            def turn(u, s):
                h, q0, k0, kn = u
                pi, pb, tp = s
                nb = kn // 128
                i, p, free = PS.take()
                PE.wait(free, tp)
                for b in range(nb):
                    tt = PE.put(lambda e: e.transpose(p[:, 128 * b:128 * b + 128], pb[:, 128 * b:128 * b + 128],
                                                      ident[:, :]), count=(b == nb - 1))
                Pb.give(pi, tt)
                ti, ptb, ptf = PTb.take()
                tc = AC.put(lambda e: e.activation(ptb[:, 0:kn], p[:, 0:kn], ACT.Copy), tt, ptf, t_hh)
                PS.give(i, tc)
                return ti, ptb, tc, tp

            att_stats = Stats(4, both, 512)
            t_att = []

            def values(u, s):
                h, q0, k0, kn = u
                ti, ptb, tc, tp = s
                if h % 2 == 0 and q0 == 0:
                    O[h // 2] = PS.take() + OT.take()
                oi, o, of, xi, ot, xf = O[h // 2]
                PE.wait(of, tc, t_v)
                nb = kn // 128
                o0 = 512 * (h % 2) + q0 // 2
                for b in range(nb):
                    tv = PE.put(lambda e: e.matmul(o[:, o0:o0 + 64], ptb[:, 128 * b:128 * b + 128],
                                                   V[:, k0 // 128 + b, 64 * h:64 * h + 64], start=(b == 0),
                                                   stop=(b == nb - 1)), count=(b == nb - 1))
                PTb.give(ti, tv)
                if q0 != b_ - 128:
                    return
                ov = o[:, 512 * (h % 2):512 * (h % 2) + 64 * nq].rearrange("p (q d) -> p q d", d=64)
                mx = MX[:, 1, nq * h:nq * h + nq]
                t1 = DVE.put(lambda e: e.reciprocal(mx, mx), tp)
                t2 = DVE.put(lambda e: e.tensor_tensor(
                    ot[:, 0:nq, 64 * (h % 2):64 * (h % 2) + 64], ov,
                    mx.rearrange("p (q d) -> p q d", d=1).broadcast_to([128, nq, 64]), ALU.mult), t1, tv, xf, t_hh)
                if h % 2 == 0:
                    return
                PS.give(oi, t2)
                O.pop(h // 2)
                pairs.append((h // 2, xi, ot, t2))

            pairs = []

            def close_pair():
                c, xi, ot, t2 = pairs.pop(0)
                i, p, free = PS.take()
                PE.wait(free, t2)
                for q in range(nq):
                    tt = PE.put(lambda e: e.transpose(p[:, 128 * q:128 * q + 128], ot[:, q, :], ident[:, :]),
                                count=(q == nq - 1))
                OT.give(xi, tt)
                tc = AC.put(lambda e: e.activation(Y[:, c, a:b_], p[:, a:b_], ACT.Copy), tt, y_free)
                PS.give(i, tc)
                t_att.append(tc)

            def conf_norm():
                i, p, free = PS.take()
                PE.wait(free, conv_tok[4], conv_tok[5])
                for (s0, sn) in both:
                    for j in range(2):
                        tm = PE.put(lambda e: e.matmul(p[:, s0:s0 + sn], ones[:, :], Y[:, 4 + j, s0:s0 + sn],
                                                       start=(j == 0), stop=(j == 1)))
                for j in range(2):
                    td = DVE.put(lambda e: e.scalar_tensor_tensor(Y[:, 4 + j, a:b_], p[:, a:b_], -1.0 / 256,
                                                                  Y[:, 4 + j, a:b_], ALU.mult, ALU.add), tm, conv_tok[4 + j])
                PS.give(i, td)
                conf["ready"] = td

            def conf_norm2():
                ri, r, tr = conf["st"].finish()
                for j in range(2):
                    tn = DVE.put(lambda e: e.scalar_tensor_tensor(Y[:, 4 + j, a:b_], Y[:, 4 + j, a:b_],
                                                                  col[:, LN_G + j:LN_G + j + 1], r[:, a:b_],
                                                                  ALU.mult, ALU.mult), tr)
                    ts = AC.put(lambda e: e.activation(Y[:, 4 + j, a:b_], Y[:, 4 + j, a:b_], ACT.Silu,
                                                       bias=col[:, LN_B + j:LN_B + j + 1]), tn)
                RS.give(ri, tn)
                conf["ready"] = ts

            def branch_scale(c0):
                def go():
                    ri, r, tr = conf["st"].finish()
                    for j in range(2):
                        g = G_BR + c0 + j
                        t = DVE.put(lambda e: e.scalar_tensor_tensor(Y[:, c0 + j, a:b_], Y[:, c0 + j, a:b_], col[:, g:g + 1],
                                                                     r[:, a:b_], ALU.mult, ALU.mult), tr)
                    RS.give(ri, t)
                    conf[c0] = t
                return go

            def square(c):
                def go():
                    if c % 2 == 0:
                        conf["st"] = Stats(2, both, 256)
                    conf["st"].add(Y[:, c, :], conf["ready"] if c < 6 else [conv_tok[6], conv_tok[7]])
                return go

            conf = {}
            background.extend([conf_norm, square(4), square(5), conf_norm2, square(4), square(5), branch_scale(4),
                               square(6), square(7), branch_scale(6)])
            scored, turned = [], []
            coming = None
            for n, u in enumerate(units + [None, None, None]):
                if u is not None:
                    scored.append((u, scores(*u)))
                    if n % per == per - 4 and u[0] + 1 < 8:
                        coming = head_in(u[0] + 1)
                if coming is not None:
                    next(coming, None)
                idle(1)
                if pairs:
                    close_pair()
                if len(scored) > 2 or (u is None and scored):
                    su = scored.pop(0)
                    turned.append((su[0], turn(*su)))
                if len(turned) > 1 or (u is None and turned):
                    values(*turned.pop(0))
                idle(1 if l == 0 else 2)
                if u is None and not background:
                    att_stats.add(Y[:, att_stats.c, :], t_att)
            while turned:
                values(*turned.pop(0))
            idle(len(background))
            while att_stats.c < 3:
                att_stats.add(Y[:, att_stats.c, :], t_att)
            close_pair()
            att_stats.add(Y[:, 3, :], t_att)

            att.close()
            z.close()
            HHs = ExitStack()
            HH, HL = sb(HHs, [128, 8, 768], FR), sb(HHs, [128, 8, 768], FR)
            t_free = [(PE.sem, PE.n), (DVE.sem, DVE.n), (AC.sem, AC.n)]
            t_m = [None] * 8
            for c in range(4, 8):
                for (s0, sn) in both:
                    zz = slice(s0, s0 + sn)
                    th = AC.put(lambda e: e.activation(HH[:, c, zz], Y[:, c, zz], ACT.Copy), conf[4], conf[6], t_free)
                    tl = DVE.put(lambda e: e.tensor_tensor(HL[:, c, zz], Y[:, c, zz], HH[:, c, zz].bitcast(F32), ALU.subtract),
                                 th, t_free)
                t_m[c] = [th, tl]
            t_m[0:4] = norm_split([Y[:, c, :] for c in range(4)], both, att_stats,
                                  lambda c, s0: col[:, G_BR + c:G_BR + c + 1], None, HH, HL, 0, t_free)
            ystats = Stats(8, both, 1024)

            def y_out(c, p, tm, sg):
                t = AC.put(lambda e: e.activation(Y[:, c, a:b_], p[:, a:b_], ACT.Copy), tm, t_m)
                ystats.add(Y[:, c, :], t)
                return [t]

            last = linear(4, 8, 256, both, HH, HL, t_m, y_out, 1, [4, 5, 6, 7, 0, 1, 2, 3])
            now = [(DVE.sem, DVE.n)]
            DVE.wait(scales(l, 1, 2, G_POST, 0.0, now), scales(l, 2, 4, G_PRE2, 1.0, now), scales(l, 3, 5, G_POST2, 0.0, now))
            AC.wait(t_m48[l])
            st = Stats(8, both, 1024)
            t_x1 = add_normed(both, ystats, A_(1), lambda c, ta: st.add(X[:, c, :], ta))
            t_h = norm_split(xs, both, st, A_(2), B_(3), HH, HL, 0, [last])
            mm = ExitStack()
            AH, AL = sb(mm, [128, 4, 768], FR), sb(mm, [128, 4, 768], FR)
            if l == 0:
                extra.extend([lambda s=s: mod_slab(1, s) for s in range(24)])

            def sqrelu(g, c, p, tm, ah, al, afree):
                ti, t, tf = T.take()
                t1 = AC.put(lambda e: e.activation(t[:, a:b_], p[:, a:b_], ACT.Relu), tm, tf)
                t2 = DVE.put(lambda e: e.tensor_tensor(t[:, a:b_], t[:, a:b_], t[:, a:b_], ALU.mult), t1)
                t3 = AC.put(lambda e: e.activation(ah[:, a:b_], t[:, a:b_], ACT.Copy), t2, afree)
                t4 = DVE.put(lambda e: e.tensor_tensor(al[:, a:b_], t[:, a:b_], ah[:, a:b_].bitcast(F32),
                                                       ALU.subtract), t3, afree)
                T.give(ti, t4)
                return t4, [t1]

            ystats = Stats(8, both, 1024)
            yl = mlp(8, both, HH, HL, AH, AL, t_h, sqrelu, [t_x1], ystats, 1)
            next_segs = [LAT, CTX] if l == 0 else [LAT]
            x_stats = Stats(8, next_segs, 1024)
            t_x2 = add_normed(both, ystats, A_(3), lambda c, ta: x_stats.add(X[:, c, :], ta))
            x_ready = [t_x2]
            mm.close()
            HHs.close()
            t_phase = [(PE.sem, PE.n), (DVE.sem, DVE.n), (AC.sem, AC.n)]
        first.close()

        L = [LAT]
        C_N1, C_N2, C_QN, C_KN, C_DQ, C_DK = 0, 8, 16, 17, 20, 23
        second = ExitStack()
        xs = [X[:, c, :] for c in range(8)]
        HHs = ExitStack()
        cosN = sb(second, [128, 512])
        sinN = sb(second, [128, 512])
        rotN = sb(second, [128, 128])
        bones = sb(second, [128, 128])
        t_t2 = [load(PO, cosN[:, :], io["cosN"], "k0", t_phase), load(PO, sinN[:, :], io["sinN"], "k1", t_phase),
                load(PO, rotN[:, :], io["rotN"], "k2", t_phase), load(PO, bones[:, :], io["bones"], "k3", t_phase)]
        HH, HL = sb(HHs, [128, 8, 512], FR), sb(HHs, [128, 8, 512], FR)
        c2 = lambda b0: (lambda c, s0: cols2[:, b0 + c:b0 + c + 1])
        t_h = norm_split(xs, L, x_stats, c2(C_N1), None, HH, HL, 0, t_phase)
        t_c8 = DVE.put(lambda e: e.tensor_scalar(cols2[:, C_QN:C_QN + 1], cols2[:, C_QN:C_QN + 1], 0.125, None, ALU.mult))
        t_c8 = DVE.put(lambda e: e.tensor_scalar(cols2[:, C_DQ:C_DQ + 3], cols2[:, C_DQ:C_DQ + 3], 0.125, None, ALU.mult))

        def head_norm_rope(zsrc, ready, g, n, raw, dsts, cos, sin, free):
            tc = AC.put(lambda e: e.activation(raw, zsrc[:, 0:n], ACT.Copy), ready, free)
            ti, t, tf = T.take()
            tq = AC.put(lambda e: e.activation(t[:, 0:n], zsrc[:, 0:n], ACT.Square), ready, tf)
            yield tq
            i, p, pf = PS.take()
            tm = PE.put(lambda e: e.matmul(p[:, 0:n], bones[:, :], t[:, 0:n], start=True, stop=True), pf, tq, t_t2)
            T.give(ti, tm)
            ri, r, rf = RS.take()
            t1 = AC.put(lambda e: e.activation(r[:, 0:n], p[:, 0:n], ACT.Ln, bias=epsc[:, 0:1], scale=1.0 / 64), tm, rf)
            PS.give(i, t1)
            t2 = AC.put(lambda e: e.activation(r[:, 0:n], r[:, 0:n], ACT.Exp, scale=-0.5), t1)
            t3 = DVE.put(lambda e: e.scalar_tensor_tensor(raw, raw, cols2[:, g:g + 1], r[:, 0:n], ALU.mult, ALU.mult),
                         tc, t2, t_c8)
            yield None
            i, p, pf = PS.take()
            tm = PE.put(lambda e: e.matmul(p[:, 0:n], rotN[:, :], raw, start=True, stop=True), pf, t3, t_t2)
            t4 = DVE.put(lambda e: e.tensor_tensor(r[:, 0:n], p[:, 0:n], sin, ALU.mult), tm, t3)
            PS.give(i, t4)
            t5 = DVE.put(lambda e: e.tensor_tensor(raw, raw, cos, ALU.mult), tm, t3)
            for (r0, r1, ap) in dsts or [(0, 128, raw)]:
                t6 = DVE.put(lambda e: e.tensor_tensor(ap, raw[r0:r1], r[r0:r1, 0:n], ALU.add), t4, t5, t_ms)
            RS.give(ri, t6)
            yield t6

        ropes = []

        def rope_step(gen=None, then=None):
            for it in list(ropes):
                t = next(it[0])
                if t is not None:
                    it[1](t)
                    ropes.remove(it)
            if gen is not None:
                t = next(gen)
                ropes.append((gen, then))
                return t

        def behind(gen):
            def go():
                if next(gen, gen) is not gen:
                    background.insert(0, go)
            background.append(go)

        obs = ExitStack()
        lent, lent_buf, lent_free = T.take()
        OB = Ring([sb(obs, [128, 512])[:, :] for _ in range(2)] + [lent_buf[:, 0:512]])
        OB.free[2] = (2, list(lent_free))

        nsa = ExitStack()
        QN = sb(nsa, [128, 4, 512])
        KS = sb(nsa, [128, 2, 512])
        KW = sb(nsa, [128, 2, 512])
        KCM = sb(nsa, [128, 2, 32])
        VCM = sb(nsa, [128, 128])
        GT = sb(nsa, [128, 4, 24])
        PEt = sb(nsa, [128, 32])
        cosC = sb(nsa, [128, 32])
        sinC = sb(nsa, [128, 32])
        kz = sb(nsa, [128, 32])
        kr = sb(nsa, [128, 32])
        BIG = sb(nsa, [128, 8192])
        W1 = BIG[:, :].rearrange("p (t c) -> p t c", t=32)
        Pb = Ring([BIG[:, 1024 * i:1024 * i + 1024] for i in range(4)])
        PTb = Ring([BIG[:, 4096 + 1024 * i:5120 + 1024 * i] for i in range(2)])
        SL = BIG[:, 6144:7040]
        CM = BIG[:, 7040:7296].rearrange("p (a q c) -> p a q c", a=2, q=4)
        sm = Ring([BIG[:, 7296 + 8 * i:7304 + 8 * i] for i in range(6)])
        cs = Ring([BIG[:, 7360 + 32 * i:7392 + 32 * i].rearrange("p (a b) -> p a b", a=4) for i in range(2)])
        yflat = Y[:, :, :].rearrange("p c t -> p (c t)")
        KVC = yflat[:, 2048:3072].rearrange("p (g t) -> p g t", g=2)
        BLK = yflat[:, 0:2048].rearrange("p (t c) -> p t c", c=64)
        W2 = yflat[:, 3072:3584].rearrange("p (a b c) -> p a b c", a=2, b=2)
        HID = yflat[:, 3584:3840].rearrange("p (a b c) -> p a b c", a=2, b=2)
        VSW = lambda tt: Y[:, 6 + tt // 2, 256 * (tt % 2):256 * (tt % 2) + 256]
        PC = Ring([X[:, :, 512:640]])
        PTC = Ring([X[:, :, 640:768], Y[:, :, 512:640]])
        t_cw = [load(PO, W1, io["cmp_w1"], "q0", t_phase), load(PO, W2, io["cmp_w2"], "q1", t_phase),
                load(PO, PEt[:, :], io["cmp_pe"], "q2", t_phase), load(PO, cosC[:, :], io["cosC"], "q3", t_phase),
                load(PO, sinC[:, :], io["sinC"], "q4", t_phase)]
        t_ms = [DVE.put(lambda e: e.memset(KS[:, :, :], 0.0), t_phase), DVE.put(lambda e: e.memset(KW[:, :, :], 0.0), t_phase),
                DVE.put(lambda e: e.memset(KCM[:, :, :], 0.0), t_phase), DVE.put(lambda e: e.memset(VCM[:, :], 0.0), t_phase)]
        ORD2 = ["kvc0", "kvc1", "q0", "q1", "q2", "q3", "ks", "kw"]
        zt = {}

        def compress():
            for g in range(2):
                for hf in range(2):
                    s = KVC[:, g, 16 * hf:16 * hf + 496].rearrange("p (c t) -> p t c", t=16)
                    pe = PEt[:, 16 * hf:16 * hf + 16].rearrange("p (t c) -> p t c", c=1).broadcast_to([128, 16, 31])
                    t_blk = DVE.put(lambda e: e.tensor_tensor(BLK[:, 16 * hf:16 * hf + 16, 31 * g:31 * g + 31], s, pe,
                                                              ALU.add), zt[f"kvc{g}"], t_cw, t_phase)
            yield
            t_hid = {}
            for kv in range(2):
                rows = slice(64 * kv, 64 * kv + 64)
                i, p, free = PS.take()
                PE.wait(free, t_blk, t_cw)
                for hc in range(2):
                    for tp in range(32):
                        tm = PE.put(lambda e: e.matmul(p[:, 64 * hc:64 * hc + 62], W1[rows, tp, 128 * hc:128 * hc + 128],
                                                       BLK[rows, tp, 0:62], start=(tp == 0), stop=(tp == 31)),
                                    count=(tp == 31))
                t_hid[kv] = AC.put(lambda e: e.activation(HID[:, kv, :, 0:62],
                                                          p[:, 0:128].rearrange("p (a b) -> p a b", a=2)[:, :, 0:62],
                                                          ACT.Gelu_apprx_tanh), tm, t_phase)
                PS.give(i, t_hid[kv])
                yield
            i, p, free = PS.take()
            PE.wait(free, t_hid[0], t_cw)
            for hc in range(2):
                tm = PE.put(lambda e: e.matmul(p[:, 0:62], W2[:, 0, hc, :], HID[:, 0, hc, 0:62], start=(hc == 0),
                                               stop=(hc == 1)))
            ta = AC.put(lambda e: e.activation(kz[0:64, 0:31], p[0:64, 0:31], ACT.Copy), tm, t_phase)
            tb = AC.put(lambda e: e.activation(kz[64:128, 0:31], p[64:128, 31:62], ACT.Copy), tm, t_phase)
            PS.give(i, tb)
            i, p, free = PS.take()
            PE.wait(free, t_hid[1], t_cw)
            for g in range(2):
                for hc in range(2):
                    tm = PE.put(lambda e: e.matmul(p[0:31, 64 * g:64 * g + 64], HID[:, 1, hc, 31 * g:31 * g + 31],
                                                   W2[:, 1, hc, 0:64], start=(hc == 0), stop=(hc == 1)))
            zt["vcm"] = AC.put(lambda e: e.activation(VCM[0:31, :], p[0:31, 0:128], ACT.Copy), tm, t_ms)
            PS.give(i, zt["vcm"])
            yield
            steps = head_norm_rope(kz, [ta, tb], C_KN, 31, kr[:, 0:31],
                                   [(0, 64, KCM[0:64, 0, 0:31]), (64, 128, KCM[64:128, 1, 0:31])],
                                   cosC[:, 0:31], sinC[:, 0:31], t_phase)
            next(steps)
            yield
            next(steps)
            yield
            zt["kcm"] = next(steps)

        def z2(c, p, tm, sg):
            kind = ORD2[c]
            if kind[0:3] == "kvc":
                j = int(kind[3])
                zt[kind] = AC.put(lambda e: e.activation(KVC[:, j, :], p[:, 0:512], ACT.Copy), tm, t_phase)
                return [zt[kind]]
            if kind[0] == "q":
                j = int(kind[1])
                t1 = rope_step(head_norm_rope(p, [tm], C_QN, 512, QN[:, j, :], [], cosN[:, :], sinN[:, :], t_phase),
                               lambda t: zt.__setitem__(kind, t))
                if j == 3:
                    behind(compress())
                return [t1]
            dst = KS if kind == "ks" else KW
            oi, ob, of = OB.take()

            def then(t):
                zt[kind] = t
                OB.give(oi, t)
            return [rope_step(head_norm_rope(p, [tm], C_KN + (1 if kind == "ks" else 2), 512, ob,
                                             [(0, 64, dst[0:64, 0, :]), (64, 128, dst[64:128, 1, :])],
                                             cosN[:, :], sinN[:, :], of), then)]

        linear(4, 8, 256, L, HH, HL, t_h, z2, 0, list(range(8)))

        def token_major(slab, w0, w, ncol, tiles, emit):
            k, wh, wl, wr = slab
            wh = wh[:, 0:8 * ncol].rearrange("p (k n) -> p k n", k=8)
            wl = wl[:, 0:8 * ncol].rearrange("p (k n) -> p k n", k=8)
            for tt, tok in enumerate(tiles):
                i, p, free = PS.take()
                PE.wait(free, wr, t_h)
                for kk in range(8):
                    last = three(p[:, 0:w], HH[:, kk, tok], HL[:, kk, tok], wh[:, kk, w0:w0 + w], wl[:, kk, w0:w0 + w],
                                 kk == 0, kk == 7)
                PS.give(i, *emit(tt, p, last))
                idle()
            return last

        nat = [slice(128 * i, 128 * i + 128) for i in range(4)]
        strided = [slice(a, 512, 4) for a in range(4)]
        zv = []

        def v_out(tt, p, tm):
            rope_step()
            zv.append(AC.put(lambda e: e.activation(VSW(tt), p[:, 0:256], ACT.Copy), tm, t_phase))
            return [zv[-1]]

        def g_out(tt, p, tm):
            zv.append(AC.put(lambda e: e.activation(GT[:, tt, :], p[:, 0:24], ACT.Sigmoid), tm, t_phase))
            return [zv[-1]]

        slab = take_slab()
        give_slab(slab[0], token_major(slab, 0, 256, 256, nat, v_out))
        slab = take_slab()
        give_slab(slab[0], token_major(slab, 0, 24, 24, nat, g_out))
        while background:
            idle()
        t_cmp = [(PE.sem, PE.n), zt["vcm"], zt["kcm"]]
        t_mk = [load(PO, CM, io["cmask"], "q0", t_cmp), load(PO, SL, io["slide"], "q1", t_cmp)]
        t_pc0 = DVE.put(lambda e: e.memset(PC.bufs[0], 0.0), t_phase)
        t_yn = []
        ptc_of = {}
        nsa_state = {}

        def block_scores(qt):
            qs = slice(128 * qt, 128 * qt + 128)
            i, p, free = PS.take()
            PE.wait(free, zt["q3"], zt["kcm"], zt["kw"])
            for h in range(8):
                tm = PE.put(lambda e: e.matmul(p[:, 32 * h:32 * h + 32], QN[:, h % 4, qs], KCM[:, h // 4, :],
                                               start=True, stop=True), count=(h == 7))
            pi, pc, pcf = PC.take()
            ci, cst, cf = cs.take()
            pcv = pc[:, :, 0:31]
            pv3 = p[:, 0:256].rearrange("p (h c) -> p h c", h=8)[:, :, 0:31]
            msk = CM[:, 0, qt, 0:31].rearrange("p (o c) -> p o c", o=1).broadcast_to([128, 8, 31])
            val = CM[:, 1, qt, 0:31].rearrange("p (o c) -> p o c", o=1).broadcast_to([128, 8, 31])
            vec = lambda j: cst[:, j, :].rearrange("p (h o) -> p h o", o=1)
            b8 = lambda j: vec(j).broadcast_to([128, 8, 31])
            t1 = DVE.put(lambda e: e.tensor_tensor(pcv, pv3, msk, ALU.add), tm, pcf, t_mk, t_pc0)
            PS.give(i, t1)
            t2 = DVE.put(lambda e: e.tensor_reduce(cst[:, 0, :], pcv, AX.X, ALU.max), t1, cf, t_cmp)
            t3 = DVE.put(lambda e: e.tensor_tensor(pcv, pcv, b8(0), ALU.subtract), t2)
            t4 = AC.put(lambda e: e.activation(pcv, pcv, ACT.Exp), t3)
            t5 = DVE.put(lambda e: e.tensor_reduce(cst[:, 1, :], pcv, AX.X, ALU.add), t4)
            t6 = DVE.put(lambda e: e.reciprocal(cst[:, 2, :], cst[:, 1, :]), t5)
            gates = GT[:, qt, :].rearrange("p (h b) -> p h b", b=3)
            t7 = DVE.put(lambda e: e.tensor_tensor(cst[:, 3, :], cst[:, 2, :], gates[:, :, 0], ALU.mult), t6, zv)
            t8 = DVE.put(lambda e: e.tensor_tensor(pcv, pcv, b8(3), ALU.mult), t7)
            t9 = DVE.put(lambda e: e.tensor_tensor(pcv, pcv, val, ALU.mult), t8)
            cs.give(ci, t9)
            nsa_state[qt] = (pi, pc, t9)

        def block_turn(qt):
            pi, pc, t9 = nsa_state.pop(qt)
            i, p, free = PS.take()
            PE.wait(free, t9)
            for h in range(8):
                tm = PE.put(lambda e: e.transpose(p[:, 128 * h:128 * h + 128], pc[:, h, :], ident[:, :]), count=(h == 7))
            PC.give(pi, tm)
            ti, ptc, tf = PTC.take()
            t = AC.put(lambda e: e.activation(ptc, p[:, :].rearrange("p (h q) -> p h q", h=8), ACT.Copy), tm, tf,
                       t_phase, t_cmp)
            PS.give(i, t)
            ptc_of[qt] = (ti, ptc, t)

        def nsa_scores(qt, h):
            g, c = h // 4, h % 4
            qs = slice(128 * qt, 128 * qt + 128)
            Lk = 128 * (qt + 1)
            i, p, free = PS.take()
            PE.wait(free, zt["q3"], zt["ks"], zt["kw"])
            for j, kk in enumerate((KS, KW)):
                tm = PE.put(lambda e: e.matmul(p[:, 512 * j:512 * j + Lk], QN[:, c, qs], kk[:, g, 0:Lk],
                                               start=True, stop=True))
            pi, pb, pf = Pb.take()
            mi, m, mf = sm.take()
            off = 384 - 128 * qt
            for j in range(2):
                pp = pb[:, Lk * j:Lk * j + Lk]
                t1 = DVE.put(lambda e: e.tensor_tensor_reduce(pp, p[:, 512 * j:512 * j + Lk], SL[:, off:off + Lk], 1.0,
                                                              -3e38, ALU.add, ALU.max, m[:, j:j + 1]),
                             tm, pf, mf, t_mk, t_cmp)
            t1 = DVE.put(lambda e: e.tensor_scalar(m[:, 2:4], m[:, 0:2], -1.0, None, ALU.mult), t1)
            PS.give(i, t1)
            for j in range(2):
                pp = pb[:, Lk * j:Lk * j + Lk]
                t2 = AC.put(lambda e: e.activation(pp, pp, ACT.Exp, bias=m[:, 2 + j:3 + j], accum_out=m[:, 4 + j:5 + j]),
                            t1)
            t3 = DVE.put(lambda e: e.reciprocal(m[:, 6:8], m[:, 4:6]), t2)
            t4 = DVE.put(lambda e: e.tensor_tensor(m[:, 6:8], m[:, 6:8], GT[:, qt, 3 * h + 1:3 * h + 3], ALU.mult), t3, zv)
            for j in range(2):
                pp = pb[:, Lk * j:Lk * j + Lk]
                t5 = DVE.put(lambda e: e.tensor_scalar(pp, pp, m[:, 6 + j:7 + j], None, ALU.mult), t4)
            sm.give(mi, t5)
            return qt, h, pi, pb, t5

        def nsa_turn(qt, h, pi, pb, tp):
            nb = qt + 1
            i, p, free = PS.take()
            PE.wait(free, tp)
            for b in range(2 * nb):
                tt = PE.put(lambda e: e.transpose(p[:, 128 * b:128 * b + 128], pb[:, 128 * b:128 * b + 128], ident[:, :]),
                            count=(b == 2 * nb - 1))
            Pb.give(pi, tt)
            ti2, ptb, ptf = PTb.take()
            tc = AC.put(lambda e: e.activation(ptb[:, 0:256 * nb], p[:, 0:256 * nb], ACT.Copy), tt, ptf, t_cmp)
            PS.give(i, tc)
            return qt, h, ti2, ptb, tc

        def nsa_values(qt, h, ti2, ptb, tc):
            g, c = h // 4, h % 4
            nb = qt + 1
            qs = slice(128 * qt, 128 * qt + 128)
            ci, ptc, t_ptc = ptc_of[qt]
            oi, o, of = PS.take()
            PE.wait(of, t_ptc, zt["vcm"], zv)
            oo = o[:, 0:128]
            PE.put(lambda e: e.matmul(oo, VCM[:, :], ptc[:, h, :], start=True, stop=False), count=False)
            PE.wait(tc)
            for j in range(2):
                for b in range(nb):
                    end = j == 1 and b == nb - 1
                    tv = PE.put(lambda e: e.matmul(oo, VSW(b)[:, 128 * j:128 * j + 128],
                                                   ptb[:, 128 * (nb * j + b):128 * (nb * j + b) + 128],
                                                   start=False, stop=end), count=end)
            PTb.give(ti2, tv)
            if h == 7:
                PTC.give(ci, tv)
            r0 = 64 * g
            ty = AC.put(lambda e: e.activation(Y[r0:r0 + 64, c, qs], o[r0:r0 + 64, 0:128], ACT.Copy), tv, t_phase)
            PS.give(oi, ty)
            t_yn.append(ty)

        def nsa_attention():
            block_scores(0)
            yield
            scored, turned = [], []
            units = [(qt, h) for qt in range(4) for h in range(8)]
            for n, (qt, h) in enumerate(units):
                if len(scored) == 2:
                    turned.append(nsa_turn(*scored.pop(0)))
                scored.append(nsa_scores(qt, h))
                if len(turned) == 2:
                    nsa_values(*turned.pop(0))
                if n == 0:
                    block_turn(0)
                if h == 3 and qt < 3:
                    block_scores(qt + 1)
                if h == 5 and qt < 3:
                    block_turn(qt + 1)
                yield
            while scored or turned:
                if scored:
                    turned.append(nsa_turn(*scored.pop(0)))
                nsa_values(*turned.pop(0))
                yield

        behind(nsa_attention())

        t_dq, t_dv = {}, {}
        for hp in range(2):
            def d_out(c, p, tm, sg):
                g, isk = c // 2, c % 2
                oi, ob, of = OB.take()

                def then(t):
                    t_dq[hp, isk, g] = load(PO, io["dqk"][hp, isk, g], ob, f"ob{oi}", t)
                    OB.give(oi, t_dq[hp, isk, g])
                t1 = rope_step(head_norm_rope(p, [tm], (C_DK if isk else C_DQ) + g, 512, ob, [], cosN[:, :], sinN[:, :], of),
                               then)
                if c != 5:
                    idle()
                return [t1]

            linear(3, 8, 256, L, HH, HL, t_h, d_out)
            for g, tiles in ((0, nat), (1, strided), (2, strided)):
                if g != 1:
                    slab = take_slab()
                for _ in range(2 * (g == 0)):
                    rope_step()
                oi, ob, of = OB.take()

                def dv_out(tt, p, tm):
                    rope_step()
                    t = AC.put(lambda e: e.activation(ob[:, 128 * tt:128 * tt + 128], p[:, 0:128], ACT.Copy), tm, of)
                    if tt == 3:
                        t_dv[hp, g] = load(PO, io["dv"][hp, g], ob, f"ob{oi}", t)
                        OB.give(oi, t_dv[hp, g])
                    return [t]

                tl = token_major(slab, 128 * (g % 2), 128, 256 if g < 2 else 128, tiles, dv_out)
                if g != 0:
                    give_slab(slab[0], tl)
        while background:
            idle()
        nsa.close()

        dil = ExitStack()
        t_free = [(PE.sem, PE.n), (DVE.sem, DVE.n), (AC.sem, AC.n)]
        QDs = [sb(dil, [128, 3, 512]) for _ in range(2)]
        KDs = [sb(dil, [128, 3, 2, 512]) for _ in range(2)]
        VDs = [X[:, :, 512:768], Y[:, :, 512:768]]
        MK = sb(dil, [128, 4, 512])
        MKs = sb(dil, [128, 256])
        T.give(lent, *[t for f in OB.free if f[0] == 2 for t in f[1]])
        Pb, PTb = T, RS
        sm = Ring([sb(dil, [128, 4]) for _ in range(4)])
        t_mk = [load(PO, MK[:, :, :], io["dmask"][:, :, 0:512], "q0", t_free),
                load(PO, MKs[:, :], io["dmask"][:, 0, 512:768], "q1", t_free)]
        t_din = []
        for hp in range(2):
            t_ms = DVE.put(lambda e: e.memset(KDs[hp][:, :, :, :], 0.0), t_free)
            dq = [t_dq[hp, i, g] for i in range(2) for g in range(3)]
            qt_ = load(PO, QDs[hp][:, :, :], io["dqk"][hp, 0].rearrange("g p t -> p g t"), f"dq{hp}", t_free, dq)
            ks_ = [load(PO, KDs[hp][64 * j:64 * j + 64, :, j, :],
                        io["dqk"][hp, 1, :, 64 * j:64 * j + 64, :].rearrange("g p t -> p g t"), f"dk{hp}{j}", t_ms)
                   for j in range(2)]
            vs_ = [load(PO, VDs[hp][:, 2 * g:2 * g + 2, :], io["dv"][hp, g].rearrange("p (r c) -> p r c", r=2),
                        f"dv{hp}{g}", t_free, t_dv[hp, g]) for g in range(3)]
            t_din.append([qt_] + ks_ + vs_ + [t_ms])
        t_yd = []

        def d_scores(hp, a, j):
            QD, KD = QDs[hp], KDs[hp]
            i, p, free = PS.take()
            PE.wait(free, t_din[hp])
            for g in range(3):
                o = p[:, 0:512] if g == 0 else p[:, 384 + 128 * g:512 + 128 * g]
                kk = KD[:, g, j, :] if g == 0 else KD[:, g, j, strided[a]]
                tm = PE.put(lambda e: e.matmul(o, QD[:, g, strided[a]], kk, start=True, stop=True), count=(g == 2))
            pi, pb, pf = Pb.take()
            mi, m, mf = sm.take()
            t0 = DVE.put(lambda e: e.tensor_tensor_reduce(pb[:, 0:512], p[:, 0:512], MK[:, a, :], 1.0, -3e38, ALU.add,
                                                          ALU.max, m[:, 0:1]), tm, pf, mf, t_mk, t_free)
            t1 = DVE.put(lambda e: e.tensor_tensor_reduce(pb[:, 512:768], p[:, 512:768], MKs[:, :], 1.0, -3e38, ALU.add,
                                                          ALU.max, m[:, 1:2]), tm, pf, mf, t_mk)
            PS.give(i, t1)
            t2 = DVE.put(lambda e: e.tensor_scalar(m[:, 3:4], m[:, 0:1], m[:, 1:2], -1.0, ALU.max, ALU.mult), t0, t1)
            t3 = AC.put(lambda e: e.activation(pb[:, :], pb[:, :], ACT.Exp, bias=m[:, 3:4], accum_out=m[:, 1:2]), t2, t1)
            t4 = DVE.put(lambda e: e.reciprocal(m[:, 2:3], m[:, 1:2]), t3)
            t5 = DVE.put(lambda e: e.tensor_scalar(pb[:, :], pb[:, :], m[:, 2:3], None, ALU.mult), t4)
            sm.give(mi, t5)
            return hp, a, j, pi, pb, t5

        def d_turn(hp, a, j, pi, pb, tp):
            i, p, free = PS.take()
            PE.wait(free, tp)
            for b in range(6):
                tt = PE.put(lambda e: e.transpose(p[:, 128 * b:128 * b + 128], pb[:, 128 * b:128 * b + 128], ident[:, :]),
                            count=(b == 5))
            Pb.give(pi, tt)
            ti, ptb, ptf = PTb.take()
            tc = AC.put(lambda e: e.activation(ptb[:, :], p[:, 0:768], ACT.Copy), tt, ptf, t_free)
            PS.give(i, tc)
            return hp, a, j, ti, ptb, tc

        def d_values(hp, a, j, ti, ptb, tc):
            oi, o, of = PS.take()
            PE.wait(of, tc, t_din[hp])
            for b in range(6):
                v = b if b < 4 else 4 * (b - 3) + a
                vv = VDs[hp][:, v // 2, 128 * (v % 2):128 * (v % 2) + 128]
                tv = PE.put(lambda e: e.matmul(o[:, 0:128], vv, ptb[:, 128 * b:128 * b + 128], start=(b == 0), stop=(b == 5)),
                            count=(b == 5))
            PTb.give(ti, tv)
            r0 = 64 * j
            ty = AC.put(lambda e: e.activation(Y[r0:r0 + 64, 4 + hp, strided[a]], o[r0:r0 + 64, 0:128], ACT.Copy), tv, t_free)
            PS.give(oi, ty)
            t_yd.append(ty)

        def dilated_attention():
            scored, turned = [], []
            for hp in range(2):
                for a in range(4):
                    for j in range(2):
                        if len(scored) == 2:
                            turned.append(d_turn(*scored.pop(0)))
                        scored.append(d_scores(hp, a, j))
                        if len(turned) == 2:
                            d_values(*turned.pop(0))
                        yield
            while scored or turned:
                if scored:
                    turned.append(d_turn(*scored.pop(0)))
                d_values(*turned.pop(0))
                yield

        t_mgd = {}
        OBm = Ring(OB.bufs[0:2])
        OBm.free = [f for f in OB.free if f[0] < 2]

        def mg_out(c, p, tm, sg):
            oi, ob, of = OBm.take()
            t = AC.put(lambda e: e.activation(ob, p[:, 0:512], ACT.Sigmoid), tm, of)
            t_mgd[c] = load(PO, io["mgd"][c], ob, f"ob{oi}", t)
            OBm.give(oi, t_mgd[c])
            if c == 3:
                behind(dilated_attention())
            if c > 9:
                idle()
            return [t]

        last = linear(8, 8, 256, L, HH, HL, t_h, mg_out)
        while background:
            idle()
        dil.close()
        obs.close()

        t_free = [(PE.sem, PE.n), (DVE.sem, DVE.n), (AC.sem, AC.n), t_mgd[14], t_mgd[15]]
        mg = ExitStack()
        YH, YL = sb(mg, [128, 6, 512], FR), sb(mg, [128, 6, 512], FR)
        UP = sb(mg, [128, 8, 512])
        GR = Ring([sb(mg, [128, 512]) for _ in range(4)])
        gates_in = {}

        def gate_in(n):
            if n < 16:
                gi, gb, gf = GR.take()
                gates_in[n] = (gi, gb, load(PO, gb[:, :], io["mgd"][n], f"gi{gi}", t_free, gf, t_mgd[n]))

        for n in range(4):
            gate_in(n)
        t_y = []
        for c in range(6):
            th = AC.put(lambda e: e.activation(YH[:, c, :], Y[:, c, 0:512], ACT.Copy), t_yn, t_yd, t_free)
            tl = DVE.put(lambda e: e.tensor_tensor(YL[:, c, :], Y[:, c, 0:512], YH[:, c, :].bitcast(F32), ALU.subtract), th, t_free)
            t_y.append([th, tl])
        ups = []
        t_m = []

        def up_nsa(c, p, tm, sg):
            gi, gb, tg = gates_in[c]
            t = DVE.put(lambda e: e.tensor_tensor(UP[:, c, :], p[:, 0:512], gb[:, :], ALU.mult), tm, tg, t_free)
            GR.give(gi, t)
            gate_in(c + 4)
            ups.append(t)
            return [t]

        def up_dil(c, p, tm, sg):
            gi, gb, tg = gates_in[8 + c]
            t1 = DVE.put(lambda e: e.tensor_tensor(gb[:, :], p[:, 0:512], gb[:, :], ALU.mult), tm, tg)
            t2 = DVE.put(lambda e: e.tensor_tensor(UP[:, c, :], UP[:, c, :], gb[:, :], ALU.add), t1, ups[c])
            GR.give(gi, t2)
            gate_in(c + 12)
            th = AC.put(lambda e: e.activation(HH[:, c, :], UP[:, c, :], ACT.Copy), t2, last)
            late_m.append((c, th))
            if c > 0:
                low_m()
            return [t1]

        late_m = []

        def low_m():
            c, th = late_m.pop(0)
            tl = DVE.put(lambda e: e.tensor_tensor(HL[:, c, :], UP[:, c, :], HH[:, c, :].bitcast(F32), ALU.subtract), th, last)
            t_m.append([th, tl])

        linear(2, 4, 512, L, YH, YL, t_y, up_nsa)
        linear(1, 2, 1024, L, YH[:, 4:6, :], YL[:, 4:6, :], t_y[4:6], up_dil)
        low_m()
        t_xx = []
        st = Stats(8, L, 1024)

        def x_out(c, p, tm, sg):
            t = DVE.put(lambda e: e.tensor_tensor(X[:, c, 0:512], X[:, c, 0:512], p[:, 0:512], ALU.add), tm)
            t_xx.append(t)
            st.add(X[:, c, :], t)
            return [t]

        last = linear(4, 8, 256, L, HH, HL, t_m, x_out)
        mg.close()

        t_h = norm_split(xs, L, st, c2(C_N2), None, HH, HL, 0, [last])
        t_free = [(PE.sem, PE.n), (DVE.sem, DVE.n), (AC.sem, AC.n)]
        gs = ExitStack()
        GR1 = sb(gs, [128, 16, 4, 32])
        pr = ExitStack()
        E1, E2, GG = (b[:, 0:512] for b in T.bufs)
        IO = sb(pr, [128, 128])
        QP = sb(pr, [128, 8, 512])
        SK = sb(pr, [128, 256])
        GA = Ring([GR1[:, :, :, :].rearrange("p b c t -> p (b c t)").rearrange("p (c t) -> p c t", c=4)])
        GST = Ring([sb(pr, [128, 128, 32]) for _ in range(1)])
        M1 = RS.bufs[1][:, 0:256].rearrange("p (a b) -> p a b", a=16)
        I1 = sb(pr, [128, 16, 16], U32)
        F1 = RS.bufs[1][:, 256:512].rearrange("p (a b) -> p a b", a=16)
        M2 = RS.bufs[1][:, 512:640].rearrange("p (a b) -> p a b", a=8)
        I2 = sb(pr, [128, 8, 16], U32)
        AB2 = sb(pr, [128, 2, 128], U32)
        AF = sb(pr, [128, 2, 128])
        EE = RS.bufs[0][:, 0:384].rearrange("p (a b) -> p a b", a=3)
        sg_ = sb(pr, [128, 2, 8])
        SX = X[:, :, 512:768].rearrange("p c (j n) -> p c j n", j=2)
        yf = Y[:, :, :].rearrange("p c t -> p (c t)")
        S2 = yf[:, 0:2048]
        CAND = yf[:, 2048:4096].rearrange("p (h a b) -> p h a b", h=8, a=16)
        OH = Ring([sb(pr, [128, 2, 8, 128]), yf[:, 4096:6144].rearrange("p (c t n) -> p c t n", c=2, t=8)])
        t_io = load(PO, IO[:, :], io["iota"], "q0", t_free)
        t_sk = load(PO, SK[:, :], io["subk"], "q1", t_free)
        tq = []

        def q_out(c, p, tm, sg):
            t = AC.put(lambda e: e.activation(QP[:, c, :], p[:, 0:512], ACT.Copy), tm, t_free)
            tq.append(t)
            return [t]

        linear(4, 8, 256, L, HH, HL, t_h, q_out, 0, list(range(8)))
        tok_S, tok_E, tok_M = [None], [None], [None]
        e_ready = {}

        def choose(tt):
            ts = slice(128 * tt, 128 * tt + 128)
            tS = []
            for hf in range(2):
                i, p, free = PS.take()
                PE.wait(free, tq, t_sk)
                for h in range(4):
                    tm = PE.put(lambda e: e.matmul(p[:, 256 * h:256 * h + 256], QP[:, 4 * hf + h, ts], SK[:, :],
                                                   start=True, stop=True), count=(h == 3))
                tS.append(AC.put(lambda e: e.activation(X[:, 4 * hf:4 * hf + 4, 512:768],
                                                        p[:, :].rearrange("p (a b) -> p a b", a=4), ACT.Copy),
                                 tm, tok_S[0], t_free))
                PS.give(i, tS[-1])
            yield

            def top16(src, tmp, mx, ix, after):
                ta = DVE.put(lambda e: e.max(mx[:, 0:8], src), after)
                DVE.put(lambda e: e.max_index(ix[:, 0:8], mx[:, 0:8], src), ta)
                tc = DVE.put(lambda e: e.match_replace(tmp, mx[:, 0:8], src, -3e38), ta)
                td = DVE.put(lambda e: e.max(mx[:, 8:16], tmp), tc)
                return DVE.put(lambda e: e.max_index(ix[:, 8:16], mx[:, 8:16], tmp), td)

            for j in range(16):
                t1 = top16(SX[:, j // 2, j % 2, :], S2[:, 128 * j:128 * j + 128], M1[:, j, :], I1[:, j, :], [tS, tok_M[0], t_free])
                if j % 2 == 1:
                    yield
            tok_S[0] = t1
            for h in range(8):
                sa = M1[:, 2 * h, :].rearrange("p (k o) -> p k o", o=1).broadcast_to([128, 16, 16])
                sbb = M1[:, 2 * h + 1, :].rearrange("p (o k) -> p o k", o=1).broadcast_to([128, 16, 16])
                t2 = DVE.put(lambda e: e.tensor_tensor(CAND[:, h, :, :], sa, sbb, ALU.add), t1)
                t3 = top16(CAND[:, h, :, :].rearrange("p a b -> p (a b)"), S2[:, 256 * h:256 * h + 256], M2[:, h, :],
                           I2[:, h, :], [t2])
                yield
            vec = lambda j: sg_[:, j, :].rearrange("p (h o) -> p h o", o=1).broadcast_to([128, 8, 16])
            gv = EE[:, 2, :].rearrange("p (h k) -> p h k", h=8)
            t4 = DVE.put(lambda e: e.tensor_tensor(gv, M2[:, :, :], M2[:, :, 0:1].broadcast_to([128, 8, 16]), ALU.subtract),
                         t3, tok_E[0])
            t5 = AC.put(lambda e: e.activation(gv, gv, ACT.Exp), t4)
            ix = I2[:, :, :].rearrange("p h k -> p (h k)")
            t9 = DVE.put(lambda e: e.tensor_scalar(AB2[:, 0, :], ix, 4, None, ALU.logical_shift_right), t3)
            t10 = DVE.put(lambda e: e.tensor_scalar(AB2[:, 1, :], ix, 15, None, ALU.bitwise_and), t3)
            t11 = DVE.put(lambda e: e.tensor_copy(AF[:, :, :], AB2[:, :, :]), t9, t10)
            t12 = DVE.put(lambda e: e.tensor_copy(F1[:, :, :], I1[:, :, :]), t1, t11)
            t6 = DVE.put(lambda e: e.tensor_reduce(sg_[:, 0, :], gv, AX.X, ALU.add), t5)
            t7 = DVE.put(lambda e: e.reciprocal(sg_[:, 1, :], sg_[:, 0, :]), t6)
            t8 = DVE.put(lambda e: e.tensor_tensor(gv, gv, vec(1), ALU.mult), t7)
            yield
            for c in range(2):
                cm = CAND[:, :, :, :].rearrange("p h a b -> p (h a) b")
                t13 = DVE.put(lambda e: e.tensor_tensor(
                    cm, AF[:, c, :].rearrange("p (k o) -> p k o", o=1).broadcast_to([128, 128, 16]),
                    IO[:, 0:16].rearrange("p (o k) -> p o k", o=1).broadcast_to([128, 128, 16]), ALU.is_equal), t12, t_io)
                yield
                for h in range(8):
                    t14 = DVE.put(lambda e: e.tensor_tensor(
                        CAND[:, h, :, :], CAND[:, h, :, :],
                        F1[:, 2 * h + c, :].rearrange("p (o k) -> p o k", o=1).broadcast_to([128, 16, 16]), ALU.mult), t13)
                t12 = DVE.put(lambda e: e.tensor_reduce(EE[:, c, :], cm, AX.X, ALU.add), t14, tok_E[0])
                yield
            tok_M[0] = t12
            i, p, free = PS.take()
            PE.wait(free, t12, t8)
            for c in range(3):
                tm = PE.put(lambda e: e.transpose(p[:, 128 * c:128 * c + 128], EE[:, c, :], ident[:, :]), count=(c == 2))
            for c, dst in enumerate((E1, E2, GG)):
                te = AC.put(lambda e: e.activation(dst[:, ts], p[:, 128 * c:128 * c + 128], ACT.Copy), tm, t_free)
            PS.give(i, te)
            tok_E[0] = tm
            e_ready[tt] = te

        t_gw = []

        def spread(tt):
            late = []

            def finish():
                b, oi, oh, tb = late.pop(0)
                if b % 4 == 0:
                    cur_st.append(GST.take())
                gi, gst, gf = cur_st[-1]
                i, p, free = PS.take()
                PE.wait(free, tb)
                for t in range(8):
                    tm = PE.put(lambda e: e.matmul(p[:, 128 * t:128 * t + 128], oh[:, 1, t, :], oh[:, 0, t, :],
                                                   start=True, stop=True), count=(t == 7))
                OH.give(oi, tm)
                o8 = b % 4
                tg = AC.put(lambda e: e.activation(gst[:, :, 8 * o8:8 * o8 + 8].rearrange("p n t -> p t n"),
                                                   p[:, :].rearrange("p (t n) -> p t n", t=8), ACT.Copy), tm, gf, t_free)
                PS.give(i, tg)
                if o8 == 3:
                    blk = 4 * tt + b // 4
                    tw = [load(eng, io["gdram"][blk, nn].rearrange("n p c -> p n c"),
                               gst[:, :, :].rearrange("p (n c) t -> p n (c t)", n=32)[:, nn], name, tg)
                          for eng, nn, name in ((PO, slice(0, 16), "g0"), (SP, slice(16, 32), "g1"))]
                    GST.give(gi, tw)
                    t_gw.append(tw)

            cur_st = []
            for b in range(16):
                oi, oh, of = OH.take()
                DVE.wait(of, e_ready[tt], t_io, t_free)
                PO.wait(of, e_ready[tt], t_io, t_free)
                for t in range(8):
                    tok = 128 * tt + 8 * b + t
                    ta = DVE.put(lambda e: e.tensor_scalar(oh[:, 0, t, :], IO[:, :], E1[:, tok:tok + 1], GG[:, tok:tok + 1],
                                                           ALU.is_equal, ALU.mult), count=(t == 7))
                    tb = PO.put(lambda e: e.tensor_scalar(oh[:, 1, t, :], IO[:, :], E2[:, tok:tok + 1], None, ALU.is_equal),
                                count=(t == 7))
                late.append((b, oi, oh, [ta, tb]))
                yield
                if len(late) > 1:
                    finish()
            finish()

        def steps(gens):
            live = list(gens)

            def go():
                for g in list(live):
                    if next(g, live) is live:
                        live.remove(g)
                return live
            return go

        phases = [[choose(0)], [spread(0), choose(1)], [spread(1), choose(2)], [spread(2), choose(3)], [spread(3)]]
        runner = [None]

        def route():
            if runner[0] is None:
                if not phases:
                    return
                runner[0] = steps(phases.pop(0))
            if not runner[0]():
                runner[0] = None

        t_aw = {}
        t_pr = t_free
        cur_ga = [None]

        def pre(g):
            def emit(c, p, tm, sg):
                if c == 0:
                    cur_ga[0] = GA.take()
                gi, ga, gf = cur_ga[0]
                t = AC.put(lambda e: e.activation(ga[:, c, :], p[:, 0:512], ACT.Gelu_apprx_tanh), tm, gf, t_pr)
                if c == 3:
                    t_aw[g] = load(SP, io["adram"][g], ga.rearrange("p c t -> p (c t)"), "aw", t)
                    GA.give(gi, t_aw[g])
                route()
                if c == 3:
                    route()
                return [t]
            return emit

        for g in range(NPRE - 1):
            linear(2, 8, 256, L, HH, HL, t_h, pre(g))
        while phases or runner[0] is not None:
            route()
        pr.close()
        ex = ExitStack()
        t_free = [(PE.sem, PE.n), (DVE.sem, DVE.n), (AC.sem, AC.n), (PO.sem, PO.n), t_gw[-1]]
        AH = [sb(ex, [128, 4, 512], FR) for _ in range(2)]
        AL = [sb(ex, [128, 4, 512], FR) for _ in range(2)]
        GR = [sb(ex, [128, 16, 4, 32]), GR1]
        AR = [sb(ex, [128, 512]) for _ in range(3)]
        g_free, a_free, h_used = [None, None], [None] * 3, [None, None]
        g_tok, a_tok = {}, {}

        def fetch(g):
            if g < 32:
                g_tok[g] = load(PO, GR[g % 2][:, :, :, :].rearrange("p b c t -> p b (c t)"),
                                io["gdram"][:, g].rearrange("b p c -> p b c"), f"r{g % 2}", t_free, g_free[g % 2], t_aw[NPRE - 1] if g == 1 else None)

        def fetch_a(m):
            if m < 4 * NPRE:
                g, c, k = m // 4, m % 4, m % 3
                a_tok[m] = load(PO, AR[k][:, :], io["adram"][g, :, 512 * c:512 * c + 512], f"s{k}", t_free, a_free[k],
                                t_aw[g])

        ready = {}

        def weigh(g, c, tv, after):
            ah, al = AH[g % 2][:, c, :], AL[g % 2][:, c, :]
            flat = tv.rearrange("p b t -> p (b t)")
            t2 = DVE.put(lambda e: e.tensor_tensor(tv, tv, GR[g % 2][:, :, c, :], ALU.mult), after, g_tok[g])
            t3 = AC.put(lambda e: e.activation(ah, flat, ACT.Copy), t2, h_used[g % 2], t_free)
            late.append((g, c, flat, al, ah, t2, t3))

        late = []

        def weigh_low():
            g, c, flat, al, ah, t2, t3 = late.pop(0)
            t4 = DVE.put(lambda e: e.tensor_tensor(al, flat, ah.bitcast(F32), ALU.subtract), t3, h_used[g % 2], t_free)
            ready.setdefault(g, []).append([t3, t4])
            if c == 3:
                g_free[g % 2] = [t4]
                fetch(g + 2)
            if g < NPRE:
                a_free[(4 * g + c) % 3] = [t4]
                fetch_a(4 * g + c + 3)
            return t4

        def prepare_spilled(g, c):
            if c < 4:
                weigh(g, c, AR[(4 * g + c) % 3][:, :].rearrange("p (b t) -> p b t", b=16), a_tok[4 * g + c])
            if 0 < c <= 4:
                weigh_low()

        def prepare(g):
            def up(c, p, tm, sg):
                ti, t, tf = T.take()
                t1 = AC.put(lambda e: e.activation(t[:, 0:512], p[:, 0:512], ACT.Gelu_apprx_tanh), tm, tf)
                weigh(g, c, t[:, 0:512].rearrange("p (b t) -> p b t", b=16), t1)
                T.give(ti, weigh_low())
                return [t1]

            linear(2, 8, 256, L, HH, HL, t_h, up)

        last_y = [None] * 8
        fetch(0)
        for m in range(3):
            fetch_a(m)
        last_pre = pre(NPRE - 1)

        def pre_and_prepare(c, p, tm, sg):
            t = last_pre(c, p, tm, sg)
            if c == 2:
                for cc in range(5):
                    prepare_spilled(0, cc)
            return t

        linear(2, 8, 256, L, HH, HL, t_h, pre_and_prepare)
        fetch(1)
        for g in range(32):
            if g >= NPRE:
                prepare(g)

            def down(c, p, tm, sg):
                if g == 0:
                    t = AC.put(lambda e: e.activation(Y[:, c, 0:512], p[:, 0:512], ACT.Copy), tm, t_free)
                elif g < 31:
                    t = DVE.put(lambda e: e.tensor_tensor(Y[:, c, 0:512], Y[:, c, 0:512], p[:, 0:512], ALU.add),
                                tm, last_y[c])
                else:
                    t = DVE.put(lambda e: e.tensor_tensor(Y[:, c, 0:512], Y[:, c, 0:512], p[:, 0:512], ALU.add),
                                tm, last_y[c])
                    t2 = DVE.put(lambda e: e.tensor_tensor(X[:, c, 0:512], X[:, c, 0:512], Y[:, c, 0:512], ALU.add), t)
                    t_out.append(load(SP, out_d[:, c, :], X[:, c, 0:512], f"o{c % 4}", t2, t_out[-4] if c >= 4 else None))
                last_y[c] = t
                if g + 1 < NPRE:
                    prepare_spilled(g + 1, c)
                return [t]

            t_out = []
            h_used[g % 2] = [linear(2, 4, 512, L, AH[g % 2], AL[g % 2], ready[g], down)]
        SP.wait(t_out)
        ex.close()
        gs.close()
        HHs.close()
        second.close()
        assert cur[0] == len(plan), (cur[0], len(plan))



def slabs(w, kc, ncol):
    k, n = w.shape
    w = w.reshape(k // (128 * kc), kc, 128, n // ncol, ncol)
    return np.ascontiguousarray(w.transpose(0, 3, 2, 1, 4)).reshape(k // (128 * kc), n // ncol, 128, kc * ncol)


def columns(v):
    return np.ascontiguousarray(np.asarray(v).reshape(-1, 128).T)


def tables():
    f = np.float32
    t = np.arange(512)
    inv = (f(1.0) / (f(10000.0) ** (np.arange(0, 16, 2, dtype=f) / f(16)))).astype(f)
    ar, ac = (t // 64).astype(f)[:, None] * inv, (t % 64).astype(f)[:, None] * inv
    ang = np.concatenate([ar, ar, ac, ac], -1).astype(f)
    cosM, sinM = np.ones((96, 512), f), np.zeros((96, 512), f)
    cosM[64:], sinM[64:] = np.cos(ang).T, np.sin(ang).T
    rotM = np.zeros((96, 96), f)
    for o in (64, 80):
        for i in range(8):
            rotM[o + 8 + i, o + i] = -1
            rotM[o + i, o + 8 + i] = 1
    inv2 = (f(500000.0) ** (-(np.arange(8, dtype=f) * f(2.0) / f(16)))).astype(f)

    def rope2(pos):
        a = (pos.astype(f)[:, None] * inv2[None, :]).astype(f)
        c, s = np.ones((128, len(pos)), f), np.zeros((128, len(pos)), f)
        for o in (0, 8, 64, 72):
            c[o:o + 8], s[o:o + 8] = np.cos(a).T, np.sin(a).T
        return c, s

    cosN, sinN = rope2(t)
    end = np.arange(31) * 16 + 31
    cc, ss = rope2(end)
    cosC, sinC = np.ones((128, 32), f), np.zeros((128, 32), f)
    cosC[:, 0:31], sinC[:, 0:31] = cc, ss
    rotN = np.zeros((128, 128), f)
    for o in (0, 64):
        for i in range(8):
            rotN[o + 8 + i, o + i] = -1
            rotN[o + i, o + 8 + i] = 1
    bones = np.zeros((128, 128), f)
    bones[:64, :64] = 1
    bones[64:, 64:] = 1
    valid = end[None, :] <= t[:, None]
    cmask = np.zeros((128, 2, 4, 32), f)
    cmask[:, 0, :, 0:31] = np.where(valid, 0, NEG).reshape(4, 128, 31).transpose(1, 0, 2)
    cmask[:, 1, :, 0:31] = valid.reshape(4, 128, 31).transpose(1, 0, 2)
    p = np.arange(128)
    slide = np.where(np.arange(896)[None, :] <= p[:, None] + 384, 0, NEG).astype(f)
    dmask = np.zeros((128, 4, 768), f)
    for a in range(4):
        q = 4 * p + a
        d = q[:, None] - t[None, :]
        dmask[:, a, 0:512] = np.where((d >= 0) & (d <= 128), 0, NEG)
        d = p[:, None] - p[None, :]
        dmask[:, a, 512:640] = np.where(d >= 0, 0, NEG)
        dmask[:, a, 640:768] = np.where((d >= 0) & (d % 4 == 0), 0, NEG)
    iota = np.tile(np.arange(128, dtype=f), (128, 1))
    return dict(cosM=cosM, sinM=sinM, rotM=rotM, cosN=cosN, sinN=sinN, cosC=cosC, sinC=sinC, rotN=rotN, bones=bones,
                cmask=cmask, slide=slide, dmask=dmask, iota=iota, ident=np.eye(128, dtype=f), ones=np.ones((128, 128), f))


def lay_out(a):
    a = {k: np.asarray(v) for k, v in a.items()}
    f = np.float32
    d = dict(tables())
    rows3 = lambda x: np.ascontiguousarray(x.T.reshape(8, 128, -1).transpose(1, 0, 2))
    d["xT"] = rows3(a["x"][0])
    d["ctxT"] = rows3(a["ctx"][0])
    d["cT"] = np.ascontiguousarray(np.stack([a["c"][0].reshape(8, 128).T, a["c_ctx"].reshape(8, 128).T], -1))
    cols = []
    for l in range(2):
        cw = a["conf_dw_w"][l].reshape(31, 2, 128).transpose(2, 1, 0).reshape(128, 62)
        sw = a["sc_dw_w"][l].reshape(3, 2, 128).transpose(2, 1, 0).reshape(128, 6)
        cols.append(np.concatenate([columns(a[n][l]) for n in ("g_pre_mix", "g_post_mix", "g_pre_mlp", "g_post_mlp", "g_q", "g_kv",
                                                              "conf_dw_b", "conf_ln_g", "conf_ln_b", "g_branch")]
                                   + [cw, sw, columns(a["b_mod"][l])], 1))
    d["cols"] = np.ascontiguousarray(np.stack(cols))
    two = lambda v: np.concatenate([v, v])[:, None]
    c2 = [columns(a["norm1_g_2"]), columns(a["norm2_g_2"]), two(a["nsa_q_norm_2"])]
    c2 += [two(a["nsa_k_norm_2"][i]) for i in range(3)]
    c2 += [two(a["dil_q_norm_2"][i]) for i in range(3)] + [two(a["dil_k_norm_2"][i]) for i in range(3)]
    c2 = np.concatenate(c2, 1)
    d["cols2"] = np.ascontiguousarray(np.concatenate([c2, np.zeros((128, 32 - c2.shape[1]), f)], 1))
    d["w_mod"] = np.stack([slabs(a["w_mod"][l], 8, 256)[0] for l in range(2)])
    w = a["w_in"]
    ch = lambda s: list(range(s, s + 128))
    order = (ch(256) + list(range(320, 416)) + list(range(320, 352)) + ch(0) + ch(128)
             + ch(672) + ch(416) + ch(800) + ch(544)
             + ch(1440) + ch(1184) + ch(1568) + ch(1312) + ch(928) + ch(1056))
    d["w_in"] = np.stack([slabs(w[l][:, order], 8, 256)[0] for l in range(2)])
    d["w_o"] = np.stack([slabs(a["w_o"][l], 8, 256)[0] for l in range(2)])
    d["w1"] = np.stack([slabs(a["w_mlp_in"][l], 8, 256)[0] for l in range(2)])
    d["w2"] = np.stack([slabs(a["w_mlp_out"][l], 4, 512).reshape(16, 128, 2048) for l in range(2)])
    d["w_q_b"] = np.ascontiguousarray(a["w_q_b"].reshape(2, 2, 128, 768).transpose(0, 2, 1, 3))
    d["w_kv_b"] = a["w_kv_b"]
    w = a["w_in_2"]
    half = lambda s: list(range(s, s + 64))
    order = half(512) + half(640) + half(576) + half(704)
    for c in range(4):
        order += half(64 * c) + half(64 * (c + 4))
    order += ch(768) + ch(1024)
    order += ch(896) + ch(1152)
    D0 = 1304
    dil = lambda g, kind, hp: ch(D0 + 768 * g + 256 * kind + 128 * hp)
    heads = slabs(w[:, order], 8, 256)[0]
    d["win2"] = heads
    d["gate2"] = slabs(w[:, 1280:1304], 8, 24)[0, 0]
    for hp in range(2):
        o = []
        for g in range(3):
            o += dil(g, 0, hp) + dil(g, 1, hp)
        d[f"wdqk{hp}"] = slabs(w[:, o], 8, 256)[0]
        d[f"dva{hp}"] = slabs(w[:, dil(0, 2, hp) + dil(1, 2, hp)], 8, 256)[0, 0]
        d[f"dvb{hp}"] = slabs(w[:, dil(2, 2, hp)], 8, 128)[0, 0]
    o = []
    for j in range(16):
        o += ch(3608 + 128 * j)
    d["wmg"] = slabs(w[:, o], 8, 256)[0]
    o = []
    for c in range(4):
        o += half(64 * c) + half(64 * (c + 4))
    d["up_nsa"] = slabs(a["w_up_nsa_2"][o], 4, 512)[0]
    d["up_dil"] = slabs(a["w_up_dil_2"], 2, 1024)[0, 0]
    d["w_o2"] = slabs(a["w_o_2"], 8, 256)[0]
    d["wq2"] = slabs(a["peer_wq_2"], 8, 256)[0]
    d["cmp_w1"] = np.concatenate([a["cmp_w1_k_2"].reshape(32, 64, 256).transpose(1, 0, 2),
                                  a["cmp_w1_v_2"].reshape(32, 64, 256).transpose(1, 0, 2)], 0)
    w2 = [a[n].reshape(2, 128, 64).transpose(1, 0, 2) for n in ("cmp_w2_k_2", "cmp_w2_v_2")]
    d["cmp_w2"] = np.ascontiguousarray(np.stack([np.concatenate([x, x], -1) for x in w2], 1))
    d["cmp_pe"] = np.ascontiguousarray(np.concatenate([a["cmp_pe_k_2"].T, a["cmp_pe_v_2"].T], 0))
    sk = np.zeros((128, 256), f)
    sk[0:64, 0:128], sk[64:128, 128:256] = a["peer_subkeys_2"][0].T, a["peer_subkeys_2"][1].T
    d["subk"] = sk
    d["u2"] = slabs(np.ascontiguousarray(a["peer_u_2"].T), 8, 256)[0]
    d["v2"] = slabs(a["peer_v_2"], 4, 512).reshape(64, 128, 2048)
    return {k: np.ascontiguousarray(v) for k, v in d.items()}


def program(nc, arrays):
    io = {n: nc.dram_tensor(f"in_{n}", v.shape, F32, kind="ExternalInput").ap() for n, v in arrays.items()}
    io["gdram"] = nc.dram_tensor("gdram", (16, 32, 128, 128), F32, kind="Internal").ap()
    io["adram"] = nc.dram_tensor("adram", (NPRE, 128, 2048), F32, kind="Internal").ap()
    io["dqk"] = nc.dram_tensor("dqk", (2, 2, 3, 128, 512), F32, kind="Internal").ap()
    io["dv"] = nc.dram_tensor("dv", (2, 3, 128, 512), F32, kind="Internal").ap()
    io["mgd"] = nc.dram_tensor("mgd", (16, 128, 512), F32, kind="Internal").ap()
    io["out"] = nc.dram_tensor("out_0", (128, 8, 512), F32, kind="ExternalOutput").ap()
    build(nc, io)


def kernel(**inputs):
    import concourse.bacc as bacc
    from concourse.bass_utils import run_bass_kernel_spmd as run

    arrays = lay_out(inputs)
    nc = bacc.Bacc("TRN2", target_bir_lowering=False, num_devices=1)
    program(nc, arrays)
    r = run(nc, [{f"in_{n}": v for n, v in arrays.items()}], core_ids=[0])
    o = np.asarray(r.results[0]["out_0"])
    return np.ascontiguousarray(o.transpose(1, 0, 2).reshape(1024, 512).T).reshape(1, 512, 1024)
```
